# Optimizing a Trainium2 kernel written in Bass

```python
import jax
import jax.numpy as jnp
from jax import lax
import numpy as np
import jax, jax.numpy as jnp

D_MODEL = 1024
BATCH = 1
SEQ = 512
DEPTH = 2

GRID_W = 64
CTX_LEN = 256
QBLK = 128
ROPE_THETA = 10000.0
EPS = 1e-6

POOL_GROUPS = 4
POOL_CH = 64
POOL_DIM = POOL_GROUPS * POOL_CH
POOL_WINDOWS = (2, 4, 8, 16)

HEAD_DIM = 64
GQA_HEADS = 12
GQA_KV_HEADS = 4
GQA_GROUP = GQA_HEADS // GQA_KV_HEADS
GQA_Q_DIM = GQA_HEADS * HEAD_DIM
GQA_KV_DIM = GQA_KV_HEADS * HEAD_DIM
L0_IN = POOL_DIM + GQA_Q_DIM + 2 * GQA_KV_DIM
L0_MIX = POOL_DIM + GQA_Q_DIM

MLA_HEADS = 8
MLA_NOPE = 64
MLA_ROPE = 32
MLA_QK = MLA_NOPE + MLA_ROPE
MLA_V = 64
MLA_Q_LORA = 384
MLA_KV_LORA = 256

NA_HEADS = 8
NA_HEAD_DIM = 64
NA_DIM = NA_HEADS * NA_HEAD_DIM
NA_ROWS = 8
NA_COLS = 16

L1_IN = MLA_Q_LORA + MLA_KV_LORA + MLA_ROPE + 3 * NA_DIM
L1_MIX = MLA_HEADS * MLA_V + NA_DIM

FFN_DIM = -(-8 * D_MODEL // (3 * 256)) * 256


def rmsnorm(x, g):
    xf = x.astype(jnp.float32)
    y = xf * lax.rsqrt(jnp.mean(xf * xf, axis=-1, keepdims=True) + EPS)
    return y.astype(x.dtype) * g

def rope_1d(x, pos):
    d = x.shape[-1]
    half = d // 2
    inv = (ROPE_THETA ** (-np.arange(half, dtype=np.float32) * 2.0 / d)).astype(np.float32)
    ang = pos.astype(jnp.float32)[:, None] * inv[None, :]
    shape = (1, x.shape[1]) + (1,) * (x.ndim - 3) + (half,)
    cos = jnp.cos(ang).reshape(shape)
    sin = jnp.sin(ang).reshape(shape)
    xf = x.astype(jnp.float32)
    x1, x2 = xf[..., :half], xf[..., half:]
    return jnp.concatenate([x1 * cos - x2 * sin, x1 * sin + x2 * cos], axis=-1).astype(x.dtype)

def axial_rope(x, row, col):
    half = x.shape[-1] // 2
    return jnp.concatenate([rope_1d(x[..., :half], row), rope_1d(x[..., half:], col)], axis=-1)

def split_cols(p, sizes):
    return jnp.split(p, [int(o) for o in np.cumsum(sizes)[:-1]], axis=-1)

def block_attention(q, k, v, scale):
    B, T = q.shape[:2]
    qb = jnp.moveaxis(q.reshape((B, T // QBLK, QBLK) + q.shape[2:]), 1, 0)

    def one_block(q_blk):
        s = jnp.einsum("bqhgd,bkhd->bhgqk", q_blk, k).astype(jnp.float32) * scale
        p = jax.nn.softmax(s, axis=-1).astype(v.dtype)
        return jnp.einsum("bhgqk,bkhd->bqhgd", p, v)

    o = lax.map(one_block, qb)
    return jnp.moveaxis(o, 0, 1).reshape((B, T) + o.shape[3:])

def multiscale_pool(u, w_grp, ch_scale):
    B, T, _ = u.shape
    ug = u.reshape(B, T, POOL_GROUPS, POOL_CH).astype(jnp.float32)
    csum = jnp.concatenate([jnp.zeros((B, 1, POOL_GROUPS, POOL_CH), jnp.float32),
                            jnp.cumsum(ug, axis=1)], axis=1)
    t = np.arange(T)
    lo = np.stack([np.clip(t - w // 2, 0, T) for w in POOL_WINDOWS], axis=-1).astype(np.int32)
    hi = np.stack([np.clip(t - w // 2 + w, 0, T) for w in POOL_WINDOWS], axis=-1).astype(np.int32)
    grp = np.arange(POOL_GROUPS, dtype=np.int32)[None, :]
    win_sum = csum[:, hi, grp] - csum[:, lo, grp]
    count = jnp.asarray((hi - lo).astype(np.float32))[None, :, :, None]
    d = (win_sum / count - ug).astype(u.dtype)
    y = jnp.einsum("btgc,gcd->btgd", d, w_grp).reshape(B, T, POOL_DIM)
    return y * ch_scale

def neighbourhood_attention(q, k, v, k_ctx, v_ctx, rpb, scale):
    B, S, H, dh = q.shape
    rows = S // GRID_W
    kr = min(NA_ROWS, rows)
    kc = NA_COLS
    cols = np.arange(GRID_W)
    key_col = (np.clip(cols - kc // 2, 0, GRID_W - kc)[:, None] + np.arange(kc)[None, :]).astype(np.int32)
    dc_idx = (key_col - cols[:, None] + (NA_COLS - 1)).astype(np.int32)
    n_win = kr * kc
    q_rows = jnp.moveaxis(q.reshape(B, rows, GRID_W, H, dh), 1, 0)

    def one_row(args):
        r, q_r = args
        r0 = jnp.clip(r - kr // 2, 0, rows - kr)
        key_row = r0 + jnp.arange(kr, dtype=jnp.int32)
        idx = (key_row[None, :, None] * GRID_W + key_col[:, None, :]).reshape(GRID_W, n_win)
        k_w = jnp.take(k, idx, axis=1)
        v_w = jnp.take(v, idx, axis=1)
        bias = rpb[:, key_row - r + (NA_ROWS - 1)][:, :, dc_idx]
        bias = jnp.transpose(bias, (0, 2, 1, 3)).reshape(H, GRID_W, n_win)
        s_win = jnp.einsum("bqhd,bqkhd->bhqk", q_r, k_w).astype(jnp.float32) * scale + bias.astype(jnp.float32)
        s_ctx = jnp.einsum("bqhd,bchd->bhqc", q_r, k_ctx).astype(jnp.float32) * scale
        p = jax.nn.softmax(jnp.concatenate([s_win, s_ctx], axis=-1), axis=-1).astype(v.dtype)
        return (jnp.einsum("bhqk,bqkhd->bqhd", p[..., :n_win], v_w)
                + jnp.einsum("bhqc,bchd->bqhd", p[..., n_win:], v_ctx))

    o = lax.map(one_row, (jnp.arange(rows, dtype=jnp.int32), q_rows))
    return jnp.moveaxis(o, 0, 1).reshape(B, S, H, dh)

def adaln(cond, w, b):
    d = w.shape[0]
    m = jax.nn.silu(cond) @ w + b
    return [m[:, None, i * d:(i + 1) * d] for i in range(6)]

def modulate(x, g, shift, scale):
    return rmsnorm(x, g) * (1.0 + scale) + shift

def swiglu(h, wg, wu, wd):
    return (jax.nn.silu(h @ wg) * (h @ wu)) @ wd

def mixer_pool_gqa(h, hc, row, col, need_ctx, w_in, pool_w, pool_scale, q_gain, k_gain, w_out):
    B, S, _ = h.shape
    Tc = hc.shape[1]
    sizes = (POOL_DIM, GQA_Q_DIM, GQA_KV_DIM, GQA_KV_DIM)
    a, q, k, v = split_cols(h @ w_in, sizes)
    ac, qc, kc, vc = split_cols(hc @ w_in, sizes)
    q = axial_rope(rmsnorm(q.reshape(B, S, GQA_KV_HEADS, GQA_GROUP, HEAD_DIM), q_gain), row, col)
    k = axial_rope(rmsnorm(k.reshape(B, S, GQA_KV_HEADS, HEAD_DIM), k_gain), row, col)
    v = v.reshape(B, S, GQA_KV_HEADS, HEAD_DIM)
    kc = rmsnorm(kc.reshape(B, Tc, GQA_KV_HEADS, HEAD_DIM), k_gain)
    vc = vc.reshape(B, Tc, GQA_KV_HEADS, HEAD_DIM)
    scale = HEAD_DIM ** -0.5
    attn = block_attention(q, jnp.concatenate([kc, k], axis=1), jnp.concatenate([vc, v], axis=1),
                           scale).reshape(B, S, GQA_Q_DIM)
    out = jnp.concatenate([multiscale_pool(a, pool_w, pool_scale), attn], axis=-1) @ w_out
    if not need_ctx:
        return out, None
    qc = rmsnorm(qc.reshape(B, Tc, GQA_KV_HEADS, GQA_GROUP, HEAD_DIM), q_gain)
    attn_c = block_attention(qc, kc, vc, scale).reshape(B, Tc, GQA_Q_DIM)
    out_c = jnp.concatenate([multiscale_pool(ac, pool_w, pool_scale), attn_c], axis=-1) @ w_out
    return out, out_c

def mixer_mla_na(h, hc, row, col, need_ctx, w_in, q_a_gain, kv_a_gain, w_uq, w_ukv,
                 mla_q_gain, mla_k_gain, na_q_gain, na_k_gain, na_rpb, w_out):
    B, S, _ = h.shape
    Tc = hc.shape[1]
    sizes = (MLA_Q_LORA, MLA_KV_LORA, MLA_ROPE, NA_DIM, NA_DIM, NA_DIM)
    cq, ckv, kr, nq, nk, nv = split_cols(h @ w_in, sizes)
    cqc, ckvc, krc, nqc, nkc, nvc = split_cols(hc @ w_in, sizes)

    def mla_q(cq_, T):
        q_ = (rmsnorm(cq_, q_a_gain) @ w_uq).reshape(B, T, MLA_HEADS, MLA_QK)
        return rmsnorm(q_, mla_q_gain)

    def mla_kv(ckv_, kr_, T):
        kv = (rmsnorm(ckv_, kv_a_gain) @ w_ukv).reshape(B, T, MLA_HEADS, MLA_NOPE + MLA_V)
        k_rope = jnp.broadcast_to(kr_[:, :, None, :], (B, T, MLA_HEADS, MLA_ROPE))
        k_ = jnp.concatenate([kv[..., :MLA_NOPE], k_rope], axis=-1)
        return rmsnorm(k_, mla_k_gain), kv[..., MLA_NOPE:]

    def rope_tail(t):
        return jnp.concatenate([t[..., :MLA_NOPE], axial_rope(t[..., MLA_NOPE:], row, col)], axis=-1)

    mq = rope_tail(mla_q(cq, S))
    mk, mv = mla_kv(ckv, kr, S)
    mk = rope_tail(mk)
    mkc, mvc = mla_kv(ckvc, krc, Tc)
    mla_scale = MLA_QK ** -0.5
    o_mla = block_attention(mq[:, :, :, None], jnp.concatenate([mkc, mk], axis=1),
                            jnp.concatenate([mvc, mv], axis=1), mla_scale).reshape(B, S, MLA_HEADS * MLA_V)

    q_na = rmsnorm(nq.reshape(B, S, NA_HEADS, NA_HEAD_DIM), na_q_gain)
    k_na = rmsnorm(nk.reshape(B, S, NA_HEADS, NA_HEAD_DIM), na_k_gain)
    v_na = nv.reshape(B, S, NA_HEADS, NA_HEAD_DIM)
    k_nac = rmsnorm(nkc.reshape(B, Tc, NA_HEADS, NA_HEAD_DIM), na_k_gain)
    v_nac = nvc.reshape(B, Tc, NA_HEADS, NA_HEAD_DIM)
    na_scale = NA_HEAD_DIM ** -0.5
    o_na = neighbourhood_attention(q_na, k_na, v_na, k_nac, v_nac, na_rpb, na_scale).reshape(B, S, NA_DIM)

    out = jnp.concatenate([o_mla, o_na], axis=-1) @ w_out
    if not need_ctx:
        return out, None
    mqc = mla_q(cqc, Tc)
    o_mla_c = block_attention(mqc[:, :, :, None], mkc, mvc, mla_scale).reshape(B, Tc, MLA_HEADS * MLA_V)
    q_nac = rmsnorm(nqc.reshape(B, Tc, NA_HEADS, NA_HEAD_DIM), na_q_gain)
    o_na_c = block_attention(q_nac[:, :, :, None], k_nac, v_nac, na_scale).reshape(B, Tc, NA_DIM)
    out_c = jnp.concatenate([o_mla_c, o_na_c], axis=-1) @ w_out
    return out, out_c

def first_inputs(seed: int = 0) -> dict:
    key = jax.random.key(seed)
    ks = iter(jax.random.split(key, 48))

    def nrm(shape, s):
        return jax.random.normal(next(ks), shape, jnp.float32) * s

    def gain(n):
        return 1.0 + nrm((n,), 0.1)

    D = D_MODEL
    inp = {}
    inp["x"] = nrm((BATCH, SEQ, D), 1.0)
    inp["c"] = nrm((BATCH, D), 1.0)
    inp["ctx"] = nrm((BATCH, CTX_LEN, D), 1.0)
    inp["c_ctx"] = nrm((D,), 1.0)
    inp["l0_ada_w"] = nrm((D, 6 * D), 0.5 * D ** -0.5)
    inp["l0_ada_b"] = nrm((6 * D,), 0.02)
    inp["l0_norm_mix"] = gain(D)
    inp["l0_norm_ffn"] = gain(D)
    inp["l0_w_in"] = nrm((D, L0_IN), D ** -0.5)
    inp["l0_pool_w"] = nrm((POOL_GROUPS, POOL_CH, POOL_CH), POOL_CH ** -0.5)
    inp["l0_pool_scale"] = gain(POOL_DIM)
    inp["l0_q_gain"] = gain(HEAD_DIM)
    inp["l0_k_gain"] = gain(HEAD_DIM)
    inp["l0_w_out"] = nrm((L0_MIX, D), L0_MIX ** -0.5)
    inp["l0_ffn_w_gate"] = nrm((D, FFN_DIM), D ** -0.5)
    inp["l0_ffn_w_up"] = nrm((D, FFN_DIM), D ** -0.5)
    inp["l0_ffn_w_down"] = nrm((FFN_DIM, D), FFN_DIM ** -0.5)
    inp["l1_ada_w"] = nrm((D, 6 * D), 0.5 * D ** -0.5)
    inp["l1_ada_b"] = nrm((6 * D,), 0.02)
    inp["l1_norm_mix"] = gain(D)
    inp["l1_norm_ffn"] = gain(D)
    inp["l1_w_in"] = nrm((D, L1_IN), D ** -0.5)
    inp["l1_mla_q_a_gain"] = gain(MLA_Q_LORA)
    inp["l1_mla_kv_a_gain"] = gain(MLA_KV_LORA)
    inp["l1_mla_w_uq"] = nrm((MLA_Q_LORA, MLA_HEADS * MLA_QK), MLA_Q_LORA ** -0.5)
    inp["l1_mla_w_ukv"] = nrm((MLA_KV_LORA, MLA_HEADS * (MLA_NOPE + MLA_V)), MLA_KV_LORA ** -0.5)
    inp["l1_mla_q_gain"] = gain(MLA_QK)
    inp["l1_mla_k_gain"] = gain(MLA_QK)
    inp["l1_na_q_gain"] = gain(NA_HEAD_DIM)
    inp["l1_na_k_gain"] = gain(NA_HEAD_DIM)
    inp["l1_na_rpb"] = nrm((NA_HEADS, 2 * NA_ROWS - 1, 2 * NA_COLS - 1), 0.1)
    inp["l1_w_out"] = nrm((L1_MIX, D), L1_MIX ** -0.5)
    inp["l1_ffn_w_gate"] = nrm((D, FFN_DIM), D ** -0.5)
    inp["l1_ffn_w_up"] = nrm((D, FFN_DIM), D ** -0.5)
    inp["l1_ffn_w_down"] = nrm((FFN_DIM, D), FFN_DIM ** -0.5)
    return inp

def first_block(x, c, ctx, c_ctx,
              l0_ada_w, l0_ada_b, l0_norm_mix, l0_norm_ffn, l0_w_in, l0_pool_w, l0_pool_scale,
              l0_q_gain, l0_k_gain, l0_w_out, l0_ffn_w_gate, l0_ffn_w_up, l0_ffn_w_down,
              l1_ada_w, l1_ada_b, l1_norm_mix, l1_norm_ffn, l1_w_in, l1_mla_q_a_gain, l1_mla_kv_a_gain,
              l1_mla_w_uq, l1_mla_w_ukv, l1_mla_q_gain, l1_mla_k_gain, l1_na_q_gain, l1_na_k_gain,
              l1_na_rpb, l1_w_out, l1_ffn_w_gate, l1_ffn_w_up, l1_ffn_w_down):
    S = x.shape[1]
    tok = jnp.arange(S, dtype=jnp.int32)
    row = tok // GRID_W
    col = tok % GRID_W
    layers = [
        (l0_ada_w, l0_ada_b, l0_norm_mix, l0_norm_ffn, l0_ffn_w_gate, l0_ffn_w_up, l0_ffn_w_down,
         mixer_pool_gqa, (l0_w_in, l0_pool_w, l0_pool_scale, l0_q_gain, l0_k_gain, l0_w_out)),
        (l1_ada_w, l1_ada_b, l1_norm_mix, l1_norm_ffn, l1_ffn_w_gate, l1_ffn_w_up, l1_ffn_w_down,
         mixer_mla_na, (l1_w_in, l1_mla_q_a_gain, l1_mla_kv_a_gain, l1_mla_w_uq, l1_mla_w_ukv,
                        l1_mla_q_gain, l1_mla_k_gain, l1_na_q_gain, l1_na_k_gain, l1_na_rpb, l1_w_out)),
    ]
    xc = ctx
    for i in range(DEPTH):
        ada_w, ada_b, n_mix, n_ffn, wg, wu, wd, mixer, mparams = layers[i]
        need_ctx = i < DEPTH - 1
        sh1, sc1, g1, sh2, sc2, g2 = adaln(c, ada_w, ada_b)
        csh1, csc1, cg1, csh2, csc2, cg2 = adaln(c_ctx[None, :], ada_w, ada_b)
        h = modulate(x, n_mix, sh1, sc1)
        hc = modulate(xc, n_mix, csh1, csc1)
        o, oc = mixer(h, hc, row, col, need_ctx, *mparams)
        x = x + g1 * o
        x = x + g2 * swiglu(modulate(x, n_ffn, sh2, sc2), wg, wu, wd)
        if need_ctx:
            xc = xc + cg1 * oc
            xc = xc + cg2 * swiglu(modulate(xc, n_ffn, csh2, csc2), wg, wu, wd)
    return x


DEPTH_2 = 1

N_HEADS = D_MODEL // HEAD_DIM
N_MOBA = N_HEADS // 4
N_FOX = (N_HEADS - N_MOBA) // 2
N_DIL = N_HEADS - N_MOBA - N_FOX
N_ALIBI = N_MOBA + N_DIL
MOBA_BLOCK = 256
MOBA_TOPK = 3
MOBA_QCHUNK = 32
FOX_QBLOCK = 128
DIL_PAIRS = ((128, 1), (512, 4), (2048, 16))
DIL_BLOCK = 128
D_FF = 4 * D_MODEL
QKV_COLS = 3 * D_MODEL
FOX_GATE_COLS = N_FOX * HEAD_DIM
N_IN_COLS = QKV_COLS + N_FOX + FOX_GATE_COLS
W_MOBA = N_MOBA * HEAD_DIM
W_FOX = N_FOX * HEAD_DIM
ATTN_SCALE = HEAD_DIM ** -0.5
NEG_INF = -1e30


def rms_norm(x, gain):
    xf = x.astype(jnp.float32)
    y = xf * lax.rsqrt(jnp.mean(xf * xf, axis=-1, keepdims=True) + EPS)
    return (y * gain.astype(jnp.float32)).astype(x.dtype)

def alibi_slopes():
    return jnp.exp2(-8.0 * jnp.arange(1, N_ALIBI + 1, dtype=jnp.float32) / N_ALIBI)

def moba_attention(q, k, v, slopes):
    b, h, s, dh = q.shape
    n_blk = -(-s // MOBA_BLOCK)
    s_pad = n_blk * MOBA_BLOCK
    pad = ((0, 0), (0, 0), (0, s_pad - s), (0, 0))
    q, k, v = jnp.pad(q, pad), jnp.pad(k, pad), jnp.pad(v, pad)
    k_blocks = k.reshape(b, h, n_blk, MOBA_BLOCK, dh)
    v_blocks = v.reshape(b, h, n_blk, MOBA_BLOCK, dh)
    k_mean = jnp.mean(k_blocks.astype(jnp.float32), axis=3)
    gate = jnp.einsum('bhsd,bhnd->bhsn', q.astype(jnp.float32), k_mean)
    q_blk = jnp.arange(s_pad) // MOBA_BLOCK
    past = jnp.arange(n_blk)[None, :] < q_blk[:, None]
    gate = jnp.where(past, gate, NEG_INF)
    top_k = min(MOBA_TOPK, n_blk)
    _, sel_idx = lax.top_k(gate, top_k)
    sel_ok = sel_idx < q_blk[:, None]
    gather = jax.vmap(jax.vmap(lambda blocks, idx: blocks[idx]))
    offs = jnp.arange(MOBA_BLOCK)

    def chunk(c):
        start = c * MOBA_QCHUNK
        qc = lax.dynamic_slice_in_dim(q, start, MOBA_QCHUNK, axis=2)
        idx = lax.dynamic_slice_in_dim(sel_idx, start, MOBA_QCHUNK, axis=2)
        ok = lax.dynamic_slice_in_dim(sel_ok, start, MOBA_QCHUNK, axis=2)
        q_pos = start + jnp.arange(MOBA_QCHUNK)
        k_sel = gather(k_blocks, idx)
        v_sel = gather(v_blocks, idx)
        d_sel = (q_pos[:, None, None] - (idx[..., None] * MOBA_BLOCK + offs)).astype(jnp.float32)
        l_sel = (jnp.einsum('bhqd,bhqnkd->bhqnk', qc, k_sel).astype(jnp.float32) * ATTN_SCALE
                 - slopes[:, None, None, None] * d_sel)
        l_sel = jnp.where(ok[..., None], l_sel, NEG_INF).reshape(b, h, MOBA_QCHUNK, top_k * MOBA_BLOCK)
        own_start = (start // MOBA_BLOCK) * MOBA_BLOCK
        k_own = lax.dynamic_slice_in_dim(k, own_start, MOBA_BLOCK, axis=2)
        v_own = lax.dynamic_slice_in_dim(v, own_start, MOBA_BLOCK, axis=2)
        d_own = q_pos[:, None] - (own_start + offs)[None, :]
        l_own = (jnp.einsum('bhqd,bhkd->bhqk', qc, k_own).astype(jnp.float32) * ATTN_SCALE
                 - slopes[:, None, None] * d_own.astype(jnp.float32))
        l_own = jnp.where(d_own >= 0, l_own, NEG_INF)
        p = jax.nn.softmax(jnp.concatenate([l_sel, l_own], axis=-1), axis=-1).astype(v.dtype)
        p_sel = p[..., :top_k * MOBA_BLOCK].reshape(b, h, MOBA_QCHUNK, top_k, MOBA_BLOCK)
        return (jnp.einsum('bhqnk,bhqnkd->bhqd', p_sel, v_sel)
                + jnp.einsum('bhqk,bhkd->bhqd', p[..., top_k * MOBA_BLOCK:], v_own))

    out = lax.map(chunk, jnp.arange(s_pad // MOBA_QCHUNK))
    return out.transpose(1, 2, 0, 3, 4).reshape(b, h, s_pad, dh)[:, :, :s]

def forgetting_attention(q, k, v, f_logit):
    b, h, s, dh = q.shape
    cum = jnp.cumsum(jax.nn.log_sigmoid(f_logit.astype(jnp.float32)), axis=1).transpose(0, 2, 1)
    k_pos = jnp.arange(s)

    def block(i):
        start = i * FOX_QBLOCK
        qb = lax.dynamic_slice_in_dim(q, start, FOX_QBLOCK, axis=2)
        cb = lax.dynamic_slice_in_dim(cum, start, FOX_QBLOCK, axis=2)
        q_pos = start + jnp.arange(FOX_QBLOCK)
        logits = (jnp.einsum('bhqd,bhkd->bhqk', qb, k).astype(jnp.float32) * ATTN_SCALE
                  + cb[..., None] - cum[:, :, None, :])
        logits = jnp.where(k_pos[None, :] <= q_pos[:, None], logits, NEG_INF)
        p = jax.nn.softmax(logits, axis=-1).astype(v.dtype)
        return jnp.einsum('bhqk,bhkd->bhqd', p, v)

    out = lax.map(block, jnp.arange(s // FOX_QBLOCK))
    return out.transpose(1, 2, 0, 3, 4).reshape(b, h, s, dh)

def dilated_branch(q, k, v, slopes, window, dilation):
    b, h, s, dh = q.shape
    steps = window // dilation
    sub_len = s // dilation
    n_blk = -(-sub_len // DIL_BLOCK)
    sub_pad = n_blk * DIL_BLOCK

    def to_sub(t):
        t = t.reshape(b, h, sub_len, dilation, dh).transpose(0, 1, 3, 2, 4)
        t = jnp.pad(t, ((0, 0), (0, 0), (0, 0), (0, sub_pad - sub_len), (0, 0)))
        return t.reshape(b, h, dilation, n_blk, DIL_BLOCK, dh)

    def band(t):
        prev = jnp.concatenate([jnp.zeros_like(t[:, :, :, :1]), t[:, :, :, :-1]], axis=3)
        return jnp.concatenate([prev, t], axis=4)

    qs = to_sub(q)
    kb, vb = band(to_sub(k)), band(to_sub(v))
    blk = jnp.arange(n_blk)[:, None]
    i_q = blk * DIL_BLOCK + jnp.arange(DIL_BLOCK)[None, :]
    i_k = (blk - 1) * DIL_BLOCK + jnp.arange(2 * DIL_BLOCK)[None, :]
    off = i_q[:, :, None] - i_k[:, None, :]
    allowed = (off >= 0) & (off <= steps) & (i_k[:, None, :] >= 0) & (i_k[:, None, :] < sub_len)
    dist = (off * dilation).astype(jnp.float32)
    logits = (jnp.einsum('bhrnqd,bhrnkd->bhrnqk', qs, kb).astype(jnp.float32) * ATTN_SCALE
              - slopes[:, None, None, None, None] * dist)
    logits = jnp.where(allowed, logits, NEG_INF)
    lse = jax.nn.logsumexp(logits, axis=-1)
    p = jnp.exp(logits - lse[..., None]).astype(v.dtype)
    o = jnp.einsum('bhrnqk,bhrnkd->bhrnqd', p, vb)
    o = o.reshape(b, h, dilation, sub_pad, dh)[:, :, :, :sub_len].transpose(0, 1, 3, 2, 4).reshape(b, h, s, dh)
    lse = lse.reshape(b, h, dilation, sub_pad)[..., :sub_len].transpose(0, 1, 3, 2).reshape(b, h, s)
    return o, lse

def dilated_attention(q, k, v, slopes):
    outs, lses = [], []
    for window, dilation in DIL_PAIRS:
        o, lse = dilated_branch(q, k, v, slopes, window, dilation)
        outs.append(o)
        lses.append(lse)
    w = jax.nn.softmax(jnp.stack(lses, axis=0), axis=0)
    o = jnp.sum(w[..., None] * jnp.stack(outs, axis=0).astype(jnp.float32), axis=0)
    return o.astype(q.dtype)

def to_bsd(o):
    b, h, s, dh = o.shape
    return o.transpose(0, 2, 1, 3).reshape(b, s, h * dh)

def mixer_sublayer(x, norm_g, w_in, b_f, q_gain, k_gain, out_gain, w_out):
    b, s, _ = x.shape
    hn = rms_norm(x, norm_g)
    proj = hn @ w_in
    q = proj[..., :D_MODEL].reshape(b, s, N_HEADS, HEAD_DIM)
    k = proj[..., D_MODEL:2 * D_MODEL].reshape(b, s, N_HEADS, HEAD_DIM)
    v = proj[..., 2 * D_MODEL:QKV_COLS].reshape(b, s, N_HEADS, HEAD_DIM)
    f_logit = proj[..., QKV_COLS:QKV_COLS + N_FOX] + b_f
    g_fox = proj[..., QKV_COLS + N_FOX:]
    q = rms_norm(q, q_gain).transpose(0, 2, 1, 3)
    k = rms_norm(k, k_gain).transpose(0, 2, 1, 3)
    v = v.transpose(0, 2, 1, 3)
    slopes = alibi_slopes()
    a0, a1 = N_MOBA, N_MOBA + N_FOX
    o_moba = moba_attention(q[:, :a0], k[:, :a0], v[:, :a0], slopes[N_DIL:])
    o_fox = forgetting_attention(q[:, a0:a1], k[:, a0:a1], v[:, a0:a1], f_logit)
    o_dil = dilated_attention(q[:, a1:], k[:, a1:], v[:, a1:], slopes[:N_DIL])
    y_moba = rms_norm(to_bsd(o_moba), out_gain[:W_MOBA])
    y_fox = rms_norm(to_bsd(o_fox), out_gain[W_MOBA:W_MOBA + W_FOX]) * jax.nn.sigmoid(g_fox)
    y_dil = rms_norm(to_bsd(o_dil), out_gain[W_MOBA + W_FOX:])
    y = jnp.concatenate([y_moba, y_fox, y_dil], axis=-1) @ w_out
    return x + y

def mlp_sublayer(x, norm_g, w_up, w_down):
    hn = rms_norm(x, norm_g)
    return x + jnp.square(jax.nn.relu(hn @ w_up)) @ w_down

def second_inputs(seed: int = 0) -> dict:
    key = jax.random.key(seed)
    ks = jax.random.split(key, 11)
    f32 = jnp.float32
    return {
        "x": jax.random.normal(ks[0], (BATCH, SEQ, D_MODEL), f32),
        "attn_norm": 1.0 + 0.02 * jax.random.normal(ks[1], (DEPTH_2, D_MODEL), f32),
        "w_in": jax.random.normal(ks[2], (DEPTH_2, D_MODEL, N_IN_COLS), f32) * D_MODEL ** -0.5,
        "b_forget": 2.0 + 0.5 * jax.random.normal(ks[3], (DEPTH_2, N_FOX), f32),
        "q_gain": 1.0 + 0.02 * jax.random.normal(ks[4], (DEPTH_2, N_HEADS, HEAD_DIM), f32),
        "k_gain": 1.0 + 0.02 * jax.random.normal(ks[5], (DEPTH_2, N_HEADS, HEAD_DIM), f32),
        "out_gain": 1.0 + 0.02 * jax.random.normal(ks[6], (DEPTH_2, D_MODEL), f32),
        "w_out": jax.random.normal(ks[7], (DEPTH_2, D_MODEL, D_MODEL), f32) * D_MODEL ** -0.5,
        "mlp_norm": 1.0 + 0.02 * jax.random.normal(ks[8], (DEPTH_2, D_MODEL), f32),
        "w_up": jax.random.normal(ks[9], (DEPTH_2, D_MODEL, D_FF), f32) * D_MODEL ** -0.5,
        "w_down": jax.random.normal(ks[10], (DEPTH_2, D_FF, D_MODEL), f32) * D_FF ** -0.5,
    }

def second_block(x, attn_norm, w_in, b_forget, q_gain, k_gain, out_gain, w_out, mlp_norm, w_up, w_down):
    for l in range(DEPTH_2):
        x = mixer_sublayer(x, attn_norm[l], w_in[l], b_forget[l], q_gain[l], k_gain[l],
                           out_gain[l], w_out[l])
        x = mlp_sublayer(x, mlp_norm[l], w_up[l], w_down[l])
    return x


def setup_inputs(seed=0):
    out = dict(first_inputs(seed))
    for name, value in second_inputs(seed + 1).items():
        if name != "x":
            out[name + "_2"] = value
    return out


def reference(
    x, c, ctx, c_ctx, l0_ada_w, l0_ada_b, l0_norm_mix, l0_norm_ffn, l0_w_in, l0_pool_w,
    l0_pool_scale, l0_q_gain, l0_k_gain, l0_w_out, l0_ffn_w_gate, l0_ffn_w_up, l0_ffn_w_down,
    l1_ada_w, l1_ada_b, l1_norm_mix, l1_norm_ffn, l1_w_in, l1_mla_q_a_gain, l1_mla_kv_a_gain,
    l1_mla_w_uq, l1_mla_w_ukv, l1_mla_q_gain, l1_mla_k_gain, l1_na_q_gain, l1_na_k_gain,
    l1_na_rpb, l1_w_out, l1_ffn_w_gate, l1_ffn_w_up, l1_ffn_w_down, attn_norm_2, w_in_2,
    b_forget_2, q_gain_2, k_gain_2, out_gain_2, w_out_2, mlp_norm_2, w_up_2, w_down_2,
):
    x = first_block(
        x, c, ctx, c_ctx, l0_ada_w, l0_ada_b, l0_norm_mix, l0_norm_ffn, l0_w_in, l0_pool_w,
        l0_pool_scale, l0_q_gain, l0_k_gain, l0_w_out, l0_ffn_w_gate, l0_ffn_w_up,
        l0_ffn_w_down, l1_ada_w, l1_ada_b, l1_norm_mix, l1_norm_ffn, l1_w_in, l1_mla_q_a_gain,
        l1_mla_kv_a_gain, l1_mla_w_uq, l1_mla_w_ukv, l1_mla_q_gain, l1_mla_k_gain, l1_na_q_gain,
        l1_na_k_gain, l1_na_rpb, l1_w_out, l1_ffn_w_gate, l1_ffn_w_up, l1_ffn_w_down,
    )
    return second_block(
        x, attn_norm_2, w_in_2, b_forget_2, q_gain_2, k_gain_2, out_gain_2, w_out_2, mlp_norm_2,
        w_up_2, w_down_2,
    )


_drawn_inputs = setup_inputs


def setup_inputs(seed=0):
    import zlib

    import numpy as np

    out = dict(_drawn_inputs(seed))
    spreads = {}
    factors = {'l0_norm_mix': 3.039,
     'l0_pool_scale': 3.076,
     'l0_q_gain': 8.0,
     'l0_k_gain': 8.0,
     'l1_norm_mix': 6.691,
     'l1_mla_q_a_gain': 8.0,
     'l1_mla_kv_a_gain': 4.081,
     'l1_mla_q_gain': 8.0,
     'l1_mla_k_gain': 8.0,
     'l1_na_q_gain': 8.0,
     'l1_na_k_gain': 8.0,
     'l1_na_rpb': 8.0,
     'attn_norm_2': 2.983,
     'q_gain_2': 6.324,
     'k_gain_2': 6.273,
     'out_gain_2': 37.494,
     'mlp_norm_2': 10.606}
    for name, (base, spread) in spreads.items():
        noise = np.random.default_rng([zlib.crc32(name.encode()), seed]).standard_normal(out[name].shape)
        drawn = base * np.exp(spread * noise) if base else spread * noise
        out[name] = jnp.asarray(drawn.astype(out[name].dtype))
    for name, factor in factors.items():
        out[name] = (out[name] * factor).astype(out[name].dtype)
    return out
```

```python
from contextlib import ExitStack

import numpy as np

import concourse.bass as bass
from concourse import mybir

ALU = mybir.AluOpType
ACT = mybir.ActivationFunctionType
F32 = mybir.dt.float32
F32R = mybir.dt.float32r
AX_X = mybir.AxisListType.X

P = 128
D = 1024
KD = D // P
TX, TC = 512, 256
T = TX + TC
FFN = 2816
FF2 = 4 * D
GRID = 64
EPS = 1e-6
NEG = -1.0e30
HD = 64
POOL_W = (2, 4, 8, 16)
GQ, GKV = 12, 4
MH, MQK, MROPE = 8, 96, 32
NAH, NAC = 8, 16
QL, KVL = 384, 256
HEADS, N_MOBA, N_FOX, N_DIL = 16, 4, 6, 6
DIL_PAIRS = ((128, 1), (512, 4), (2048, 16))
BW = 7 * P
RING = 4
X_ONLY = ((0, TX),)
X_CTX = ((0, TX), (TX, TC))


def shape_tables():
    p = np.arange(P)
    same64 = (p[:, None] // HD == p[None, :] // HD)
    mats = np.zeros((P, 8, P), np.float32)
    mats[:, 0] = np.eye(P)
    mats[:, 1] = 1.0 / D
    mats[:, 2] = same64 / HD
    mats[:, 3] = 1.0 / QL
    mats[:, 4] = 1.0 / KVL
    mats[:MQK, 5, :MQK] = 1.0 / MQK
    for m in range(P):
        low = m % 32 < 16
        mats[m + 16 if low else m - 16, 6, m] = -1.0 if low else 1.0
    for m in range(HD, MQK):
        low = m % 16 < 8
        mats[m + 8 if low else m - 8, 7, m] = -1.0 if low else 1.0
    tok = np.arange(TX)
    row, col = (tok // GRID).astype(np.float32), (tok % GRID).astype(np.float32)

    def angles(rows, first, d):
        out = np.zeros((rows, TX), np.float32)
        inv = (10000.0 ** (-np.arange(d // 2, dtype=np.float32) * 2.0 / d)).astype(np.float32)
        for q in range(first, rows):
            pos = row if (q - first) % (2 * d) < d else col
            out[q] = pos * inv[(q - first) % (d // 2)]
        return out

    a0, a1 = angles(P, 0, 32), angles(P, HD, 16)
    a1[MQK:] = 0.0
    rope = np.stack([np.cos(a0), np.sin(a0), np.cos(a1), np.sin(a1)], 1).astype(np.float32)
    icnt = np.zeros((P, 2, T), np.float32)
    for g, w in enumerate(POOL_W):
        for lo_t, n in ((0, TX), (TX, TC)):
            t = np.arange(n)
            cnt = np.clip(t - w // 2 + w, 0, n) - np.clip(t - w // 2, 0, n)
            icnt[64 * (g % 2):64 * (g % 2) + 64, g // 2, lo_t:lo_t + n] = 1.0 / cnt
    c = p % GRID
    start = np.clip(c - NAC // 2, 0, GRID - NAC)[:, None]
    kc = np.arange(GRID)[None, :]
    namask = np.where((kc >= start) & (kc < start + NAC), 0.0, NEG).astype(np.float32)[:, ::-1].copy()
    dist = p[:, None] - np.arange(BW)[None, :] + 3 * P
    causal = dist >= 0
    times = sum(((dist % d == 0) & (dist <= w)).astype(np.int64) for w, d in DIL_PAIRS) * causal
    dil = np.where(times > 0, np.log(np.maximum(times, 1)), NEG)
    band = np.stack([np.where(causal, dist, -NEG), np.where(causal, dist, 0), dil,
                     np.where(causal, 0.0, NEG)], 1).astype(np.float32)
    sel = np.zeros((N_FOX, N_FOX, P), np.float32)
    for h in range(N_FOX):
        sel[h, h] = 1.0
    return {"mats": mats, "rope": rope, "icnt": icnt, "namask": namask, "band": band, "sel": sel}


SLOPES = [float(np.float32(2.0 ** (-8.0 * i / (N_MOBA + N_DIL)))) for i in range(1, N_MOBA + N_DIL + 1)]


def split_width(total, width):
    return [(i, min(width, total - i)) for i in range(0, total, width)]


FFN_CHUNKS = split_width(FFN // P, 8)
FF2_CHUNKS = split_width(FF2 // P, 8)


def build(nc, A, out):
    with ExitStack() as ctx:
        def sb(name, shape, dt=F32):
            return ctx.enter_context(nc.sbuf_tensor(name, shape, dt))

        def sem(name):
            return ctx.enter_context(nc.semaphore(name))

        at_a = -(-nc.sbuf_base // 32) * 32
        big_a = sb("big_a", [P, 2 * KD * T], F32R)
        big_b = sb("big_b", [P, 2 * KD * T], F32R)
        plain_a = nc.alloc_sbuf_tensor_at("plain_a", [P, 2 * KD * T], F32, offset=at_a)
        plain_b = nc.alloc_sbuf_tensor_at("plain_b", [P, 2 * KD * T], F32, offset=at_a + 8 * KD * T)
        xT = sb("xT", [P, KD, T])
        raw = sb("raw", [P, RING, KD, P])
        whi = sb("whi", [P, 2, KD, P], F32R)
        wlo = sb("wlo", [P, 2, KD, P], F32R)
        sq = sb("sq", [P, 2, T])
        qr = sb("qr", [P, 2, T])
        tmp = sb("tmp", [P, 2, T])
        rsb = sb("rsb", [P, 2, T])
        ssq = sb("ssq", [P, T])
        rt = sb("rt", [P, 2, TX])
        vreg = sb("vreg", [P, 2 * T])
        rope = sb("rope", [P, 2, TX])
        mats = sb("mats", [P, 8, P])
        namask = sb("namask", [P, GRID])
        vrow = sb("vrow", [P, 2, P])
        vcol = sb("vcol", [P, 2, P])
        mod = sb("mod", [P, 2, 48, 2])
        amix = sb("amix", [P, 4, KD, 2])
        cs = sb("cs", [P, KD, 2])
        poolw = sb("poolw", [P, 2, P])
        eps = sb("eps", [P, 1])
        zero8 = sb("zero8", [P, KD])
        bfox = sb("bfox", [N_FOX, 1])
        krbuf = sb("krbuf", [P, T])
        stat = sb("stat", [P, 4, 80])
        ss12 = sb("ss12", [P, 2, 3, 4])
        G = [ctx.enter_context(nc.psum_tensor(f"G{i}", [P, 1024], F32)) for i in range(4)]
        pad_dram = nc.dram_tensor("rpb_padded", (NAH * 15, 127), F32, kind="Internal").ap()

        hhi = big_a[:, 0:KD * T].rearrange("p (k t) -> p k t", k=KD)
        hlo = big_a[:, KD * T:].rearrange("p (k t) -> p k t", k=KD)
        ahi = big_b[:, 0:KD * T].rearrange("p (k t) -> p k t", k=KD)
        alo = big_b[:, KD * T:].rearrange("p (k t) -> p k t", k=KD)
        af, bf = plain_a[:], plain_b[:]

        def part(base, at, *dims):
            n = int(np.prod(dims))
            v = base[:, at:at + n]
            if len(dims) == 1:
                return v
            return v.rearrange("p (a b) -> p a b", a=dims[0])

        ident, ones_d, blk64, ones_q, ones_kv, ones96, rot64, rot32 = (mats[:, i, :] for i in range(8))
        q0T, k0T = part(bf, 0, 6, T), part(bf, 6 * T, 2, T)
        PB = 8 * T
        UPW = 8 + TX + 8 + 8 + TC + 8
        upad, ptmp = part(bf, PB, 2, UPW), part(bf, PB + 2 * UPW, 2, UPW)
        dT = part(bf, PB + 4 * UPW, 2, T)
        o0 = part(bf, PB, 6, GQ * HD)
        v0 = part(vreg, 0, 6, GKV * HD)
        nqT, nkT = part(bf, 0, 4, TX), part(bf, 4 * TX, 4, T)
        nv = part(bf, 5120, 6, NAH * HD)
        ckvn, cqn = part(bf, 8192, 2, T), part(bf, 9728, 3, TX)
        mqT, mkT = part(af, 0, MH, TX), part(af, MH * TX, MH, T)
        omla = part(af, 10240, 4, 512)
        mvx, mvc = part(bf, 9728, 4, 512), part(vreg, 0, 2, 512)
        nabias = [part(bf, 8192, 14, GRID), part(bf, 11392, 14, GRID)]
        ona = part(bf, 9088, 4, 512)
        craw = part(vreg, 0, 3, TX)
        kvraw = part(bf, 5120, 2, T)
        q2T, k2T, v2 = part(bf, 0, 8, TX), part(bf, 4096, 8, TX), part(bf, 8192, 4, D)
        o2 = part(af, 0, 4, D)
        band = part(af, 4096, 4, BW)
        th = part(af, 4096 + 4 * BW, 2, BW)
        sel = part(af, 4096 + 6 * BW, N_FOX, P)
        gsig = part(vreg, 0, 3, TX)
        cum = rope[:, 0, :]
        lsig = rope[:, 1, :]
        xtok = part(af, 0, 6, D)
        ostage = part(af, 0, 4, D)
        zpad, zrow = part(bf, 0, 127), part(bf, 128, 31)
        Pm, PT = qr, sq

        landed = [sem(f"landed{i}") for i in range(RING)]
        raw_free = [sem(f"raw_free{i}") for i in range(RING)]
        hi_done = sem("hi_done")
        unit_done = sem("unit_done")
        aux_done = sem("aux_done")
        gfree = [sem(f"gfree{i}") for i in range(4)]

        plan = {}
        cnt = {"r": 0, "u": 0, "g": 0, "a": 0}
        ring_dmas = []
        ring_total = []
        unit_ring = []

        def use_ring(n_dmas=1):
            r = cnt["r"]
            cnt["r"] += 1
            before = ring_total[r - RING] if r >= RING else 0
            ring_total.append(before + 16 * n_dmas)
            return r

        def plan_unit(key, split=True, n_dmas=1):
            r = use_ring(n_dmas)
            u = None
            if split:
                u = cnt["u"]
                cnt["u"] += 1
                unit_ring.append(r)
            plan[key] = (u, r, cnt["g"])
            cnt["g"] += 1

        def plan_aux(key, group=None):
            if group is None:
                group = cnt["g"]
                cnt["g"] += 1
            plan[key] = (cnt["a"], group)
            cnt["a"] += 1
            return group

        for l in range(2):
            plan["ada", l] = cnt["r"]
            for _ in range(48):
                use_ring()
        plan_aux("vec")
        plan_aux(("adag", 0))
        plan_aux(("adag", 1))
        for m in range(KD):
            plan_aux(("xin", m))

        def plan_norm(n):
            plan_aux(("norm", n))

        def plan_inputs(st, units, vts, sums, split=True, two=()):
            seq = []
            open_group = None
            for n in range(len(units) + 2):
                if n < len(units):
                    plan_unit((st, "U", n), split, 2 if n in two else 1)
                    seq.append(("U", n))
                if n - 1 in vts:
                    plan_aux((st, "V", n - 1))
                    seq.append(("V", n - 1))
                if n - 1 in sums:
                    open_group = plan_aux((st, "S", n - 1), None if sums[n - 1]["start"] else open_group)
                    seq.append(("S", n - 1))
                if n - 2 in sums and sums[n - 2]["rope"]:
                    plan_aux((st, "R", n - 2))
                    seq.append(("R", n - 2))
            plan[st, "seq"] = seq

        def item(s, dst, gain, n, mat, rows=P, rope=False, raw_at=None, start=True, stop=True, members=None,
                 kr=False):
            return dict(s=s, dst=dst, gain=gain, n=n, mat=mat, rows=rows, rope=rope, raw=raw_at,
                        start=start, stop=stop, members=members, kr=kr)

        VC = {}
        at = 0
        for name, n in (("c", 8), ("c_ctx", 8), ("an2", 8), ("mn2", 8), ("pscale", 2), ("qa", 3), ("kva", 2),
                        ("og2", 8), ("q2", 8), ("k2", 8), ("q0", 1), ("k0", 1), ("nq", 1), ("nk", 1),
                        ("mq", 1), ("mk", 1)):
            VC[name] = at
            at += n
        VROWS2 = at

        def vc(name, i=0):
            return vcol[:, 1, VC[name] + i:VC[name] + i + 1]

        plan_norm(0)
        L0_COLS = [[(0, 128)], [(128, 128)], [(1280, 128)], [(1408, 128)], [(1024, 128)], [(1152, 128)]]
        for t in range(6):
            a = 6 * (t // 3) + t % 3
            L0_COLS.append([(256 + HD * a, HD), (256 + HD * (a + 3), HD)])
        S0 = {}
        for i in range(2):
            S0[4 + i] = item(i, k0T[:, i], vc("k0"), T, blk64, rope=True)
        for i in range(6):
            S0[6 + i] = item(2 + i, q0T[:, i], vc("q0"), T, blk64, rope=True)
        plan_inputs("in0", L0_COLS, (2, 3), S0, two=range(6, 12))
        plan_aux(("pool", 0))
        plan_aux(("pool", 1))

        def plan_ot(st, n):
            for m in range(n):
                plan_aux((st, "OT", m))

        plan_ot("ot0", 6)

        def plan_wout(l):
            for m in range(KD):
                plan_unit(("wout", l, m))

        def plan_ffn(l, chunks, gated):
            for c, (f0, nf) in enumerate(chunks):
                for i in range(nf * (2 if gated else 1)):
                    plan_unit(("up", l, c, i))
                for m in range(KD * 1):
                    plan_unit(("down", l, c, m))

        plan_wout(0)
        plan_norm(1)
        plan_ffn(0, FFN_CHUNKS, True)
        plan_norm(2)
        L1_COLS = [[(c0, 128)] for c0 in (0, 128, 256, 384, 512, 576)] + [[(672 + 128 * i, 128)] for i in range(12)]
        S1 = {}
        for i in range(3):
            S1[i] = item(i, None, None, TX, ones_q, raw_at=craw[:, i], start=i == 0, stop=i == 2,
                         members=[(craw[:, j], cqn[:, j], vc("qa", j)) for j in range(3)])
        for i in range(2):
            S1[3 + i] = item(3 + i, None, None, T, ones_kv, raw_at=kvraw[:, i], start=i == 0, stop=i == 1,
                             members=[(kvraw[:, j], ckvn[:, j], vc("kva", j)) for j in range(2)])
        for i in range(4):
            S1[6 + i] = item(5 + i, nqT[:, i], vc("nq"), TX, blk64)
            S1[10 + i] = item(9 + i, nkT[:, i], vc("nk"), T, blk64)
        plan_inputs("in1", L1_COLS, (14, 15, 16, 17), S1)
        SQ = {h: item(h, mqT[0:MQK, h], vc("mq"), TX, ones96, rows=MQK, rope=True) for h in range(MH)}
        plan_inputs("mq", range(MH), (), SQ, split=False)
        SK = {h: item(h, mkT[0:MQK, h], vc("mk"), T, ones96, rows=MQK, rope=True, kr=True) for h in range(MH)}
        plan_inputs("mk", range(MH), range(MH), SK, split=False)
        plan_ot("ot1", 4)
        plan_ot("ot2", 4)
        plan_wout(1)
        plan_norm(3)
        plan_ffn(1, FFN_CHUNKS, True)
        plan_norm(4)
        B2_COLS = [[(128 * i, 128)] for i in range(25)] + [[(3078 + 128 * i, 128)] for i in range(3)]
        S2 = {}
        for i in range(8):
            S2[i] = item(i, q2T[:, i], vc("q2", i), TX, blk64)
            S2[8 + i] = item(8 + i, k2T[:, i], vc("k2", i), TX, blk64)
        plan_inputs("in2", B2_COLS, range(16, 24), S2)
        plan_ot("ot3", 8)
        plan_wout(2)
        plan_norm(5)
        plan_ffn(2, FF2_CHUNKS, False)
        for m in range(4):
            plan_aux(("xout", m))

        def attention_units():
            st0, st1, st2, st3 = [], [], [], []
            for h in range(GQ):
                pr, off = h // 6, HD * ((h % 6) // 3)
                t = 3 * pr + h % 3
                kt = k0T[off:off + HD, pr]
                for qt in range(6):
                    ctx_only = qt >= 4
                    vs = [v0[:, j, HD * (h // 3):HD * (h // 3) + HD] for j in (range(4, 6) if ctx_only else range(6))]
                    st0.append(dict(q=q0T[off:off + HD, t, P * qt:P * qt + P],
                                    ks=[(kt[:, TX:T], 0, TC)] if ctx_only else [(kt[:, 0:TX], 0, TX), (kt[:, TX:T], TX, TC)],
                                    vs=vs, o=o0[:, qt, HD * h:HD * h + HD], kind="plain"))
            for h in range(MH):
                for qt in range(4):
                    vs = [mvx[:, j, HD * h:HD * h + HD] for j in range(4)] + [mvc[:, j, HD * h:HD * h + HD] for j in range(2)]
                    st1.append(dict(q=mqT[0:MQK, h, P * qt:P * qt + P],
                                    ks=[(mkT[0:MQK, h, 0:TX], 0, TX), (mkT[0:MQK, h, TX:T], TX, TC)],
                                    vs=vs, o=omla[:, qt, HD * h:HD * h + HD], kind="plain"))
            for h in range(NAH):
                off = HD * (h % 2)
                for qt in range(4):
                    kt = nkT[off:off + HD, h // 2]
                    st2.append(dict(q=nqT[off:off + HD, h // 2, P * qt:P * qt + P],
                                    ks=[(kt[:, 0:TX], 0, TX), (kt[:, TX:T], TX, TC)],
                                    vs=[nv[:, j, HD * h:HD * h + HD] for j in range(6)],
                                    o=ona[:, qt, HD * h:HD * h + HD], kind="na", head=h, qt=qt,
                                    bias=nabias[h % 2][:, 6 - 2 * qt:14 - 2 * qt, ::-1]))
            for h in range(HEADS):
                off = HD * (h % 2)
                fox = N_MOBA <= h < N_MOBA + N_FOX
                for qt in range(4):
                    n = P * (qt + 1)
                    table = band[:, 3] if fox else th[:, h % 2]
                    st3.append(dict(q=q2T[off:off + HD, h // 2, P * qt:P * qt + P],
                                    ks=[(k2T[off:off + HD, h // 2, 0:n], 0, n)],
                                    vs=[v2[:, j, HD * h:HD * h + HD] for j in range(qt + 1)],
                                    o=o2[:, qt, HD * h:HD * h + HD], kind="band", head=h, qt=qt,
                                    bias=table[:, 3 * P - P * qt:3 * P - P * qt + n], fox=h - N_MOBA if fox else None))
            return st0, st1, st2, st3

        ATT = attention_units()
        PH = {}

        def stage_sems(st, *names):
            for n in names:
                PH[st, n] = sem(f"{st}_{n}")

        stage_sems("set", "tables", "zero", "rows", "cols", "xload", "padrow", "pad", "poolw", "poolz",
                   "silu", "b", "rope1", "icnt", "band", "steps")
        stage_sems("in0", "pooled", "pooly", "pooldone")
        stage_sems("in1", "kr")
        stage_sems("in2", "fg", "cum", "outsq", "outstd", "outn")
        stage_sems("att2", "bias0", "bias1", "masked")
        stage_sems("fin", "x", "copy", "out")
        BASE = {}

        def shared_sems(names, stages):
            for i, name in enumerate(names):
                s = sem(name)
                total = 0
                for st, counts in stages:
                    PH[st, name.split("_")[-1]] = s
                    BASE[st, name.split("_")[-1]] = total
                    total += counts[i]

        def input_counts(sums, vts):
            n = len(sums)
            stops = sum(1 for it in sums.values() if it["stop"])
            ropes = sum(1 for it in sums.values() if it["rope"])
            return (len(vts), len(vts), n, stops, stops, ropes)

        shared_sems(("in_vcopy", "in_vdone", "in_square", "in_std", "in_normed", "in_rotated"),
                    [("in0", input_counts(S0, (2, 3))), ("in1", input_counts(S1, range(4))),
                     ("mq", input_counts(SQ, ())), ("mk", input_counts(SK, range(MH))),
                     ("in2", input_counts(S2, range(8)))])
        shared_sems(("att_scores", "att_max", "att_prob", "att_turned", "att_pt", "att_pv", "att_o"),
                    [(f"att{i}", (len(ATT[i]),) * 7) for i in range(4)])
        shared_sems(("ot_a", "ot_b", "ot_hi", "ot_done"),
                    [(f"ot{i}", (0, 0, n, n)) for i, n in enumerate((6, 4, 4, 8))])
        shared_sems(("res_x", "res_sq", "res_ssq"), [(f"res{i}", (KD,) * 3) for i in range(6)])
        shared_sems(("norm_std", "norm_tmp", "norm_hi", "norm_h"), [(f"norm{i}", (1, KD, KD, KD)) for i in range(6)])
        shared_sems(("ffn_act", "ffn_prod", "ffn_hi", "ffn_lo"),
                    [(f"ffn{i}", (n // P,) * 4) for i, n in enumerate((FFN, FFN, FF2))])

        def when(what, count):
            return PH[what], count + BASE.get(what, 0)

        def product_of(key, j=0):
            u, r, _ = plan[key]
            if u is None:
                return raw_free[r % RING], r // RING + 1
            return unit_done, u + 1 + 4 * j

        def auxiliary(key):
            return aux_done, plan[key][0] + 1

        def group_of(key):
            return plan[key][-1]

        def release(ins, key):
            return ins.then_inc(gfree[group_of(key) % 4], 1)

        def free(eng, key):
            eng.sem_inc(gfree[group_of(key) % 4], 1)

        def ps(key, n=T, rows=P):
            return G[group_of(key) % 4][0:rows, 0:n]

        block = ctx.enter_context(nc.Block())

        @block.sync
        def _(sp):
            with nc.allow_non_contiguous_dma(reason="small vectors"):
                sp.dma_start(mats[:], A["mats"]).then_inc(PH["set", "tables"], 16)
                sp.dma_start(rope[:], A["rope"][:, 0:2]).then_inc(PH["set", "tables"], 16)
                sp.dma_start(namask[:], A["namask"]).then_inc(PH["set", "tables"], 16)

                def rows_of(name, width=P):
                    return A[name].rearrange("(a p) -> a p", p=width)

                at = 0
                for name in ("l0_ada_b", "l0_norm_mix", "l0_norm_ffn", "l1_ada_b", "l1_norm_mix", "l1_norm_ffn"):
                    n = A[name].shape[0] // P
                    sp.dma_start(vrow[at:at + n, 0, :], rows_of(name)).then_inc(PH["set", "rows"], 16)
                    at += n
                sp.wait_ge(*when(("set", "zero"), 1))
                two = lambda name, w: A[name].rearrange("a (b p) -> (a b) p", p=w)
                for key, src in (("c", two("c", P)), ("c_ctx", rows_of("c_ctx")), ("an2", two("attn_norm_2", P)),
                                 ("mn2", two("mlp_norm_2", P)), ("pscale", rows_of("l0_pool_scale")),
                                 ("qa", rows_of("l1_mla_q_a_gain")), ("kva", rows_of("l1_mla_kv_a_gain")),
                                 ("og2", two("out_gain_2", P)),
                                 ("q2", A["q_gain_2"].rearrange("a (b c) d -> (a b) (c d)", c=2)),
                                 ("k2", A["k_gain_2"].rearrange("a (b c) d -> (a b) (c d)", c=2))):
                    n = src.shape[0]
                    sp.dma_start(vrow[VC[key]:VC[key] + n, 1, :], src).then_inc(PH["set", "rows"], 16)
                for key, name in (("q0", "l0_q_gain"), ("k0", "l0_k_gain"), ("nq", "l1_na_q_gain"), ("nk", "l1_na_k_gain")):
                    for i in range(2):
                        sp.dma_start(vrow[VC[key]:VC[key] + 1, 1, HD * i:HD * i + HD],
                                     A[name].rearrange("(a p) -> a p", a=1)).then_inc(PH["set", "rows"], 16)
                for key, name in (("mq", "l1_mla_q_gain"), ("mk", "l1_mla_k_gain")):
                    sp.dma_start(vrow[VC[key]:VC[key] + 1, 1, 0:MQK],
                                 A[name].rearrange("(a p) -> a p", a=1)).then_inc(PH["set", "rows"], 16)
                sp.dma_start(dT, A["icnt"]).then_inc(PH["set", "icnt"], 16)
                sp.dma_start(bfox[:], A["b_forget_2"].rearrange("a b -> b a")).then_inc(PH["set", "b"], 16)
                sp.wait_ge(*when(("set", "poolz"), 1))
                for g in range(4):
                    o = HD * (g % 2)
                    sp.dma_start(poolw[o:o + HD, g // 2, o:o + HD], A["l0_pool_w"][g]).then_inc(PH["set", "poolw"], 16)

            def columns(name):
                return A[name].rearrange("(k p) n -> p k n", p=P)

            def load(r, blocks, j=0, rows=KD):
                if r >= RING:
                    sp.wait_ge(raw_free[r % RING], r // RING + j)
                at = 0
                for src, width in blocks:
                    ins = sp.dma_start(raw[:, r % RING, 0:rows, at:at + width], src)
                    ins.then_inc(landed[r % RING], 16)
                    at += width

            def ada(l):
                w, r0 = columns(f"l{l}_ada_w"), plan["ada", l]
                for b in range(4):
                    load(r0 + b, [(w[:, :, P * b:P * b + P], P)])
                with sp.Fori(1, 12) as j:
                    for b in range(4):
                        load(r0 + b + (RING if r0 == 0 else 0), [(w[:, :, bass.ds((j * 4 + b) * P, P)], P)],
                             j - 1 if r0 == 0 else j)

            for l in range(2):
                ada(l)
                if l == 0:
                    sp.dma_start(xtok[:, 0:4, :], A["x"].rearrange("a (t p) d -> p (a t) d", p=P)).then_inc(PH["set", "xload"], 16)
                    sp.dma_start(xtok[:, 4:6, :], A["ctx"].rearrange("a (t p) d -> p (a t) d", p=P)).then_inc(PH["set", "xload"], 16)

            def inputs(st, name, cols):
                w = columns(name) if len(A[name].shape) == 2 else A[name].rearrange("a (k p) n -> p (a k) n", p=P)
                for n, blocks in enumerate(cols):
                    load(plan[st, "U", n][1], [(w[:, :, c:c + m], m) for c, m in blocks])

            def square_matrix(name, l):
                w = columns(name) if len(A[name].shape) == 2 else A[name].rearrange("a (k p) n -> p (a k) n", p=P)
                r0 = plan["wout", l, 0][1]
                with sp.Fori(0, 2) as j:
                    for b in range(4):
                        load(r0 + b, [(w[:, :, bass.ds((j * 4 + b) * P, P)], P)], j)

            def ffn(l, ups, down, chunks):
                for c, (f0, nf) in enumerate(chunks):
                    r0 = plan["up", l, c, 0][1]
                    per = 4 // len(ups)
                    with sp.Fori(0, nf // per) as j:
                        for b in range(4):
                            w = ups[b % len(ups)]
                            load(r0 + b, [(w[:, :, bass.ds((j * per + (f0 + b // len(ups))) * P, P)], P)], j)
                    r0 = plan["down", l, c, 0][1]
                    with sp.Fori(0, 2) as j:
                        for b in range(4):
                            load(r0 + b, [(down[:, f0:f0 + nf, bass.ds((j * 4 + b) * P, P)], P)], j, rows=nf)

            inputs("in0", "l0_w_in", L0_COLS)
            square_matrix("l0_w_out", 0)
            ffn(0, [columns("l0_ffn_w_gate"), columns("l0_ffn_w_up")], columns("l0_ffn_w_down"), FFN_CHUNKS)
            inputs("in1", "l1_w_in", L1_COLS)
            wq, wkv = columns("l1_mla_w_uq"), columns("l1_mla_w_ukv")
            for h in range(MH):
                load(plan["mq", "U", h][1], [(wq[:, :, MQK * h:MQK * h + MQK], MQK)], rows=3)
            for h in range(MH):
                load(plan["mk", "U", h][1], [(wkv[:, :, P * h:P * h + P], P)], rows=2)
            square_matrix("l1_w_out", 1)
            ffn(1, [columns("l1_ffn_w_gate"), columns("l1_ffn_w_up")], columns("l1_ffn_w_down"), FFN_CHUNKS)
            inputs("in2", "w_in_2", B2_COLS)
            square_matrix("w_out_2", 2)
            up2 = A["w_up_2"].rearrange("a (k p) n -> p (a k) n", p=P)
            down2 = A["w_down_2"].rearrange("a (k p) n -> p (a k) n", p=P)
            ffn(2, [up2], down2, FF2_CHUNKS)
            for t in range(4):
                sp.wait_ge(*when(("fin", "copy"), t + 1))
                sp.dma_start(out[0, P * t:P * t + P, :], ostage[:, t, :]).then_inc(PH["fin", "out"], 16)
            sp.wait_ge(*when(("fin", "out"), 64))

        @block.gpsimd
        def _(pool):
            pool.memset(vrow[:, 1, :], 0.0).then_inc(PH["set", "zero"], 1)
            pool.memset(poolw[:], 0.0).then_inc(PH["set", "poolz"], 1)
            pool.memset(zpad[0:NAH * 15, :], 0.0).then_inc(PH["set", "pad"], 1)
            pool.wait_ge(*when(("set", "pad"), 1))
            with nc.allow_non_contiguous_dma(reason="small table"):
                pool.dma_start(zrow[0:NAH * 15, :], A["l1_na_rpb"].rearrange("h r c -> (h r) c")).then_inc(PH["set", "padrow"], 16)
            pool.wait_ge(*when(("set", "padrow"), 16))
            pool.tensor_copy(zpad[0:NAH * 15, 48:79], zrow[0:NAH * 15, ::-1]).then_inc(PH["set", "pad"], 1)
            pool.wait_ge(*when(("set", "pad"), 2))
            pool.dma_start(pad_dram, zpad[0:NAH * 15, :]).then_inc(PH["set", "padrow"], 16)
            pool.wait_ge(*when(("set", "padrow"), 32))

            def lower(u, j=0):
                r = unit_ring[u]
                pool.wait_ge(hi_done, u + 1 + 4 * j)
                pool.tensor_tensor(wlo[:, u % 2], raw[:, r % RING], whi[:, u % 2].bitcast(F32),
                                   ALU.subtract).then_inc(raw_free[r % RING], 1)

            def lowers(u0, u1):
                turns = (u1 - u0) // 4
                if turns > 1:
                    with pool.Fori(0, turns) as j:
                        for b in range(4):
                            lower(u0 + b, j)
                    u0 += 4 * turns
                for u in range(u0, u1):
                    lower(u)

            first = {k: plan[k][0] for k in (("wout", 0, 0), ("in1", "U", 0), ("wout", 1, 0), ("in2", "U", 0),
                                             ("wout", 2, 0))}
            for u in range(0, first["wout", 0, 0]):
                lower(u)
            lowers(first["wout", 0, 0], first["in1", "U", 0])
            for u in range(first["in1", "U", 0], first["wout", 1, 0] + 2):
                lower(u)
            for h in range(NAH):
                pool.wait_ge(*when(("att2", f"bias{h % 2}"), 32 * (h // 2 + 1)))
                pool.tensor_tensor(nabias[h % 2], nabias[h % 2],
                                   namask[:].rearrange("p (a c) -> p a c", a=1).broadcast_to([P, 14, GRID]),
                                   ALU.add).then_inc(PH["att2", "masked"], 1)
            lower(first["wout", 1, 0] + 2)
            lower(first["wout", 1, 0] + 3)
            lowers(first["wout", 1, 0] + 4, first["in2", "U", 0])
            for u in range(first["in2", "U", 0], first["wout", 2, 0]):
                lower(u)
            lowers(first["wout", 2, 0], cnt["u"])

        @block.scalar
        def _(act):
            n_split = cnt["u"]

            def upper(u, j=0):
                r = unit_ring[u]
                act.wait_ge(landed[r % RING], ring_total[r] + 16 * j)
                if u >= 2:
                    act.wait_ge(unit_done, u - 1 + 4 * j)
                act.activation(whi[:, u % 2], raw[:, r % RING], ACT.Copy).then_inc(hi_done, 1)

            chain = [0]

            def link(ins):
                chain[0] += 1
                ins.then_inc(act_step, 1)
                act.wait_ge(act_step, chain[0])

            def residual_squares(i, ctx_too):
                n = T if ctx_too else TX
                for m in range(KD):
                    act.wait_ge(*when((f"res{i}", "x"), m + 1))
                    if m >= 2:
                        act.wait_ge(*when((f"res{i}", "ssq"), m - 1))
                    act.activation(sq[:, m % 2, 0:n], xT[:, m, 0:n], ACT.Square).then_inc(PH[f"res{i}", "sq"], 1)

            def residual_square(i, m, n):
                act.wait_ge(*when((f"res{i}", "x"), m + 1))
                if m >= 2:
                    act.wait_ge(*when((f"res{i}", "ssq"), m - 1))
                act.activation(sq[:, m % 2, 0:n], xT[:, m, 0:n], ACT.Square).then_inc(PH[f"res{i}", "sq"], 1)

            def norm(i, ranges, shift):
                n = sum(r[1] for r in ranges)
                act.wait_ge(*auxiliary(("norm", i)))
                release(act.activation(rsb[:, 0, 0:n], ps(("norm", i), n), ACT.Sqrt, bias=eps[:, 0:1]), ("norm", i))
                act.wait_ge(gfree[group_of(("norm", i)) % 4], group_of(("norm", i)) // 4 + 1)
                act.sem_inc(PH[f"norm{i}", "std"], 1)
                for k in range(KD):
                    act.wait_ge(*when((f"norm{i}", "tmp"), k + 1))
                    for q, (t0, w) in enumerate(ranges):
                        ins = act.activation(hhi[:, k, t0:t0 + w], tmp[:, k % 2, t0:t0 + w], ACT.Identity,
                                             bias=shift(k, q))
                    ins.then_inc(PH[f"norm{i}", "hi"], 1)

            def inputs(st, sums, vts, n_units, other, split=True, prefetch=True):
                vs = sorted(vts)
                done_std = 0
                for n in range(n_units + 1):
                    if n < n_units:
                        key = (st, "U", n)
                        act.wait_ge(*product_of(key))
                        if split:
                            u = plan[key][0] + 2
                            if u < n_split and (prefetch or n + 2 < n_units):
                                upper(u)
                        if n in vts:
                            i = vs.index(n)
                            if i >= 2:
                                act.wait_ge(aux_done, plan[st, "V", vs[i - 2]][0] + 1)
                            ins = act.activation(tmp[:, i % 2, :] if st != "in2" else tmp[:, i % 2, 0:TX],
                                                 ps(key, T if st != "in2" else TX), ACT.Copy)
                            ins.then_inc(PH[st, "vcopy"], 1)
                            if n not in sums:
                                act.wait_ge(*when((st, "vcopy"), i + 1))
                                free(act, key)
                        if n in sums:
                            it = sums[n]
                            s, w = it["s"], it["n"]
                            dst = it["raw"]
                            rows = it["rows"] if not it["kr"] else HD
                            if dst is None:
                                if s >= 2:
                                    act.wait_ge(*when((st, "normed"), normed_before(sums, s - 1)))
                                dst = qr[0:rows, s % 2, 0:w]
                            act.activation(dst, ps(key, w, rows), ACT.Copy)
                            if s >= 2:
                                prev = [m for m in sums if sums[m]["s"] == s - 2][0]
                                act.wait_ge(aux_done, plan[st, "S", prev][0] + 1)
                            act.activation(sq[0:rows, s % 2, 0:w], ps(key, w, rows), ACT.Square).then_inc(PH[st, "square"], 1)
                            act.wait_ge(*when((st, "square"), s + 1))
                            free(act, key)
                        if n in other:
                            other[n](key)
                    if n - 1 in sums and sums[n - 1]["stop"]:
                        it, key = sums[n - 1], (st, "S", n - 1)
                        rows, w = it["rows"], it["n"]
                        act.wait_ge(*auxiliary(key))
                        if done_std >= 2:
                            act.wait_ge(*when((st, "normed"), done_std - 1))
                        root = act.activation(rsb[0:rows, done_std % 2, 0:w], ps(key, w, rows), ACT.Sqrt,
                                              bias=eps[0:rows, 0:1])
                        root.then_inc(PH[st, "std"], 1)
                        done_std += 1

            def attention(i):
                units = ATT[i]
                st = f"att{i}"
                for n in range(len(units) + 1):
                    if i == 2 and n < len(units) and n % 4 == 0:
                        for h in ([0, 1] if n == 0 else [n // 4 + 1]):
                            if h < NAH:
                                if h >= 2:
                                    act.wait_ge(*when((st, "max"), 4 * (h - 1)))
                                for r2 in range(2):
                                    src = bass.AP(pad_dram.tensor, (h * 15 + 1 - r2) * 127,
                                                  [[1, GRID], [127, 14], [1, GRID]])
                                    act.dma_start(nabias[h % 2][GRID * r2:GRID * r2 + GRID], src).then_inc(PH[st, f"bias{h % 2}"], 16)
                    if n < len(units):
                        un = units[n]
                        w = sum(k[2] for k in un["ks"])
                        act.wait_ge(*when((st, "max"), n + 1))
                        if n >= 2:
                            act.wait_ge(*when((st, "turned"), n - 1))
                        g = G[n % 2]
                        if un["kind"] == "plain":
                            ins = act.activation(Pm[:, n % 2, 0:w], g[:, 0:w], ACT.Exp, bias=stat[:, 0, n:n + 1],
                                                 accum_out=stat[:, 1, n:n + 1])
                        elif un["kind"] == "na":
                            act.activation(Pm[:, n % 2, 0:TX], Pm[:, n % 2, 0:TX], ACT.Exp, bias=stat[:, 0, n:n + 1],
                                           accum_out=stat[:, 1, n:n + 1])
                            ins = act.activation(Pm[:, n % 2, TX:T], g[:, TX:T], ACT.Exp, bias=stat[:, 0, n:n + 1],
                                                 accum_out=stat[:, 2, n:n + 1])
                        else:
                            ins = act.activation(Pm[:, n % 2, 0:w], Pm[:, n % 2, 0:w], ACT.Exp, bias=stat[:, 0, n:n + 1],
                                                 accum_out=stat[:, 1, n:n + 1])
                        ins.then_inc(PH[st, "prob"], 1)
                    if n >= 1:
                        m = n - 1
                        w = sum(k[2] for k in units[m]["ks"])
                        act.wait_ge(*when((st, "turned"), m + 1))
                        if m >= 2:
                            act.wait_ge(*when((st, "pv"), m - 1))
                        act.activation(PT[:, m % 2, 0:w], G[2][:, 0:w], ACT.Copy).then_inc(PH[st, "pt"], 1)

            def output_tiles(i, n_tiles, w, dst_hi, t0, scale=None, gated=()):
                for m in range(n_tiles):
                    key = (f"ot{i}", "OT", m)
                    act.wait_ge(*auxiliary(key))
                    s = 1.0 if scale is None else scale(m)
                    if m in gated:
                        act.wait_ge(*when((f"ot{i}", "done"), m - 1))
                        act.activation(tmp[:, m % 2, 0:w], ps(key, w), ACT.Copy, scale=s).then_inc(PH[f"ot{i}", "a"], 1)
                        act.wait_ge(*when((f"ot{i}", "b"), 1 + sorted(gated).index(m)))
                        ins = act.activation(dst_hi[:, t0 + m, 0:w], tmp[:, m % 2, 0:w], ACT.Copy)
                    else:
                        ins = act.activation(dst_hi[:, t0 + m, 0:w], ps(key, w), ACT.Copy, scale=s)
                    ins.then_inc(PH[f"ot{i}", "hi"], 1)

            def wout(l, i, n):
                for m in range(KD):
                    act.wait_ge(*product_of(("wout", l, m)))
                    upper(plan["wout", l, m][0] + 2)
                    residual_square(i, m, n)

            def ffn(l, chunks, ranges, last_i):
                n = sum(r[1] for r in ranges)
                sems = f"ffn{l}"
                tiles = 0
                for c, (f0, nf) in enumerate(chunks):
                    key0 = ("up", l, c, 0)
                    u0 = plan[key0][0]
                    if c:
                        act.wait_ge(unit_done, plan["down", l, c - 1, KD - 1][0] + 1)

                    def gated_turn(j):
                        for b in range(4):
                            act.wait_ge(unit_done, u0 + b + 1 + 4 * j)
                            upper(u0 + b + 2, j)
                            t = tiles + b // 2
                            if b % 2 == 0:
                                if t >= 2 or not isinstance(j, int):
                                    act.wait_ge(*when((sems, "prod"), t - 1 + 2 * j))
                                g = (plan[key0][2] + b) % 4
                                act.activation(qr[:, b // 2, 0:n], G[g][:, 0:n], ACT.Silu).then_inc(PH[sems, "act"], 1)
                            else:
                                act.wait_ge(*when((sems, "prod"), t + 1 + 2 * j))
                                act.activation(ahi[:, bass.ds(j * 2 + b // 2, 1), 0:n] if not isinstance(j, int)
                                               else ahi[:, b // 2 + 2 * j:b // 2 + 2 * j + 1, 0:n],
                                               sq[:, b // 2:b // 2 + 1, 0:n], ACT.Copy).then_inc(PH[sems, "hi"], 1)

                    def plain_turn(j):
                        for b in range(4):
                            act.wait_ge(unit_done, u0 + b + 1 + 4 * j)
                            upper(u0 + b + 2, j)
                            t = tiles + b
                            if t >= 2 or not isinstance(j, int):
                                act.wait_ge(*when((sems, "lo"), t - 1 + 4 * j))
                            g = (plan[key0][2] + b) % 4
                            ins = act.activation(qr[:, b % 2, 0:n], G[g][:, 0:n], ACT.Relu)
                            ins.then_inc(PH[sems, "act"], 1)
                            act.wait_ge(*when((sems, "prod"), t + 1 + 4 * j))
                            act.activation(ahi[:, bass.ds(j * 4 + b, 1), 0:n] if not isinstance(j, int)
                                           else ahi[:, b + 4 * j:b + 4 * j + 1, 0:n],
                                           sq[:, b % 2:b % 2 + 1, 0:n], ACT.Copy).then_inc(PH[sems, "hi"], 1)

                    turn = plain_turn if l == 2 else gated_turn
                    per = 4 if l == 2 else 2
                    turn(0)
                    if nf // per > 1:
                        with act.Fori(1, nf // per) as j:
                            turn(j)
                    tiles += nf
                    last = c == len(chunks) - 1
                    for m in range(KD):
                        act.wait_ge(*product_of(("down", l, c, m)))
                        u = plan["down", l, c, m][0] + 2
                        if u < n_split:
                            upper(u)
                        if last and last_i is not None:
                            residual_square(last_i, m, n)

            act_step = PH["set", "silu"]
            act.wait_ge(*when(("set", "cols"), 2))
            act.activation(cs[:, :, 0], vcol[:, 1, VC["c"]:VC["c"] + 8], ACT.Silu)
            act.activation(cs[:, :, 1], vcol[:, 1, VC["c_ctx"]:VC["c_ctx"] + 8], ACT.Silu).then_inc(PH["set", "silu"], 1)
            residual_squares(0, True)
            upper(0)
            upper(1)
            norm(0, X_CTX, lambda k, q: mod[:, 0, k, q:q + 1])

            def pool_tile(i):
                def f(key):
                    g = ps(key)
                    act.activation(upad[:, i, 8:8 + TX], g[:, 0:TX], ACT.Copy)
                    ins = act.activation(upad[:, i, 24 + TX:24 + T], g[:, TX:T], ACT.Copy)
                    release(ins, key)
                return f

            inputs("in0", S0, (2, 3), 12, {0: pool_tile(0), 1: pool_tile(1)})
            for i in range(2):
                key = ("pool", i)
                act.wait_ge(*auxiliary(key))
                act.activation(hhi[:, i, :], ps(key), ACT.Copy, scale=vc("pscale", i)).then_inc(PH["in0", "pooly"], 1)
            attention(0)
            output_tiles(0, 6, T, hhi, 2)
            wout(0, 1, T)
            norm(1, X_CTX, lambda k, q: mod[:, 0, 24 + k, q:q + 1])
            ffn(0, FFN_CHUNKS, X_CTX, 2)
            norm(2, X_CTX, lambda k, q: mod[:, 1, k, q:q + 1])

            act.dma_start(rope[:], A["rope"][:, 2:4]).then_inc(PH["set", "rope1"], 16)

            def kr_rows(key):
                g = ps(key)
                ins = act.activation(krbuf[HD:MQK, :], g[HD:MQK, :], ACT.Copy)
                ins.then_inc(PH["in1", "kr"], 1)
                act.wait_ge(*when(("in1", "kr"), 1))
                free(act, key)

            inputs("in1", S1, (14, 15, 16, 17), 18, {5: kr_rows}, prefetch=False)
            inputs("mq", SQ, (), MH, {}, split=False)
            act.wait_ge(*when(("mq", "normed"), MH))
            act.wait_ge(aux_done, plan["mq", "S", MH - 1][0] + 1)
            for s in range(2):
                act.activation(qr[HD:MQK, s, :], krbuf[HD:MQK, :], ACT.Copy)
                act.activation(sq[HD:MQK, s, :], krbuf[HD:MQK, :], ACT.Square)
            inputs("mk", SK, tuple(range(MH)), MH, {}, split=False)
            upper(plan["wout", 1, 0][0])
            upper(plan["wout", 1, 1][0])
            attention(1)
            output_tiles(1, 4, TX, hhi, 0)
            attention(2)
            output_tiles(2, 4, TX, hhi, 4)
            wout(1, 3, TX)
            norm(3, X_ONLY, lambda k, q: mod[:, 1, 24 + k, q:q + 1])
            ffn(1, FFN_CHUNKS, X_ONLY, 4)
            norm(4, X_ONLY, lambda k, q: zero8[:, k:k + 1])

            def forget(key):
                g = ps(key, TX, N_FOX)
                act.wait_ge(*when(("set", "b"), 16))
                act.wait_ge(*when(("mk", "rotated"), MH))
                link2(act.activation(cum[0:N_FOX, :], g, ACT.Identity, bias=bfox[:, 0:1]))
                link2(act.activation(lsig[0:N_FOX, :], cum[0:N_FOX, :], ACT.Abs))
                link2(act.activation(lsig[0:N_FOX, :], lsig[0:N_FOX, :], ACT.Exp, scale=-1.0))
                link2(act.activation(lsig[0:N_FOX, :], lsig[0:N_FOX, :], ACT.Ln, bias=1.0))
                free(act, key)

            fcount = [0]

            def link2(ins):
                fcount[0] += 1
                ins.then_inc(PH["in2", "fg"], 1)
                act.wait_ge(*when(("in2", "fg"), fcount[0]))

            def out_gate(i):
                def f(key):
                    release(act.activation(gsig[:, i, :], ps(key, TX), ACT.Sigmoid), key)
                return f

            inputs("in2", S2, tuple(range(16, 24)), 28, {24: forget, 25: out_gate(0), 26: out_gate(1), 27: out_gate(2)})
            act.wait_ge(unit_done, plan["in2", "U", 27][0] + 1)
            act.dma_start(band, A["band"]).then_inc(PH["set", "band"], 16)
            act.dma_start(sel[0:N_FOX], A["sel"]).then_inc(PH["set", "band"], 16)
            attention(3)
            act.wait_ge(*when(("att3", "o"), len(ATT[3])))
            groups = ((0, 256), (256, 384), (640, 384))
            for q in range(4):
                for gi, (c0, w) in enumerate(groups):
                    ins = act.activation(tmp[:, 0, 0:w], o2[:, q, c0:c0 + w], ACT.Square, accum_out=ss12[:, 0, gi, q:q + 1])
                    ins.then_inc(PH["in2", "outsq"], 1)
                    act.wait_ge(*when(("in2", "outsq"), 3 * q + gi + 1))
            act.activation(ss12[:, 1, 0:1, :], ss12[:, 0, 0:1, :], ACT.Sqrt, bias=eps[:, 0:1], scale=1.0 / 256)
            act.activation(ss12[:, 1, 1:3, :], ss12[:, 0, 1:3, :], ACT.Sqrt, bias=eps[:, 0:1],
                           scale=1.0 / 384).then_inc(PH["in2", "outstd"], 1)
            output_tiles(3, 8, TX, ahi, 0, lambda m: vc("og2", m), (2, 3, 4))
            wout(2, 5, TX)
            norm(5, X_ONLY, lambda k, q: zero8[:, k:k + 1])
            ffn(2, FF2_CHUNKS, X_ONLY, None)

        @block.tensor
        def _(pe):
            def take_group(g):
                if g >= 4:
                    pe.wait_ge(gfree[g % 4], g // 4)

            def unit(key, rhi, rlo, ranges, k_tiles=KD, j=0, h_ready=None):
                u, r, g = plan[key]
                pe.wait_ge(raw_free[r % RING], r // RING + 1 + j)
                if g >= 4:
                    pe.wait_ge(gfree[g % 4], g // 4 + j)
                for k in range(k_tiles):
                    if h_ready is not None:
                        pe.wait_ge(*when(h_ready, k + 1))
                    for t0, w in ranges:
                        o = G[g % 4][:, t0:t0 + w]
                        pe.matmul(o, whi[:, u % 2, k], rlo[:, k, t0:t0 + w], start=k == 0, stop=False)
                        pe.matmul(o, wlo[:, u % 2, k], rhi[:, k, t0:t0 + w], start=False, stop=False)
                        mm = pe.matmul(o, whi[:, u % 2, k], rhi[:, k, t0:t0 + w], start=False, stop=k == k_tiles - 1)
                mm.then_inc(unit_done, 1)

            def direct(key, x, m, ranges, k_tiles):
                _, r, g = plan[key]
                pe.wait_ge(landed[r % RING], ring_total[r])
                take_group(g)
                for k in range(k_tiles):
                    for t0, w in ranges:
                        mm = pe.matmul(G[g % 4][0:m, t0:t0 + w], raw[:, r % RING, k, 0:m], x[:, k, t0:t0 + w],
                                       start=k == 0, stop=k == k_tiles - 1)
                mm.then_inc(raw_free[r % RING], 1)

            def aux(mm):
                mm.then_inc(aux_done, 1)

            def norm(i, n):
                a, g = plan["norm", i]
                pe.wait_ge(*when((f"res{i}", "ssq"), KD))
                take_group(g)
                for t0 in range(0, n, 512):
                    w = min(512, n - t0)
                    mm = pe.matmul(G[g % 4][:, t0:t0 + w], ones_d, ssq[:, t0:t0 + w], start=True, stop=True)
                aux(mm)

            def inputs(st, sums, vts, rhs, n_units, ranges_of, h_ready=None, direct_of=None):
                vs = sorted(vts)
                for op, n in plan[st, "seq"]:
                    if op == "U":
                        if direct_of is not None:
                            direct_of((st, "U", n))
                        else:
                            unit((st, "U", n), rhs[0], rhs[1], ranges_of(n), h_ready=h_ready if n == 0 else None)
                        continue
                    a, g = plan[st, op, n]
                    if op == "V":
                        i = vs.index(n)
                        pe.wait_ge(*when((st, "vcopy"), i + 1))
                        take_group(g)
                        tiles = 4 if st == "in2" else 6
                        for t in range(tiles):
                            mm = pe.transpose(G[g % 4][:, P * t:P * t + P], tmp[:, i % 2, P * t:P * t + P], ident)
                    elif op == "S":
                        it = sums[n]
                        pe.wait_ge(*when((st, "square"), it["s"] + 1))
                        if it["start"]:
                            take_group(g)
                        rows = it["rows"]
                        for t0 in range(0, it["n"], 512):
                            w = min(512, it["n"] - t0)
                            mm = pe.matmul(G[g % 4][0:rows, t0:t0 + w], it["mat"][0:rows, 0:rows],
                                           sq[0:rows, it["s"] % 2, t0:t0 + w], start=it["start"], stop=it["stop"])
                    else:
                        it = sums[n]
                        pe.wait_ge(*when((st, "normed"), normed_before(sums, it["s"] + 1)))
                        take_group(g)
                        rows = it["rows"]
                        m = rot64 if rows == P else rot32
                        mm = pe.matmul(G[g % 4][0:rows, 0:TX], m[0:rows, 0:rows], it["dst"][:, 0:TX], start=True, stop=True)
                    aux(mm)

            def attention(i, g_done):
                st = f"att{i}"
                units = ATT[i]
                for q in range(4):
                    uses = (g_done - q + 3) // 4
                    if uses > 0:
                        pe.wait_ge(gfree[q], uses)
                for n in range(len(units) + 2):
                    if n < len(units):
                        un = units[n]
                        if n >= 2:
                            pe.wait_ge(*when((st, "prob"), n - 1))
                        fox = un.get("fox")
                        for q, (kt, c0, w) in enumerate(un["ks"]):
                            o = G[n % 2][:, c0:c0 + w]
                            mm = pe.matmul(o, un["q"], kt, start=True, stop=fox is None)
                            if fox is not None:
                                mm = pe.matmul(o, sel[0:N_FOX, fox, :], cum[0:N_FOX, 0:w], start=False, stop=True)
                        mm.then_inc(PH[st, "scores"], 1)
                    if 1 <= n <= len(units):
                        m = n - 1
                        pe.wait_ge(*when((st, "prob"), m + 1))
                        if m >= 1:
                            pe.wait_ge(*when((st, "pt"), m))
                        for t in range(len(units[m]["vs"])):
                            mm = pe.transpose(G[2][:, P * t:P * t + P], Pm[:, m % 2, P * t:P * t + P], ident)
                        mm.then_inc(PH[st, "turned"], 1)
                    if n >= 2:
                        m = n - 2
                        pe.wait_ge(*when((st, "pt"), m + 1))
                        if m >= 2:
                            pe.wait_ge(*when((st, "o"), m - 1))
                        vs = units[m]["vs"]
                        for t, v in enumerate(vs):
                            mm = pe.matmul(G[3][:, 512 * (m % 2):512 * (m % 2) + HD], PT[:, m % 2, P * t:P * t + P], v,
                                           start=t == 0, stop=t == len(vs) - 1)
                        mm.then_inc(PH[st, "pv"], 1)

            def turn_outputs(i, n_tiles, o, tiles, ready, value):
                pe.wait_ge(*when(ready, value))
                for m in range(n_tiles):
                    a, g = plan[f"ot{i}", "OT", m]
                    take_group(g)
                    for t in range(tiles):
                        mm = pe.transpose(G[g % 4][:, P * t:P * t + P], o[:, t, P * m:P * m + P], ident)
                    aux(mm)

            def wout(l, rhs, ranges):
                for m in range(KD):
                    unit(("wout", l, m), rhs[0], rhs[1], ranges)

            def ffn(l, chunks, ranges, h_ready):
                per = 4 if l == 2 else 2
                tiles = 0
                for c, (f0, nf) in enumerate(chunks):
                    if c == 0:
                        unit(("up", l, 0, 0), hhi, hlo, ranges, h_ready=h_ready)
                        for b in range(1, 4):
                            unit(("up", l, 0, b), hhi, hlo, ranges)
                    with pe.Fori(1 if c == 0 else 0, nf // per) as j:
                        for b in range(4):
                            unit(("up", l, c, b), hhi, hlo, ranges, j=j)
                    tiles += nf
                    pe.wait_ge(*when((f"ffn{l}", "lo"), tiles))
                    with pe.Fori(0, 2) as j:
                        for b in range(4):
                            unit(("down", l, c, b), ahi, alo, ranges, k_tiles=nf, j=j)

            pe.wait_ge(*when(("set", "tables"), 48))
            pe.wait_ge(*when(("set", "rows"), 16 * 26))
            a, g = plan["vec"]
            pe.transpose(G[g % 4][:, 0:P], vrow[:, 0, :], ident)
            aux(pe.transpose(G[g % 4][:, P:P + VROWS2], vrow[0:VROWS2, 1, :], ident[0:VROWS2, 0:VROWS2]))
            pe.wait_ge(*when(("set", "silu"), 1))
            for l in range(2):
                r0 = plan["ada", l]
                a, g = plan["adag", l]
                with pe.Fori(0, 12) as j:
                    for b in range(4):
                        r = r0 + b
                        pe.wait_ge(landed[r % RING], ring_total[r] + 16 * j)
                        for k in range(KD):
                            mm = pe.matmul(G[g % 4][:, bass.ds(j * 8 + 2 * b, 2)], raw[:, r % RING, k], cs[:, k, :],
                                           start=k == 0, stop=k == KD - 1)
                        mm.then_inc(raw_free[r % RING], 1)
                pe.matmul(G[g % 4][:, 512:514], ident, cs[:, 0, :], start=True, stop=True).then_inc(aux_done, 1)
                if l == 0:
                    pe.wait_ge(*when(("set", "xload"), 32))
            for m in range(KD):
                a, g = plan["xin", m]
                take_group(g)
                for t in range(6):
                    mm = pe.transpose(G[g % 4][:, P * t:P * t + P], xtok[:, t, P * m:P * m + P], ident)
                aux(mm)
            norm(0, T)
            inputs("in0", S0, (2, 3), (hhi, hlo), 12, lambda n: X_CTX, h_ready=("norm0", "h"))
            pe.wait_ge(*when(("in0", "pooled"), 1))
            pe.wait_ge(*when(("set", "poolw"), 64))
            for i in range(2):
                a, g = plan["pool", i]
                take_group(g)
                for t0, w in X_CTX:
                    mm = pe.matmul(G[g % 4][:, t0:t0 + w], poolw[:, i, :], dT[:, i, t0:t0 + w], start=True, stop=True)
                aux(mm)
            pe.wait_ge(*when(("in0", "rotated"), 8))
            pe.wait_ge(*when(("in0", "vdone"), 2))
            attention(0, group_of(("pool", 1)) + 1)
            turn_outputs(0, 6, o0, 6, ("att0", "o"), len(ATT[0]))
            pe.wait_ge(*when(("ot0", "done"), 6))
            pe.wait_ge(*when(("in0", "pooldone"), 2))
            wout(0, (hhi, hlo), X_CTX)
            norm(1, T)
            ffn(0, FFN_CHUNKS, X_CTX, ("norm1", "h"))
            norm(2, T)
            inputs("in1", S1, (14, 15, 16, 17), (hhi, hlo), 18,
                   lambda n: X_ONLY if n < 3 or 6 <= n < 10 else X_CTX, h_ready=("norm2", "h"))
            pe.wait_ge(*when(("in1", "normed"), 2))
            inputs("mq", SQ, (), None, MH, None, direct_of=lambda key: direct(key, cqn, MQK, X_ONLY, 3))
            inputs("mk", SK, range(MH), None, MH, None, direct_of=lambda key: direct(key, ckvn, P, X_CTX, 2))
            pe.wait_ge(*when(("mq", "rotated"), MH))
            pe.wait_ge(*when(("mk", "rotated"), MH))
            pe.wait_ge(*when(("mk", "vdone"), MH))
            attention(1, group_of(("mk", "R", MH - 1)) + 1)
            turn_outputs(1, 4, omla, 4, ("att1", "o"), len(ATT[1]))
            pe.wait_ge(*when(("in1", "vdone"), 4))
            pe.wait_ge(*when(("in1", "normed"), 10))
            attention(2, group_of(("ot1", "OT", 3)) + 1)
            turn_outputs(2, 4, ona, 4, ("att2", "o"), len(ATT[2]))
            pe.wait_ge(*when(("ot1", "done"), 4))
            pe.wait_ge(*when(("ot2", "done"), 4))
            wout(1, (hhi, hlo), X_ONLY)
            norm(3, TX)
            ffn(1, FFN_CHUNKS, X_ONLY, ("norm3", "h"))
            norm(4, TX)
            inputs("in2", S2, tuple(range(16, 24)), (hhi, hlo), 28, lambda n: X_ONLY, h_ready=("norm4", "h"))
            pe.wait_ge(*when(("in2", "normed"), 16))
            pe.wait_ge(*when(("in2", "vdone"), 8))
            pe.wait_ge(*when(("in2", "cum"), 1))
            pe.wait_ge(*when(("set", "band"), 32))
            attention(3, group_of(("in2", "U", 27)) + 1)
            turn_outputs(3, 8, o2, 4, ("in2", "outn"), 12)
            pe.wait_ge(*when(("ot3", "done"), 8))
            wout(2, (ahi, alo), X_ONLY)
            norm(5, TX)
            ffn(2, FF2_CHUNKS, X_ONLY, ("norm5", "h"))
            pe.wait_ge(*when(("fin", "x"), KD))
            for t in range(4):
                a, g = plan["xout", t]
                take_group(g)
                for m in range(KD):
                    mm = pe.transpose(G[g % 4][:, P * m:P * m + P], xT[:, m, P * t:P * t + P], ident)
                aux(mm)

        @block.vector
        def _(dve):
            dve_step = PH["set", "steps"]
            chain = [0]

            def mark(ins):
                chain[0] += 1
                return ins.then_inc(dve_step, 1)

            def link(ins):
                mark(ins)
                dve.wait_ge(dve_step, chain[0])

            def sum_squares(i, m, n):
                dve.wait_ge(*when((f"res{i}", "sq"), m + 1))
                if m == 0:
                    ins = dve.tensor_copy(ssq[:, 0:n], sq[:, 0, 0:n])
                else:
                    dve.wait_ge(*when((f"res{i}", "ssq"), m))
                    ins = dve.tensor_tensor(ssq[:, 0:n], ssq[:, 0:n], sq[:, m % 2, 0:n], ALU.add)
                ins.then_inc(PH[f"res{i}", "ssq"], 1)

            def norm(i, ranges, gain, shift):
                n = sum(r[1] for r in ranges)
                dve.wait_ge(*when((f"norm{i}", "std"), 1))
                link(dve.reciprocal(rsb[:, 0, 0:n], rsb[:, 0, 0:n]))
                for k in range(KD + 1):
                    if k < KD:
                        if k >= 2:
                            dve.wait_ge(*when((f"norm{i}", "h"), k - 1))
                        for q, (t0, w) in enumerate(ranges):
                            ins = dve.scalar_tensor_tensor(out=tmp[:, k % 2, t0:t0 + w], in0=xT[:, k, t0:t0 + w],
                                                           scalar=gain(k, q), in1=rsb[:, 0, t0:t0 + w],
                                                           op0=ALU.mult, op1=ALU.mult)
                        ins.then_inc(PH[f"norm{i}", "tmp"], 1)
                    if k >= 1:
                        dve.wait_ge(*when((f"norm{i}", "hi"), k))
                        for q, (t0, w) in enumerate(ranges):
                            ins = dve.scalar_tensor_tensor(out=hlo[:, k - 1, t0:t0 + w], in0=tmp[:, (k - 1) % 2, t0:t0 + w],
                                                           scalar=shift(k - 1, q),
                                                           in1=hhi[:, k - 1, t0:t0 + w].bitcast(F32),
                                                           op0=ALU.add, op1=ALU.subtract)
                        ins.then_inc(PH[f"norm{i}", "h"], 1)

            def inputs(st, sums, vts, n_units, vdst, extra=None):
                vs = sorted(vts)
                done = rotated = 0
                for n in range(1, n_units + 2):
                    if n - 1 in vts:
                        key, i = (st, "V", n - 1), vs.index(n - 1)
                        dve.wait_ge(*auxiliary(key))
                        vdst(i, key)
                    if n - 1 in sums and sums[n - 1]["stop"]:
                        it, key = sums[n - 1], (st, "S", n - 1)
                        rows, w = it["rows"], it["n"]
                        dve.wait_ge(*when((st, "std"), done + 1))
                        rs = rsb[0:rows, done % 2, 0:w]
                        release(dve.reciprocal(rs, rs), key)
                        dve.wait_ge(gfree[group_of(key) % 4], group_of(key) // 4 + 1)
                        members = it["members"] or [(qr[0:rows, it["s"] % 2, 0:w], it["dst"][:, 0:w], it["gain"])]
                        for src, dst, gain in members:
                            ins = dve.scalar_tensor_tensor(out=dst, in0=src, scalar=gain[0:rows], in1=rs,
                                                           op0=ALU.mult, op1=ALU.mult)
                        ins.then_inc(PH[st, "normed"], 1)
                        done += 1
                    if n - 2 in sums and sums[n - 2]["rope"]:
                        it, key = sums[n - 2], (st, "R", n - 2)
                        rows = it["rows"]
                        dve.wait_ge(*auxiliary(key))
                        if rotated:
                            dve.wait_ge(*when((st, "rotated"), rotated))
                        rotated += 1
                        release(dve.tensor_tensor(rt[0:rows, 0, :], ps(key, TX, rows), rope[0:rows, 1, :], ALU.mult), key)
                        link(dve.tensor_tensor(rt[0:rows, 1, :], it["dst"][:, 0:TX], rope[0:rows, 0, :], ALU.mult))
                        dve.wait_ge(gfree[group_of(key) % 4], group_of(key) // 4 + 1)
                        dve.tensor_tensor(it["dst"][:, 0:TX], rt[0:rows, 1, :], rt[0:rows, 0, :],
                                          ALU.add).then_inc(PH[st, "rotated"], 1)
                    if extra and n in extra:
                        extra[n]()

            def attention(i):
                st = f"att{i}"
                units = ATT[i]
                for n in range(len(units) + 2):
                    if n < len(units):
                        un = units[n]
                        w = sum(k[2] for k in un["ks"])
                        g = G[n % 2]
                        if un["kind"] == "na" and n % 4 == 0:
                            dve.wait_ge(*when((st, "masked"), un["head"] + 1))
                        if un["kind"] == "band" and n % 4 == 0 and un["fox"] is None:
                            h = un["head"]
                            moba = h < N_MOBA
                            slope = SLOPES[N_DIL + h] if moba else SLOPES[h - N_MOBA - N_FOX]
                            if n == 0:
                                dve.wait_ge(*when(("set", "band"), 32))
                            if h >= 2:
                                dve.wait_ge(*when((st, "max"), 4 * (h - 1)))
                            if moba:
                                link(dve.tensor_scalar(th[:, h % 2], band[:, 0], -slope, None, ALU.mult))
                            else:
                                link(dve.scalar_tensor_tensor(out=th[:, h % 2], in0=band[:, 1], scalar=-slope,
                                                              in1=band[:, 2], op0=ALU.mult, op1=ALU.add))
                        dve.wait_ge(*when((st, "scores"), n + 1))
                        if un["kind"] == "plain":
                            dve.tensor_reduce(stat[:, 0, n:n + 1], g[:, 0:w], AX_X, ALU.max,
                                              negate=True).then_inc(PH[st, "max"], 1)
                        else:
                            if n >= 2:
                                dve.wait_ge(*when((st, "turned"), n - 1))
                            wb = TX if un["kind"] == "na" else w
                            dst, src = Pm[:, n % 2, 0:wb], g[:, 0:wb]
                            if un["kind"] == "na":
                                dst, src = (v.rearrange("p (a b) -> p a b", b=GRID) for v in (dst, src))
                            mark(dve.tensor_tensor(dst, src, un["bias"], ALU.add))
                            dve.wait_ge(dve_step, chain[0])
                            if un["kind"] == "na":
                                mark(dve.tensor_reduce(stat[:, 2, n:n + 1], Pm[:, n % 2, 0:wb], AX_X, ALU.max, negate=True))
                                link(dve.tensor_reduce(stat[:, 3, n:n + 1], g[:, TX:T], AX_X, ALU.max, negate=True))
                                dve.tensor_tensor(stat[:, 0, n:n + 1], stat[:, 2, n:n + 1], stat[:, 3, n:n + 1],
                                                  ALU.min).then_inc(PH[st, "max"], 1)
                            else:
                                dve.tensor_reduce(stat[:, 0, n:n + 1], Pm[:, n % 2, 0:wb], AX_X, ALU.max,
                                                  negate=True).then_inc(PH[st, "max"], 1)
                    if n >= 2:
                        m = n - 2
                        dve.wait_ge(*when((st, "pv"), m + 1))
                        total = stat[:, 1, m:m + 1]
                        if units[m]["kind"] == "na":
                            link(dve.tensor_tensor(total, total, stat[:, 2, m:m + 1], ALU.add))
                        link(dve.reciprocal(stat[:, 3, m:m + 1], total))
                        dve.tensor_scalar(units[m]["o"], G[3][:, 512 * (m % 2):512 * (m % 2) + HD],
                                          stat[:, 3, m:m + 1], None, ALU.mult).then_inc(PH[st, "o"], 1)

            def output_tiles(i, n_tiles, w, dst_hi, dst_lo, t0, scale=None, gated=()):
                for m in range(n_tiles):
                    key = (f"ot{i}", "OT", m)
                    if m in gated:
                        gi = sorted(gated).index(m)
                        dve.wait_ge(*when((f"ot{i}", "a"), gi + 1))
                        t = tmp[:, m % 2, 0:w]
                        dve.tensor_tensor(t, t, gsig[:, gi, 0:w], ALU.mult).then_inc(PH[f"ot{i}", "b"], 1)
                        dve.wait_ge(*when((f"ot{i}", "hi"), m + 1))
                        ins = dve.tensor_tensor(dst_lo[:, t0 + m, 0:w], t, dst_hi[:, t0 + m, 0:w].bitcast(F32), ALU.subtract)
                    else:
                        dve.wait_ge(*when((f"ot{i}", "hi"), m + 1))
                        s = 1.0 if scale is None else scale(m)
                        ins = dve.scalar_tensor_tensor(out=dst_lo[:, t0 + m, 0:w], in0=ps(key, w), scalar=s,
                                                       in1=dst_hi[:, t0 + m, 0:w].bitcast(F32), op0=ALU.mult, op1=ALU.subtract)
                    ins.then_inc(PH[f"ot{i}", "done"], 1)
                    dve.wait_ge(*when((f"ot{i}", "done"), m + 1))
                    free(dve, key)

            def residual(key, m, ranges, gate, j=0, dyn=False):
                g = group_of(key) % 4
                for q, (t0, w) in enumerate(ranges):
                    x = xT[:, bass.ds(j * 4 + m, 1), t0:t0 + w] if dyn else xT[:, m:m + 1, t0:t0 + w]
                    src = G[g][:, t0:t0 + w].rearrange("p (a t) -> p a t", a=1)
                    if gate is None:
                        ins = dve.tensor_tensor(x, src, x, ALU.add)
                    else:
                        ins = dve.scalar_tensor_tensor(out=x, in0=src, scalar=gate(m, q, j, dyn), in1=x,
                                                       op0=ALU.mult, op1=ALU.add)
                return ins

            def residual_tiles(keys, i, ranges, gate):
                n = sum(r[1] for r in ranges)
                for m in range(KD + 1):
                    if m < KD:
                        dve.wait_ge(*product_of(keys(m)))
                        ins = residual(keys(m), m, ranges, gate)
                        ins.then_inc(PH[f"res{i}", "x"] if i is not None else PH["fin", "x"], 1)
                        dve.wait_ge(*when((f"res{i}", "x") if i is not None else ("fin", "x"), m + 1))
                        free(dve, keys(m))
                    if m >= 1 and i is not None:
                        sum_squares(i, m - 1, n)

            def gate_of(l, at):
                def f(m, q, j, dyn):
                    if dyn:
                        return mod[:, l, bass.ds(j * 4 + (at + m), 1), q:q + 1].rearrange("p a b -> p (a b)")
                    return mod[:, l, at + m, q:q + 1]
                return f

            def ffn(l, chunks, ranges, gate, last_i):
                n = sum(r[1] for r in ranges)
                sems = f"ffn{l}"
                tiles = 0
                for c, (f0, nf) in enumerate(chunks):
                    key0 = ("up", l, c, 0)
                    u0, _, g0 = plan[key0]

                    def tile_at(j, per, b):
                        if isinstance(j, int):
                            return slice(per * j + b, per * j + b + 1)
                        return bass.ds(j * per + b, 1)

                    def gated_turn(j):
                        for b in range(2):
                            t = tiles + b
                            dve.wait_ge(unit_done, u0 + 2 * b + 2 + 4 * j)
                            dve.wait_ge(*when((sems, "act"), t + 1 + 2 * j))
                            if t >= 2 or not isinstance(j, int):
                                dve.wait_ge(*when((sems, "lo"), t - 1 + 2 * j))
                            gg, gu = (g0 + 2 * b) % 4, (g0 + 2 * b + 1) % 4
                            dve.tensor_tensor(sq[:, b, 0:n], G[gu][:, 0:n], qr[:, b, 0:n], ALU.mult).then_inc(PH[sems, "prod"], 1)
                            dve.wait_ge(*when((sems, "prod"), t + 1 + 2 * j))
                            dve.sem_inc(gfree[gg], 1)
                            dve.sem_inc(gfree[gu], 1)
                            dve.wait_ge(*when((sems, "hi"), t + 1 + 2 * j))
                            dve.tensor_tensor(alo[:, tile_at(j, 2, b), 0:n], sq[:, b:b + 1, 0:n],
                                              ahi[:, tile_at(j, 2, b), 0:n].bitcast(F32),
                                              ALU.subtract).then_inc(PH[sems, "lo"], 1)

                    def plain_turn(j):
                        for b in range(4):
                            t = tiles + b
                            dve.wait_ge(*when((sems, "act"), t + 1 + 4 * j))
                            dve.tensor_tensor(sq[:, b % 2, 0:n], qr[:, b % 2, 0:n], qr[:, b % 2, 0:n],
                                              ALU.mult).then_inc(PH[sems, "prod"], 1)
                            dve.sem_inc(gfree[(g0 + b) % 4], 1)
                            dve.wait_ge(*when((sems, "hi"), t + 1 + 4 * j))
                            dve.tensor_tensor(alo[:, tile_at(j, 4, b), 0:n], sq[:, b % 2:b % 2 + 1, 0:n],
                                              ahi[:, tile_at(j, 4, b), 0:n].bitcast(F32),
                                              ALU.subtract).then_inc(PH[sems, "lo"], 1)

                    turn = plain_turn if l == 2 else gated_turn
                    per = 4 if l == 2 else 2
                    turn(0)
                    if nf // per > 1:
                        with dve.Fori(1, nf // per) as j:
                            turn(j)
                    tiles += nf
                    if c == len(chunks) - 1:
                        residual_tiles(lambda m: ("down", l, c, m), last_i, ranges, gate)
                    else:
                        with dve.Fori(0, 2) as j:
                            for b in range(4):
                                key = ("down", l, c, b)
                                dve.wait_ge(*product_of(key, j))
                                residual(key, b, ranges, gate, j, dyn=True).then_inc(gfree[group_of(key) % 4], 1)

            mark(dve.memset(eps[:], EPS))
            mark(dve.memset(zero8[:], 0.0))
            mark(dve.memset(stat[:], 0.0))
            dve.wait_ge(*auxiliary("vec"))
            link(dve.tensor_copy(vcol[:, 0, :], ps("vec")[:, 0:P]))
            key = "vec"
            dve.tensor_copy(vcol[:, 1, 0:VROWS2], ps("vec")[:, P:P + VROWS2]).then_inc(PH["set", "cols"], 1)
            dve.wait_ge(*when(("set", "cols"), 1))
            scaled = ((VC["q2"], 8, HD), (VC["q0"], 1, HD), (VC["nq"], 1, HD), (VC["mq"], 1, MQK))
            for c0, w, d in scaled:
                ins = mark(dve.tensor_scalar(vcol[:, 1, c0:c0 + w], vcol[:, 1, c0:c0 + w], float(d) ** -0.5, None, ALU.mult))
            dve.wait_ge(dve_step, chain[0])
            dve.sem_inc(PH["set", "cols"], 1)
            free(dve, "vec")
            for l in range(2):
                key = ("adag", l)
                dve.wait_ge(*auxiliary(key))
                link(dve.tensor_tensor(mod[:, l], ps(key, 96).rearrange("p (a b) -> p a b", b=2),
                                       vcol[:, 0, 64 * l:64 * l + 48].rearrange("p (a b) -> p a b", b=1).broadcast_to([P, 48, 2]),
                                       ALU.add))
                free(dve, key)
                for s in range(2):
                    gains = vcol[:, 0, 64 * l + 48 + 8 * s:64 * l + 56 + 8 * s]
                    link(dve.scalar_tensor_tensor(out=amix[:, 2 * l + s], in0=mod[:, l, 24 * s + 8:24 * s + 16, :], scalar=1.0,
                                                  in1=gains.rearrange("p (a b) -> p a b", b=1).broadcast_to([P, KD, 2]),
                                                  op0=ALU.add, op1=ALU.mult))
            for m in range(KD + 1):
                if m < KD:
                    key = ("xin", m)
                    dve.wait_ge(*auxiliary(key))
                    dve.tensor_copy(xT[:, m, :], ps(key)).then_inc(PH["res0", "x"], 1)
                    dve.wait_ge(*when(("res0", "x"), m + 1))
                    free(dve, key)
                if m >= 1:
                    sum_squares(0, m - 1, T)
            with nc.allow_non_contiguous_dma(reason="edges"):
                mark(dve.memset(upad[:], 0.0))
            dve.wait_ge(dve_step, chain[0])
            norm(0, X_CTX, lambda k, q: amix[:, 0, k, q:q + 1], lambda k, q: mod[:, 0, k, q:q + 1])

            def v0_tile(i, key):
                dst = v0[:, :, P * i:P * i + P]
                release(dve.tensor_copy(dst, ps(key).rearrange("p (a b) -> p a b", a=6)), key)
                dve.wait_ge(gfree[group_of(key) % 4], group_of(key) // 4 + 1)
                dve.sem_inc(PH["in0", "vdone"], 1)

            def pooling():
                for i in range(2):
                    key = ("in0", "U", i)
                    dve.wait_ge(gfree[group_of(key) % 4], group_of(key) // 4 + 1)
                dve.wait_ge(*when(("set", "icnt"), 16))
                L = UPW
                for i in range(2):
                    u, a, b = upad[:, i], ptmp[:, 0], ptmp[:, 1]
                    link(dve.tensor_tensor(a[:, 1:L], u[:, 1:L], u[:, 0:L - 1], ALU.add))
                    link(dve.tensor_tensor(b[:, 2:L - 1], a[:, 1:L - 2], a[:, 3:L], ALU.add))
                    if i == 0:
                        tiers = ((0, a), (1, b))
                    else:
                        link(dve.tensor_tensor(a[:, 4:L - 3], b[:, 2:L - 5], b[:, 6:L - 1], ALU.add))
                        link(dve.tensor_tensor(b[:, 8:L - 7], a[:, 4:L - 11], a[:, 12:L - 3], ALU.add))
                        tiers = ((0, a), (1, b))
                    for half, s in tiers:
                        rows = slice(HD * half, HD * half + HD)
                        for t0, w, p0 in ((0, TX, 8), (TX, TC, 24 + TX)):
                            d = dT[rows, i, t0:t0 + w]
                            link(dve.tensor_tensor(d, s[rows, p0:p0 + w], d, ALU.mult))
                            link(dve.tensor_tensor(d, d, u[rows, p0:p0 + w], ALU.subtract))
                dve.sem_inc(PH["in0", "pooled"], 1)

            inputs("in0", S0, (2, 3), 12, v0_tile, {4: pooling})
            for i in range(2):
                key = ("pool", i)
                dve.wait_ge(*when(("in0", "pooly"), i + 1))
                ins = dve.scalar_tensor_tensor(out=hlo[:, i, :], in0=ps(key), scalar=vc("pscale", i),
                                               in1=hhi[:, i, :].bitcast(F32), op0=ALU.mult, op1=ALU.subtract)
                ins.then_inc(PH["in0", "pooldone"], 1)
                dve.wait_ge(*when(("in0", "pooldone"), i + 1))
                free(dve, key)
            attention(0)
            output_tiles(0, 6, T, hhi, hlo, 2)
            residual_tiles(lambda m: ("wout", 0, m), 1, X_CTX, gate_of(0, 16))
            norm(1, X_CTX, lambda k, q: amix[:, 1, k, q:q + 1], lambda k, q: mod[:, 0, 24 + k, q:q + 1])
            ffn(0, FFN_CHUNKS, X_CTX, gate_of(0, 40), 2)
            norm(2, X_CTX, lambda k, q: amix[:, 2, k, q:q + 1], lambda k, q: mod[:, 1, k, q:q + 1])

            def nv_tile(i, key):
                release(dve.tensor_copy(nv[:, :, P * i:P * i + P], ps(key).rearrange("p (a b) -> p a b", a=6)), key)
                dve.wait_ge(gfree[group_of(key) % 4], group_of(key) // 4 + 1)
                dve.sem_inc(PH["in1", "vdone"], 1)

            def mv_tile(h, key):
                src = ps(key).rearrange("p (a b) -> p a b", a=6)
                if h == 0:
                    dve.wait_ge(*product_of(("mq", "U", MH - 1)))
                mark(dve.tensor_copy(mvx[:, :, HD * h:HD * h + HD], src[:, 0:4, HD:P]))
                dve.tensor_copy(mvc[:, :, HD * h:HD * h + HD], src[:, 4:6, HD:P]).then_inc(PH["mk", "vdone"], 1)
                dve.wait_ge(*when(("mk", "vdone"), h + 1))
                free(dve, key)

            inputs("in1", S1, (14, 15, 16, 17), 18, nv_tile)
            dve.wait_ge(*when(("set", "rope1"), 16))
            inputs("mq", SQ, (), MH, None)
            inputs("mk", SK, tuple(range(MH)), MH, mv_tile)
            attention(1)
            output_tiles(1, 4, TX, hhi, hlo, 0)
            attention(2)
            output_tiles(2, 4, TX, hhi, hlo, 4)
            residual_tiles(lambda m: ("wout", 1, m), 3, X_ONLY, gate_of(1, 16))
            norm(3, X_ONLY, lambda k, q: amix[:, 3, k, q:q + 1], lambda k, q: mod[:, 1, 24 + k, q:q + 1])
            ffn(1, FFN_CHUNKS, X_ONLY, gate_of(1, 40), 4)
            norm(4, X_ONLY, lambda k, q: vc("an2", k), lambda k, q: zero8[:, k:k + 1])

            def v2_tile(i, key):
                release(dve.tensor_copy(v2[:, :, P * i:P * i + P], ps(key, TX).rearrange("p (a b) -> p a b", a=4)), key)
                dve.wait_ge(gfree[group_of(key) % 4], group_of(key) // 4 + 1)
                dve.sem_inc(PH["in2", "vdone"], 1)

            def forget_sums():
                dve.wait_ge(*when(("in2", "fg"), 4))
                c, s = cum[0:N_FOX, :], lsig[0:N_FOX, :]
                link(dve.tensor_scalar(c, c, 0.0, -1.0, ALU.min, ALU.mult))
                link(dve.tensor_tensor(s, s, c, ALU.add))
                dve.tensor_tensor_scan(c, s, s, 0.0, ALU.add, ALU.bypass).then_inc(PH["in2", "cum"], 1)

            inputs("in2", S2, tuple(range(16, 24)), 28, v2_tile, {26: forget_sums})
            attention(3)
            dve.wait_ge(*when(("in2", "outstd"), 1))
            link(dve.reciprocal(ss12[:, 0], ss12[:, 1]))
            for q in range(4):
                for gi, (c0, w) in enumerate(((0, 256), (256, 384), (640, 384))):
                    dve.tensor_scalar(o2[:, q, c0:c0 + w], o2[:, q, c0:c0 + w], ss12[:, 0, gi, q:q + 1], None,
                                      ALU.mult).then_inc(PH["in2", "outn"], 1)
            output_tiles(3, 8, TX, ahi, alo, 0, lambda m: vc("og2", m), (2, 3, 4))
            residual_tiles(lambda m: ("wout", 2, m), 5, X_ONLY, None)
            norm(5, X_ONLY, lambda k, q: vc("mn2", k), lambda k, q: zero8[:, k:k + 1])
            ffn(2, FF2_CHUNKS, X_ONLY, None, None)
            for t in range(4):
                dve.wait_ge(*auxiliary(("xout", t)))
                dve.tensor_copy(ostage[:, t, :], G[group_of(("xout", t)) % 4][:]).then_inc(PH["fin", "copy"], 1)


def normed_before(sums, s):
    return sum(1 for it in sums.values() if it["stop"] and it["s"] < s)


_INS = [
    "x", "c", "ctx", "c_ctx", "l0_ada_w", "l0_ada_b", "l0_norm_mix", "l0_norm_ffn", "l0_w_in", "l0_pool_w",
    "l0_pool_scale", "l0_q_gain", "l0_k_gain", "l0_w_out", "l0_ffn_w_gate", "l0_ffn_w_up", "l0_ffn_w_down",
    "l1_ada_w", "l1_ada_b", "l1_norm_mix", "l1_norm_ffn", "l1_w_in", "l1_mla_q_a_gain", "l1_mla_kv_a_gain",
    "l1_mla_w_uq", "l1_mla_w_ukv", "l1_mla_q_gain", "l1_mla_k_gain", "l1_na_q_gain", "l1_na_k_gain",
    "l1_na_rpb", "l1_w_out", "l1_ffn_w_gate", "l1_ffn_w_up", "l1_ffn_w_down", "attn_norm_2", "w_in_2",
    "b_forget_2", "q_gain_2", "k_gain_2", "out_gain_2", "w_out_2", "mlp_norm_2", "w_up_2", "w_down_2",
]


def kernel(**inputs):
    import concourse.bacc as _bacc
    from concourse.bass_utils import run_bass_kernel_spmd as _run

    nc = _bacc.Bacc("TRN2", target_bir_lowering=False, num_devices=1)
    arrays, aps = {}, {}
    for name in _INS:
        a = np.ascontiguousarray(inputs[name])
        arrays[f"in_{name}_dram"] = a
        aps[name] = nc.dram_tensor(f"in_{name}_dram", a.shape, mybir.dt.from_np(a.dtype), kind="ExternalInput").ap()
    for name, a in shape_tables().items():
        arrays[f"const_{name}_dram"] = a
        aps[name] = nc.dram_tensor(f"const_{name}_dram", a.shape, mybir.dt.from_np(a.dtype), kind="ExternalInput").ap()
    out = nc.dram_tensor("out_0_dram", (1, TX, D), F32, kind="ExternalOutput").ap()
    build(nc, aps, out)
    r = _run(nc, [arrays], core_ids=[0])
    return r.results[0]["out_0_dram"]
```

```python
from contextlib import ExitStack

import numpy as np

import concourse.bass as bass
from concourse import mybir

ALU = mybir.AluOpType
ACT = mybir.ActivationFunctionType
F32 = mybir.dt.float32
F32R = mybir.dt.float32r
AX_X = mybir.AxisListType.X

P = 128
D = 1024
KD = D // P
TX, TC = 512, 256
T = TX + TC
FFN = 2816
FF2 = 4 * D
GRID = 64
EPS = 1e-6
NEG = -1.0e30
HD = 64
POOL_W = (2, 4, 8, 16)
GQ, GKV = 12, 4
MH, MQK, MROPE = 8, 96, 32
NAH, NAC = 8, 16
QL, KVL = 384, 256
HEADS, N_MOBA, N_FOX, N_DIL = 16, 4, 6, 6
DIL_PAIRS = ((128, 1), (512, 4), (2048, 16))
BW = 7 * P
RING = 4
X_ONLY = ((0, TX),)
X_CTX = ((0, TX), (TX, TC))


def shape_tables():
    p = np.arange(P)
    same64 = (p[:, None] // HD == p[None, :] // HD)
    mats = np.zeros((P, 8, P), np.float32)
    mats[:, 0] = np.eye(P)
    mats[:, 1] = 1.0 / D
    mats[:, 2] = same64 / HD
    mats[:, 3] = 1.0 / QL
    mats[:, 4] = 1.0 / KVL
    mats[:MQK, 5, :MQK] = 1.0 / MQK
    for m in range(P):
        low = m % 32 < 16
        mats[m + 16 if low else m - 16, 6, m] = -1.0 if low else 1.0
    for m in range(HD, MQK):
        low = m % 16 < 8
        mats[m + 8 if low else m - 8, 7, m] = -1.0 if low else 1.0
    tok = np.arange(TX)
    row, col = (tok // GRID).astype(np.float32), (tok % GRID).astype(np.float32)

    def angles(rows, first, d):
        out = np.zeros((rows, TX), np.float32)
        inv = (10000.0 ** (-np.arange(d // 2, dtype=np.float32) * 2.0 / d)).astype(np.float32)
        for q in range(first, rows):
            pos = row if (q - first) % (2 * d) < d else col
            out[q] = pos * inv[(q - first) % (d // 2)]
        return out

    a0, a1 = angles(P, 0, 32), angles(P, HD, 16)
    a1[MQK:] = 0.0
    rope = np.stack([np.cos(a0), np.sin(a0), np.cos(a1), np.sin(a1)], 1).astype(np.float32)
    icnt = np.zeros((P, 2, T), np.float32)
    for g, w in enumerate(POOL_W):
        for lo_t, n in ((0, TX), (TX, TC)):
            t = np.arange(n)
            cnt = np.clip(t - w // 2 + w, 0, n) - np.clip(t - w // 2, 0, n)
            icnt[64 * (g % 2):64 * (g % 2) + 64, g // 2, lo_t:lo_t + n] = 1.0 / cnt
    c = p % GRID
    start = np.clip(c - NAC // 2, 0, GRID - NAC)[:, None]
    kc = np.arange(GRID)[None, :]
    namask = np.where((kc >= start) & (kc < start + NAC), 0.0, NEG).astype(np.float32)[:, ::-1].copy()
    dist = p[:, None] - np.arange(BW)[None, :] + 3 * P
    causal = dist >= 0
    times = sum(((dist % d == 0) & (dist <= w)).astype(np.int64) for w, d in DIL_PAIRS) * causal
    dil = np.where(times > 0, np.log(np.maximum(times, 1)), NEG)
    band = np.stack([np.where(causal, dist, -NEG), np.where(causal, dist, 0), dil,
                     np.where(causal, 0.0, NEG)], 1).astype(np.float32)
    sel = np.zeros((N_FOX, N_FOX, P), np.float32)
    for h in range(N_FOX):
        sel[h, h] = 1.0
    return {"mats": mats, "rope": rope, "icnt": icnt, "namask": namask, "band": band, "sel": sel}


SLOPES = [float(np.float32(2.0 ** (-8.0 * i / (N_MOBA + N_DIL)))) for i in range(1, N_MOBA + N_DIL + 1)]


def split_width(total, width):
    return [(i, min(width, total - i)) for i in range(0, total, width)]


FFN_CHUNKS = split_width(FFN // P, 8)
FF2_CHUNKS = split_width(FF2 // P, 8)


def build(nc, A, out):
    with ExitStack() as ctx:
        def sb(name, shape, dt=F32):
            return ctx.enter_context(nc.sbuf_tensor(name, shape, dt))

        def sem(name):
            return ctx.enter_context(nc.semaphore(name))

        at_a = -(-nc.sbuf_base // 32) * 32
        big_a = sb("big_a", [P, 2 * KD * T], F32R)
        big_b = sb("big_b", [P, 2 * KD * T], F32R)
        plain_a = nc.alloc_sbuf_tensor_at("plain_a", [P, 2 * KD * T], F32, offset=at_a)
        plain_b = nc.alloc_sbuf_tensor_at("plain_b", [P, 2 * KD * T], F32, offset=at_a + 8 * KD * T)
        xT = sb("xT", [P, KD, T])
        raw = sb("raw", [P, RING, KD, P])
        whi = sb("whi", [P, 2, KD, P], F32R)
        wlo = sb("wlo", [P, 2, KD, P], F32R)
        sq = sb("sq", [P, 2, T])
        qr = sb("qr", [P, 2, T])
        tmp = sb("tmp", [P, 2, T])
        rsb = sb("rsb", [P, 2, T])
        ssq = sb("ssq", [P, T])
        rt = sb("rt", [P, 2, TX])
        vreg = sb("vreg", [P, 2 * T])
        rope = sb("rope", [P, 2, TX])
        mats = sb("mats", [P, 8, P])
        namask = sb("namask", [P, GRID])
        vrow = sb("vrow", [P, 2, P])
        vcol = sb("vcol", [P, 2, P])
        mod = sb("mod", [P, 2, 48, 2])
        amix = sb("amix", [P, 4, KD, 2])
        cs = sb("cs", [P, KD, 2])
        arow = sb("arow", [2, 2, 512])
        poolw = sb("poolw", [P, 2, P])
        eps = sb("eps", [P, 1])
        zero8 = sb("zero8", [P, KD])
        bfox = sb("bfox", [N_FOX, 1])

        stat = sb("stat", [P, 4, 80])
        ss12 = sb("ss12", [P, 2, 3, 4])
        G = [ctx.enter_context(nc.psum_tensor(f"G{i}", [P, 1024], F32)) for i in range(4)]
        pad_dram = nc.dram_tensor("rpb_padded", (NAH * 15, 127), F32, kind="Internal").ap()

        hhi = big_a[:, 0:KD * T].rearrange("p (k t) -> p k t", k=KD)
        hlo = big_a[:, KD * T:].rearrange("p (k t) -> p k t", k=KD)
        ahi = big_b[:, 0:KD * T].rearrange("p (k t) -> p k t", k=KD)
        alo = big_b[:, KD * T:].rearrange("p (k t) -> p k t", k=KD)
        af, bf = plain_a[:], plain_b[:]

        def part(base, at, *dims):
            n = int(np.prod(dims))
            v = base[:, at:at + n]
            if len(dims) == 1:
                return v
            return v.rearrange("p (a b) -> p a b", a=dims[0])

        ident, ones_d, blk64, ones_q, ones_kv, ones96, rot64, rot32 = (mats[:, i, :] for i in range(8))
        q0T, k0T = part(bf, 0, 6, T), part(bf, 6 * T, 2, T)
        PB = 8 * T
        UPW = 8 + TX + 8 + 8 + TC + 8
        upad, ptmp = part(bf, PB, 2, UPW), part(bf, PB + 2 * UPW, 2, UPW)
        dT = part(bf, PB + 4 * UPW, 2, T)
        o0 = part(bf, PB, 6, GQ * HD)
        v0 = part(vreg, 0, 6, GKV * HD)
        nqT, nkT = part(bf, 0, 4, TX), part(bf, 4 * TX, 4, T)
        nv = part(bf, 5120, 6, NAH * HD)
        ckvn, cqn = part(bf, 8192, 2, T), part(bf, 9728, 3, TX)
        mqT, mkT = part(af, 0, MH, TX), part(af, MH * TX, MH, T)
        omla = part(af, 10240, 4, 512)
        mvx, mvc = part(bf, 9728, 4, 512), part(vreg, 0, 2, 512)
        nabias = [part(bf, 8192, 14, GRID), part(rsb[:].rearrange("p a b -> p (a b)"), 0, 14, GRID)]
        ona = part(bf, 9088, 4, 512)
        craw = part(vreg, 0, 3, TX)
        krbuf = ssq
        kvraw = part(bf, 5120, 2, T)
        q2T, k2T, v2 = part(bf, 0, 8, TX), part(bf, 4096, 8, TX), part(bf, 8192, 4, D)
        o2 = part(af, 0, 4, D)
        band = part(af, 4096, 4, BW)
        th = part(af, 4096 + 4 * BW, 2, BW)
        sel = part(af, 4096 + 6 * BW, N_FOX, P)
        gsig = part(vreg, 0, 3, TX)
        cum = rope[:, 0, :]
        lsig = rope[:, 1, :]
        xtok = part(af, 0, 6, D)
        ostage = part(af, 0, 4, D)
        zpad, zrow = part(bf, 0, 127), part(bf, 128, 31)
        qz = tmp
        Pm, PT = qr, sq

        landed = [sem(f"landed{i}") for i in range(RING)]
        raw_free = [sem(f"raw_free{i}") for i in range(RING)]
        hi_done = sem("hi_done")
        unit_done = sem("unit_done")
        aux_done = sem("aux_done")
        gfree = [sem(f"gfree{i}") for i in range(4)]

        plan = {}
        cnt = {"r": 0, "u": 0, "g": 0, "a": 0}
        ring_dmas = []
        ring_total = []
        unit_ring = []

        def use_ring(n_dmas=1):
            r = cnt["r"]
            cnt["r"] += 1
            before = ring_total[r - RING] if r >= RING else 0
            ring_total.append(before + 16 * n_dmas)
            return r

        def plan_unit(key, split=True, n_dmas=1, r=None):
            if r is None:
                r = use_ring(n_dmas)
            u = None
            if split:
                u = cnt["u"]
                cnt["u"] += 1
                unit_ring.append(r)
            plan[key] = (u, r, cnt["g"])
            cnt["g"] += 1

        def plan_aux(key, group=None):
            if group is None:
                group = cnt["g"]
                cnt["g"] += 1
            plan[key] = (cnt["a"], group)
            cnt["a"] += 1
            return group

        def plan_ada(l, i):
            for q in range(4):
                plan_unit(("ada", l, i, q), split=False)
                if q:
                    cnt["g"] -= 1
                    plan["ada", l, i, q] = plan["ada", l, i, q][:2] + (cnt["g"] - 1,)

        plan_aux("cond")
        for i in range(4):
            plan_ada(0, i)
            if i == 0:
                plan_aux("vec")
            else:
                plan_aux(("adaT", 0, i - 1))
        plan_aux(("adaT", 0, 3))
        for m in range(KD):
            plan_aux(("xin", m))

        def plan_norm(n):
            plan_aux(("norm", n))
            plan_aux(("spread", n))

        def plan_inputs(st, units, vts, sums, split=True, two=(), ada=()):
            seq = []
            open_group = None
            early = None
            for n in range(len(units) + 2):
                if n < len(units):
                    plan_unit((st, "U", n), split, 2 if n in two else 1, early)
                    early = None
                    seq.append(("U", n))
                if 0 < n <= len(ada):
                    plan_aux(("adaT",) + ada[n - 1])
                    seq.append(("AT", ada[n - 1]))
                if n < len(ada):
                    early = use_ring(2 if n + 1 in two else 1)
                    plan_ada(*ada[n])
                    seq.append(("A", ada[n]))
                if n - 1 in vts:
                    plan_aux((st, "V", n - 1))
                    seq.append(("V", n - 1))
                if n - 1 in sums:
                    open_group = plan_aux((st, "S", n - 1), None if sums[n - 1]["start"] else open_group)
                    seq.append(("S", n - 1))
                if n - 2 in sums and sums[n - 2]["rope"]:
                    plan_aux((st, "R", n - 2))
                    seq.append(("R", n - 2))
            plan[st, "seq"] = seq

        def item(s, dst, gain, n, mat, rows=P, rope=False, raw_at=None, start=True, stop=True, members=None,
                 kr=False):
            return dict(s=s, dst=dst, gain=gain, n=n, mat=mat, rows=rows, rope=rope, raw=raw_at,
                        start=start, stop=stop, members=members, kr=kr)

        VC = {}
        at = 0
        for name, n in (("c", 8), ("c_ctx", 8), ("an2", 8), ("mn2", 8), ("pscale", 2), ("qa", 3), ("kva", 2),
                        ("og2", 8), ("q2", 8), ("k2", 8), ("q0", 1), ("k0", 1), ("nq", 1), ("nk", 1),
                        ("mq", 1), ("mk", 1)):
            VC[name] = at
            at += n
        VROWS2 = at

        def vc(name, i=0):
            return vcol[:, 1, VC[name] + i:VC[name] + i + 1]

        plan_norm(0)
        S0, L0_Q, L0_POOL, L0_V = {}, range(4, 10), (2, 3), (10, 11)
        L0_COLS = {0: [(1024, 128)], 1: [(1152, 128)], 2: [(0, 128)], 3: [(128, 128)],
                   10: [(1280, 128)], 11: [(1408, 128)]}
        for i in range(2):
            S0[i] = item(i, k0T[:, i], vc("k0"), T, blk64, rope=True)
        for t, n in enumerate(L0_Q):
            a = 6 * (t // 3) + t % 3
            L0_COLS[n] = [(256 + HD * a, HD), (256 + HD * (a + 3), HD)]
            S0[n] = item(2 + t, q0T[:, t], vc("q0"), T, blk64, rope=True)
        ADA_IN0 = [(0, 4 + i) for i in range(8)]
        ADA_WOUT0 = [(1, i) for i in range(7)]
        ADA_DOWN0 = [None] + [(1, 7 + i) for i in range(5)]
        plan_inputs("in0", L0_COLS, L0_V, S0, two=L0_Q, ada=ADA_IN0)
        plan_aux(("pool", 0))
        plan_aux(("pool", 1))

        def plan_ot(st, n):
            for m in range(n):
                plan_aux((st, "OT", m))

        plan_ot("ot0", 6)

        def plan_square(key, ada=()):
            early = None
            for m in range(KD):
                plan_unit(key + (m,), r=early)
                early = None
                if 0 < m <= len(ada) and ada[m - 1]:
                    plan_aux(("adaT",) + ada[m - 1])
                if m < len(ada) and ada[m]:
                    early = use_ring()
                    plan_ada(*ada[m])

        def plan_wout(l):
            plan_square(("wout", l), ADA_WOUT0 if l == 0 else ())

        def plan_ffn(l, chunks, gated):
            for c, (f0, nf) in enumerate(chunks):
                for i in range(nf * (2 if gated else 1)):
                    plan_unit(("up", l, c, i))
                plan_square(("down", l, c), ADA_DOWN0 if l == 0 and c == len(chunks) - 1 else ())

        plan_wout(0)
        plan_norm(1)
        plan_ffn(0, FFN_CHUNKS, True)
        plan_norm(2)
        L1_COLS = [[(c0, 128)] for c0 in (0, 128, 256, 384, 512, 576)] + [[(672 + 128 * i, 128)] for i in range(12)]
        S1 = {}
        for i in range(3):
            S1[i] = item(i, None, None, TX, ones_q, raw_at=craw[:, i], start=i == 0, stop=i == 2,
                         members=[(craw[:, j], cqn[:, j], vc("qa", j)) for j in range(3)])
        for i in range(2):
            S1[3 + i] = item(3 + i, None, None, T, ones_kv, raw_at=kvraw[:, i], start=i == 0, stop=i == 1,
                             members=[(kvraw[:, j], ckvn[:, j], vc("kva", j)) for j in range(2)])
        for i in range(4):
            S1[6 + i] = item(5 + i, nqT[:, i], vc("nq"), TX, blk64)
            S1[10 + i] = item(9 + i, nkT[:, i], vc("nk"), T, blk64)
        plan_inputs("in1", L1_COLS, (14, 15, 16, 17), S1)
        SQ = {h: item(h, mqT[0:MQK, h], vc("mq"), TX, ones96, rows=MQK, rope=True) for h in range(MH)}
        plan_inputs("mq", range(MH), (), SQ, split=False)
        SK = {h: item(h, mkT[0:MQK, h], vc("mk"), T, ones96, rows=MQK, rope=True, kr=True) for h in range(MH)}
        plan_inputs("mk", range(MH), range(MH), SK, split=False)
        plan_ot("ot1", 4)
        plan_ot("ot2", 4)
        plan_wout(1)
        plan_norm(3)
        plan_ffn(1, FFN_CHUNKS, True)
        plan_norm(4)
        B2_COLS = [[(128 * i, 128)] for i in range(25)] + [[(3078 + 128 * i, 128)] for i in range(3)]
        S2 = {}
        for i in range(8):
            S2[i] = item(i, q2T[:, i], vc("q2", i), TX, blk64)
            S2[8 + i] = item(8 + i, k2T[:, i], vc("k2", i), TX, blk64)
        plan_inputs("in2", B2_COLS, range(16, 24), S2)
        plan_ot("ot3", 8)
        plan_wout(2)
        plan_norm(5)
        plan_ffn(2, FF2_CHUNKS, False)
        for m in range(4):
            plan_aux(("xout", m))

        HEADS0 = [6 * (i // 6) + i % 6 // 2 + 3 * (i % 2) for i in range(GQ)]
        QUERIES = {
            0: [(q0T, 3 * (h // 6) + h % 3, HD * (h % 6 // 3), T) for h in HEADS0],
            2: [(nqT, h // 2, HD * (h % 2), TX) for h in range(NAH)],
            3: [(q2T, h // 2, HD * (h % 2), TX) for h in range(HEADS)],
        }

        def attention_units():
            st0, st1, st2, st3 = [], [], [], []
            for h in HEADS0:
                pr, off = h // 6, HD * ((h % 6) // 3)
                kt = k0T[:, pr]
                for qt in range(6):
                    ctx_only = qt >= 4
                    vs = [v0[:, j, HD * (h // 3):HD * (h // 3) + HD] for j in (range(4, 6) if ctx_only else range(6))]
                    st0.append(dict(q=qz[:, off // HD, P * qt:P * qt + P],
                                    ks=[(kt[:, TX:T], 0, TC)] if ctx_only else [(kt[:, 0:TX], 0, TX), (kt[:, TX:T], TX, TC)],
                                    vs=vs, o=o0[:, qt, HD * h:HD * h + HD], kind="plain"))
            for h in range(MH):
                for qt in range(4):
                    vs = [mvx[:, j, HD * h:HD * h + HD] for j in range(4)] + [mvc[:, j, HD * h:HD * h + HD] for j in range(2)]
                    st1.append(dict(q=mqT[:, h, P * qt:P * qt + P],
                                    ks=[(mkT[:, h, 0:TX], 0, TX), (mkT[:, h, TX:T], TX, TC)],
                                    vs=vs, o=omla[:, qt, HD * h:HD * h + HD], kind="plain"))
            for h in range(NAH):
                off = HD * (h % 2)
                for qt in range(4):
                    kt = nkT[:, h // 2]
                    st2.append(dict(q=qz[:, off // HD, P * qt:P * qt + P],
                                    ks=[(kt[:, 0:TX], 0, TX), (kt[:, TX:T], TX, TC)],
                                    vs=[nv[:, j, HD * h:HD * h + HD] for j in range(6)],
                                    o=ona[:, qt, HD * h:HD * h + HD], kind="na", head=h, qt=qt,
                                    bias=nabias[h % 2][:, 6 - 2 * qt:14 - 2 * qt, ::-1]))
            for h in range(HEADS):
                off = HD * (h % 2)
                fox = N_MOBA <= h < N_MOBA + N_FOX
                for qt in range(4):
                    n = P * (qt + 1)
                    table = band[:, 3] if fox else th[:, h % 2]
                    st3.append(dict(q=qz[:, off // HD, P * qt:P * qt + P],
                                    ks=[(k2T[:, h // 2, 0:n], 0, n)],
                                    vs=[v2[:, j, HD * h:HD * h + HD] for j in range(qt + 1)],
                                    o=o2[:, qt, HD * h:HD * h + HD], kind="band", head=h, qt=qt,
                                    bias=table[:, 3 * P - P * qt:3 * P - P * qt + n], fox=h - N_MOBA if fox else None))
            return st0, st1, st2, st3

        ATT = attention_units()
        PH = {}

        def stage_sems(st, *names):
            for n in names:
                PH[st, n] = sem(f"{st}_{n}")

        stage_sems("set", "cond", "below", "tables", "zero", "rows", "cols", "xload", "padrow", "pad", "poolw", "poolz",
                   "silu", "b", "rope1", "icnt", "band", "steps")
        stage_sems("in0", "pooled", "pooly", "pooldone")
        stage_sems("in1", "kr")
        stage_sems("in2", "fg", "cum", "outsq", "outstd", "outn")
        stage_sems("att2", "bias0", "bias1", "masked")
        stage_sems("fin", "x", "copy", "out")
        BASE = {}

        def shared_sems(names, stages):
            for i, name in enumerate(names):
                s = sem(name)
                total = 0
                for st, counts in stages:
                    PH[st, name.split("_")[-1]] = s
                    BASE[st, name.split("_")[-1]] = total
                    total += counts[i]

        def input_counts(sums, vts):
            n = len(sums)
            stops = sum(1 for it in sums.values() if it["stop"])
            ropes = sum(1 for it in sums.values() if it["rope"])
            return (len(vts), len(vts), n, stops, stops, ropes)

        shared_sems(("in_vcopy", "in_vdone", "in_square", "in_std", "in_normed", "in_rotated"),
                    [("in0", input_counts(S0, L0_V)), ("in1", input_counts(S1, range(4))),
                     ("mq", input_counts(SQ, ())), ("mk", input_counts(SK, range(MH))),
                     ("in2", input_counts(S2, range(8)))])
        shared_sems(("att_scores", "att_max", "att_prob", "att_turned", "att_pt", "att_pv", "att_o"),
                    [(f"att{i}", (len(ATT[i]),) * 7) for i in range(4)])
        shared_sems(("queries_zeros", "queries_head"),
                    [(f"att{i}", (2, len(QUERIES[i]))) for i in (0, 2, 3)])
        shared_sems(("ot_a", "ot_b", "ot_hi", "ot_done"),
                    [(f"ot{i}", (0, 0, n, n)) for i, n in enumerate((6, 4, 4, 8))])
        shared_sems(("res_x", "res_sq", "res_ssq"), [(f"res{i}", (KD,) * 3) for i in range(6)])
        shared_sems(("norm_std", "norm_diag", "norm_tmp", "norm_hi", "norm_h"), [(f"norm{i}", (1, 1, KD, KD, KD)) for i in range(6)])
        shared_sems(("ffn_act", "ffn_prod", "ffn_hi", "ffn_lo"),
                    [(f"ffn{i}", (n // P,) * 4) for i, n in enumerate((FFN, FFN, FF2))])

        def when(what, count):
            return PH[what], count + BASE.get(what, 0)

        def product_of(key, j=0):
            u, r, _ = plan[key]
            if u is None:
                return raw_free[r % RING], r // RING + 1
            return unit_done, u + 1 + 4 * j

        def auxiliary(key):
            return aux_done, plan[key][0] + 1

        def group_of(key):
            return plan[key][-1]

        def release(ins, key):
            return ins.then_inc(gfree[group_of(key) % 4], 1)

        def free(eng, key):
            eng.sem_inc(gfree[group_of(key) % 4], 1)

        def ps(key, n=T, rows=P):
            return G[group_of(key) % 4][0:rows, 0:n]

        block = ctx.enter_context(nc.Block())

        @block.sync
        def _(sp):
            def load_ada(l, i, q):
                w = A[f"l{l}_ada_w"].rearrange("(k p) n -> p k n", p=P)
                r = plan["ada", l, i, q][1]
                if r >= RING:
                    sp.wait_ge(raw_free[r % RING], r // RING)
                sp.dma_start(raw[:, r % RING].rearrange("p (a b) c -> p a (b c)", a=2),
                             w[:, 2 * q:2 * q + 2, 512 * i:512 * i + 512]).then_inc(landed[r % RING], 16)

            with nc.allow_non_contiguous_dma(reason="small vectors"):
                def rows_of(name, width=P):
                    return A[name].rearrange("(a p) -> a p", p=width)

                two = lambda name, w: A[name].rearrange("a (b p) -> (a b) p", p=w)
                sp.dma_start(mats[:], A["mats"]).then_inc(PH["set", "cond"], 16)
                sp.wait_ge(*when(("set", "zero"), 1))
                for key, src in (("c", two("c", P)), ("c_ctx", rows_of("c_ctx"))):
                    sp.dma_start(vrow[VC[key]:VC[key] + KD, 1, :], src).then_inc(PH["set", "cond"], 16)
                for q in range(RING):
                    load_ada(0, 0, q)
                sp.dma_start(rope[:], A["rope"][:, 0:2]).then_inc(PH["set", "tables"], 16)
                sp.dma_start(namask[:], A["namask"]).then_inc(PH["set", "tables"], 16)

                at = 0
                for name in ("l0_ada_b", "l0_norm_mix", "l0_norm_ffn", "l1_ada_b", "l1_norm_mix", "l1_norm_ffn"):
                    n = A[name].shape[0] // P
                    sp.dma_start(vrow[at:at + n, 0, :], rows_of(name)).then_inc(PH["set", "rows"], 16)
                    at += n
                for key, src in (("an2", two("attn_norm_2", P)),
                                 ("mn2", two("mlp_norm_2", P)), ("pscale", rows_of("l0_pool_scale")),
                                 ("qa", rows_of("l1_mla_q_a_gain")), ("kva", rows_of("l1_mla_kv_a_gain")),
                                 ("og2", two("out_gain_2", P)),
                                 ("q2", A["q_gain_2"].rearrange("a (b c) d -> (a b) (c d)", c=2)),
                                 ("k2", A["k_gain_2"].rearrange("a (b c) d -> (a b) (c d)", c=2))):
                    n = src.shape[0]
                    sp.dma_start(vrow[VC[key]:VC[key] + n, 1, :], src).then_inc(PH["set", "rows"], 16)
                for key, name in (("q0", "l0_q_gain"), ("k0", "l0_k_gain"), ("nq", "l1_na_q_gain"), ("nk", "l1_na_k_gain")):
                    for i in range(2):
                        sp.dma_start(vrow[VC[key]:VC[key] + 1, 1, HD * i:HD * i + HD],
                                     A[name].rearrange("(a p) -> a p", a=1)).then_inc(PH["set", "rows"], 16)
                for key, name in (("mq", "l1_mla_q_gain"), ("mk", "l1_mla_k_gain")):
                    sp.dma_start(vrow[VC[key]:VC[key] + 1, 1, 0:MQK],
                                 A[name].rearrange("(a p) -> a p", a=1)).then_inc(PH["set", "rows"], 16)
                sp.dma_start(dT, A["icnt"]).then_inc(PH["set", "icnt"], 16)
                sp.dma_start(bfox[:], A["b_forget_2"].rearrange("a b -> b a")).then_inc(PH["set", "b"], 16)
                sp.wait_ge(*when(("set", "poolz"), 1))
                for g in range(4):
                    o = HD * (g % 2)
                    sp.dma_start(poolw[o:o + HD, g // 2, o:o + HD], A["l0_pool_w"][g]).then_inc(PH["set", "poolw"], 16)

            def columns(name):
                return A[name].rearrange("(k p) n -> p k n", p=P)

            def load(r, blocks, j=0, rows=KD):
                if r >= RING:
                    sp.wait_ge(raw_free[r % RING], r // RING + j)
                at = 0
                for src, width in blocks:
                    ins = sp.dma_start(raw[:, r % RING, 0:rows, at:at + width], src)
                    ins.then_inc(landed[r % RING], 16)
                    at += width

            def ada(l, i):
                for q in range(4):
                    load_ada(l, i, q)

            for i in range(1, 4):
                ada(0, i)
            sp.dma_start(xtok[:, 0:4, :], A["x"].rearrange("a (t p) d -> p (a t) d", p=P)).then_inc(PH["set", "xload"], 16)
            sp.dma_start(xtok[:, 4:6, :], A["ctx"].rearrange("a (t p) d -> p (a t) d", p=P)).then_inc(PH["set", "xload"], 16)

            def inputs(st, name, cols, ada_groups=()):
                w = columns(name) if len(A[name].shape) == 2 else A[name].rearrange("a (k p) n -> p (a k) n", p=P)
                for n in range(len(cols)):
                    if n == 0 or n > len(ada_groups):
                        load(plan[st, "U", n][1], [(w[:, :, c:c + m], m) for c, m in cols[n]])
                    if n < len(ada_groups):
                        load(plan[st, "U", n + 1][1], [(w[:, :, c:c + m], m) for c, m in cols[n + 1]])
                        ada(*ada_groups[n])

            def square_with_ada(key, w, rows, ada_groups):
                def tile(m):
                    load(plan[key + (m,)][1], [(w[:, :, P * m:P * m + P], P)], rows=rows)

                for m in range(KD):
                    if not (0 < m <= len(ada_groups) and ada_groups[m - 1]):
                        tile(m)
                    if m < len(ada_groups) and ada_groups[m]:
                        tile(m + 1)
                        ada(*ada_groups[m])

            def square_matrix(name, l):
                w = columns(name) if len(A[name].shape) == 2 else A[name].rearrange("a (k p) n -> p (a k) n", p=P)
                r0 = plan["wout", l, 0][1]
                with sp.Fori(0, 2) as j:
                    for b in range(4):
                        load(r0 + b, [(w[:, :, bass.ds((j * 4 + b) * P, P)], P)], j)

            def ffn(l, ups, down, chunks):
                for c, (f0, nf) in enumerate(chunks):
                    r0 = plan["up", l, c, 0][1]
                    per = 4 // len(ups)
                    with sp.Fori(0, nf // per) as j:
                        for b in range(4):
                            w = ups[b % len(ups)]
                            load(r0 + b, [(w[:, :, bass.ds((j * per + (f0 + b // len(ups))) * P, P)], P)], j)
                    if l == 0 and c == len(chunks) - 1:
                        square_with_ada(("down", l, c), down[:, f0:f0 + nf], nf, ADA_DOWN0)
                        continue
                    r0 = plan["down", l, c, 0][1]
                    with sp.Fori(0, 2) as j:
                        for b in range(4):
                            load(r0 + b, [(down[:, f0:f0 + nf, bass.ds((j * 4 + b) * P, P)], P)], j, rows=nf)

            inputs("in0", "l0_w_in", L0_COLS, ADA_IN0)
            square_with_ada(("wout", 0), columns("l0_w_out"), KD, ADA_WOUT0)
            ffn(0, [columns("l0_ffn_w_gate"), columns("l0_ffn_w_up")], columns("l0_ffn_w_down"), FFN_CHUNKS)
            inputs("in1", "l1_w_in", L1_COLS)
            wq, wkv = columns("l1_mla_w_uq"), columns("l1_mla_w_ukv")
            for h in range(MH):
                load(plan["mq", "U", h][1], [(wq[:, :, MQK * h:MQK * h + MQK], MQK)], rows=3)
            for h in range(MH):
                load(plan["mk", "U", h][1], [(wkv[:, :, P * h:P * h + P], P)], rows=2)
            square_matrix("l1_w_out", 1)
            ffn(1, [columns("l1_ffn_w_gate"), columns("l1_ffn_w_up")], columns("l1_ffn_w_down"), FFN_CHUNKS)
            inputs("in2", "w_in_2", B2_COLS)
            square_matrix("w_out_2", 2)
            up2 = A["w_up_2"].rearrange("a (k p) n -> p (a k) n", p=P)
            down2 = A["w_down_2"].rearrange("a (k p) n -> p (a k) n", p=P)
            ffn(2, [up2], down2, FF2_CHUNKS)
            for t in range(4):
                sp.wait_ge(*when(("fin", "copy"), t + 1))
                sp.dma_start(out[0, P * t:P * t + P, :], ostage[:, t, :]).then_inc(PH["fin", "out"], 16)
            sp.wait_ge(*when(("fin", "out"), 64))

        @block.gpsimd
        def _(pool):
            pool.memset(vrow[:, 1, :], 0.0).then_inc(PH["set", "zero"], 1)
            pool.memset(poolw[:], 0.0).then_inc(PH["set", "poolz"], 1)
            pool.memset(zpad[0:NAH * 15, :], 0.0).then_inc(PH["set", "pad"], 1)
            pool.wait_ge(*when(("set", "pad"), 1))
            with nc.allow_non_contiguous_dma(reason="small table"):
                pool.dma_start(zrow[0:NAH * 15, :], A["l1_na_rpb"].rearrange("h r c -> (h r) c")).then_inc(PH["set", "padrow"], 16)
            pool.wait_ge(*when(("set", "padrow"), 16))
            pool.tensor_copy(zpad[0:NAH * 15, 48:79], zrow[0:NAH * 15, ::-1]).then_inc(PH["set", "pad"], 1)
            pool.wait_ge(*when(("set", "pad"), 2))
            pool.dma_start(pad_dram, zpad[0:NAH * 15, :]).then_inc(PH["set", "padrow"], 16)
            pool.wait_ge(*when(("set", "padrow"), 32))

            def lower(u, j=0):
                r = unit_ring[u]
                pool.wait_ge(hi_done, u + 1 + 4 * j)
                pool.tensor_tensor(wlo[:, u % 2], raw[:, r % RING], whi[:, u % 2].bitcast(F32),
                                   ALU.subtract).then_inc(raw_free[r % RING], 1)

            def lowers(u0, u1):
                turns = (u1 - u0) // 4
                if turns > 1:
                    with pool.Fori(0, turns) as j:
                        for b in range(4):
                            lower(u0 + b, j)
                    u0 += 4 * turns
                for u in range(u0, u1):
                    lower(u)

            def padded_queries(i, before, last_unit):
                st = f"att{i}"
                pool.wait_ge(*before)
                r = unit_ring[last_unit]
                pool.wait_ge(raw_free[r % RING], r // RING + 1)
                for slot in range(2):
                    other = HD * (1 - slot)
                    if slot:
                        pool.wait_ge(*when((st, "zeros"), 1))
                    pool.memset(qz[other:other + HD, slot, :], 0.0).then_inc(PH[st, "zeros"], 1)
                per = len(ATT[i]) // len(QUERIES[i])
                for n, (q, t, off, w) in enumerate(QUERIES[i]):
                    if n == 0:
                        pool.wait_ge(*when((st, "zeros"), 2))
                    if n >= 2:
                        pool.wait_ge(*when((st, "scores"), per * (n - 1)))
                    if n and i == 2:
                        pool.wait_ge(*when((st, "masked"), n))
                    pool.tensor_copy(qz[off:off + HD, off // HD, 0:w], q[off:off + HD, t, 0:w]).then_inc(PH[st, "head"], 1)
                    pool.wait_ge(*when((st, "head"), n + 1))
                    if i == 2:
                        pool.wait_ge(*when((st, f"bias{n % 2}"), 32 * (n // 2 + 1)))
                        pool.tensor_tensor(nabias[n % 2], nabias[n % 2],
                                           namask[:].rearrange("p (a c) -> p a c", a=1).broadcast_to([P, 14, GRID]),
                                           ALU.add).then_inc(PH[st, "masked"], 1)
                if i == 2:
                    pool.wait_ge(*when((st, "masked"), NAH))

            first = {k: plan[k][0] for k in (("up", 0, 0, 0), ("down", 0, 2, 0), ("wout", 0, 0), ("wout", 1, 0),
                                             ("in2", "U", 0), ("wout", 2, 0))}
            for u in range(0, first["wout", 0, 0] + 2):
                lower(u)
            pool.wait_ge(*when(("in0", "rotated"), len(S0)))
            padded_queries(0, when(("in0", "vdone"), 2), first["wout", 0, 0] + 1)
            for u in range(first["wout", 0, 0] + 2, first["up", 0, 0, 0]):
                lower(u)
            lowers(first["up", 0, 0, 0], first["down", 0, 2, 0])
            for u in range(first["down", 0, 2, 0], first["wout", 1, 0] + 2):
                lower(u)
            u = first["wout", 1, 0] + 1
            pool.wait_ge(raw_free[unit_ring[u] % RING], unit_ring[u] // RING + 1)
            pool.wait_ge(unit_done, first["wout", 1, 0])
            pool.memset(plain_a[MQK:P, 0:MH * (TX + T)], 0.0).then_inc(PH["set", "below"], 1)
            pool.wait_ge(*when(("set", "below"), 1))
            padded_queries(2, when(("mk", "vdone"), MH), first["wout", 1, 0] + 1)
            lower(first["wout", 1, 0] + 2)
            lower(first["wout", 1, 0] + 3)
            lowers(first["wout", 1, 0] + 4, first["in2", "U", 0])
            for u in range(first["in2", "U", 0], first["wout", 2, 0] + 2):
                lower(u)
            padded_queries(3, when(("in2", "vdone"), 8), first["wout", 2, 0] + 1)
            lower(first["wout", 2, 0] + 2)
            lower(first["wout", 2, 0] + 3)
            lowers(first["wout", 2, 0] + 4, cnt["u"])

        @block.scalar
        def _(act):
            n_split = cnt["u"]

            def upper(u, j=0):
                r = unit_ring[u]
                act.wait_ge(landed[r % RING], ring_total[r] + 16 * j)
                if u >= 2:
                    act.wait_ge(unit_done, u - 1 + 4 * j)
                act.activation(whi[:, u % 2], raw[:, r % RING], ACT.Copy).then_inc(hi_done, 1)

            chain = [0]

            def link(ins):
                chain[0] += 1
                ins.then_inc(act_step, 1)
                act.wait_ge(act_step, chain[0])

            def residual_squares(i, ctx_too):
                n = T if ctx_too else TX
                for m in range(KD):
                    act.wait_ge(*when((f"res{i}", "x"), m + 1))
                    if m >= 2:
                        act.wait_ge(*when((f"res{i}", "ssq"), m - 1))
                    act.activation(sq[:, m % 2, 0:n], xT[:, m, 0:n], ACT.Square).then_inc(PH[f"res{i}", "sq"], 1)

            def ada(l, i):
                act.wait_ge(*product_of(("ada", l, i, 3)))
                turn = i + 12 * l
                if turn >= 2:
                    act.wait_ge(*auxiliary(("adaT", (turn - 2) // 12, (turn - 2) % 12)))
                key = ("ada", l, i, 3)
                release(act.activation(arow[:, turn % 2, :], G[group_of(key) % 4][0:2, 0:512], ACT.Copy), key)

            def residual_square(i, m, n):
                act.wait_ge(*when((f"res{i}", "x"), m + 1))
                if m >= 2:
                    act.wait_ge(*when((f"res{i}", "ssq"), m - 1))
                act.activation(sq[:, m % 2, 0:n], xT[:, m, 0:n], ACT.Square).then_inc(PH[f"res{i}", "sq"], 1)

            def norm(i, ranges, shift):
                n = sum(r[1] for r in ranges)
                act.wait_ge(*auxiliary(("norm", i)))
                release(act.activation(rsb[:, 1, 0:n // P], ps(("norm", i), n // P), ACT.Sqrt, bias=eps[:, 0:1]),
                        ("norm", i))
                act.wait_ge(gfree[group_of(("norm", i)) % 4], group_of(("norm", i)) // 4 + 1)
                act.sem_inc(PH[f"norm{i}", "std"], 1)
                for k in range(KD):
                    act.wait_ge(*when((f"norm{i}", "tmp"), k + 1))
                    for q, (t0, w) in enumerate(ranges):
                        ins = act.activation(hhi[:, k, t0:t0 + w], tmp[:, k % 2, t0:t0 + w], ACT.Identity,
                                             bias=shift(k, q))
                    ins.then_inc(PH[f"norm{i}", "hi"], 1)

            def inputs(st, sums, vts, n_units, other, split=True, prefetch=True, ada_groups=()):
                vs = sorted(vts)
                done_std = 0
                for n in range(n_units + 1):
                    if n < n_units:
                        key = (st, "U", n)
                        act.wait_ge(*product_of(key))
                        if split:
                            u = plan[key][0] + 2
                            if u < n_split and (prefetch or n + 2 < n_units):
                                upper(u)
                        if n in vts:
                            i = vs.index(n)
                            if i >= 2:
                                act.wait_ge(aux_done, plan[st, "V", vs[i - 2]][0] + 1)
                            ins = act.activation(tmp[:, i % 2, :] if st != "in2" else tmp[:, i % 2, 0:TX],
                                                 ps(key, T if st != "in2" else TX), ACT.Copy)
                            ins.then_inc(PH[st, "vcopy"], 1)
                            if n not in sums:
                                act.wait_ge(*when((st, "vcopy"), i + 1))
                                free(act, key)
                        if n in sums:
                            it = sums[n]
                            s, w = it["s"], it["n"]
                            dst = it["raw"]
                            rows = it["rows"] if not it["kr"] else HD
                            if dst is None:
                                if s >= 2:
                                    act.wait_ge(*when((st, "normed"), normed_before(sums, s - 1)))
                                dst = qr[0:rows, s % 2, 0:w]
                            act.activation(dst, ps(key, w, rows), ACT.Copy)
                            if s >= 2:
                                prev = [m for m in sums if sums[m]["s"] == s - 2][0]
                                act.wait_ge(aux_done, plan[st, "S", prev][0] + 1)
                            act.activation(sq[0:rows, s % 2, 0:w], ps(key, w, rows), ACT.Square).then_inc(PH[st, "square"], 1)
                            act.wait_ge(*when((st, "square"), s + 1))
                            free(act, key)
                        if n in other:
                            other[n](key)
                        if n < len(ada_groups):
                            ada(*ada_groups[n])
                    if n - 1 in sums and sums[n - 1]["stop"]:
                        it, key = sums[n - 1], (st, "S", n - 1)
                        rows, w = it["rows"], it["n"]
                        act.wait_ge(*auxiliary(key))
                        if done_std >= 2:
                            act.wait_ge(*when((st, "normed"), done_std - 1))
                        root = act.activation(rsb[0:rows, done_std % 2, 0:w], ps(key, w, rows), ACT.Sqrt,
                                              bias=eps[0:rows, 0:1])
                        root.then_inc(PH[st, "std"], 1)
                        done_std += 1

            def load_bias(h):
                for r2 in range(2):
                    src = bass.AP(pad_dram.tensor, (h * 15 + 1 - r2) * 127, [[1, GRID], [127, 14], [1, GRID]])
                    act.dma_start(nabias[h % 2][GRID * r2:GRID * r2 + GRID], src).then_inc(PH["att2", f"bias{h % 2}"], 16)

            def attention(i):
                units = ATT[i]
                st = f"att{i}"
                for n in range(len(units) + 1):
                    if i == 2 and n % 4 == 0 and 0 < n // 4 < NAH - 1:
                        h = n // 4 + 1
                        act.wait_ge(*when((st, "max"), 4 * (h - 1)))
                        load_bias(h)
                    if n < len(units):
                        un = units[n]
                        w = sum(k[2] for k in un["ks"])
                        act.wait_ge(*when((st, "max"), n + 1))
                        if n >= 2:
                            act.wait_ge(*when((st, "turned"), n - 1))
                        g = G[n % 2]
                        if un["kind"] == "plain":
                            ins = act.activation(Pm[:, n % 2, 0:w], g[:, 0:w], ACT.Exp, bias=stat[:, 0, n:n + 1],
                                                 accum_out=stat[:, 1, n:n + 1])
                        elif un["kind"] == "na":
                            act.activation(Pm[:, n % 2, 0:TX], Pm[:, n % 2, 0:TX], ACT.Exp, bias=stat[:, 0, n:n + 1],
                                           accum_out=stat[:, 1, n:n + 1])
                            ins = act.activation(Pm[:, n % 2, TX:T], g[:, TX:T], ACT.Exp, bias=stat[:, 0, n:n + 1],
                                                 accum_out=stat[:, 2, n:n + 1])
                        else:
                            ins = act.activation(Pm[:, n % 2, 0:w], Pm[:, n % 2, 0:w], ACT.Exp, bias=stat[:, 0, n:n + 1],
                                                 accum_out=stat[:, 1, n:n + 1])
                        ins.then_inc(PH[st, "prob"], 1)
                    if n >= 1:
                        m = n - 1
                        w = sum(k[2] for k in units[m]["ks"])
                        act.wait_ge(*when((st, "turned"), m + 1))
                        if m >= 2:
                            act.wait_ge(*when((st, "pv"), m - 1))
                        act.activation(PT[:, m % 2, 0:w], G[2][:, 0:w], ACT.Copy).then_inc(PH[st, "pt"], 1)

            def output_tiles(i, n_tiles, w, dst_hi, t0, scale=None, gated=()):
                for m in range(n_tiles):
                    key = (f"ot{i}", "OT", m)
                    act.wait_ge(*auxiliary(key))
                    s = 1.0 if scale is None else scale(m)
                    if m in gated:
                        act.wait_ge(*when((f"ot{i}", "done"), m - 1))
                        act.activation(tmp[:, m % 2, 0:w], ps(key, w), ACT.Copy, scale=s).then_inc(PH[f"ot{i}", "a"], 1)
                        act.wait_ge(*when((f"ot{i}", "b"), 1 + sorted(gated).index(m)))
                        ins = act.activation(dst_hi[:, t0 + m, 0:w], tmp[:, m % 2, 0:w], ACT.Copy)
                    else:
                        ins = act.activation(dst_hi[:, t0 + m, 0:w], ps(key, w), ACT.Copy, scale=s)
                    ins.then_inc(PH[f"ot{i}", "hi"], 1)

            def wout(l, i, n):
                for m in range(KD):
                    act.wait_ge(*product_of(("wout", l, m)))
                    upper(plan["wout", l, m][0] + 2)
                    if l == 0 and m < len(ADA_WOUT0):
                        ada(*ADA_WOUT0[m])
                    residual_square(i, m, n)

            def ffn(l, chunks, ranges, last_i):
                n = sum(r[1] for r in ranges)
                sems = f"ffn{l}"
                tiles = 0
                for c, (f0, nf) in enumerate(chunks):
                    key0 = ("up", l, c, 0)
                    u0 = plan[key0][0]
                    if c:
                        act.wait_ge(unit_done, plan["down", l, c - 1, KD - 1][0] + 1)

                    def gated_turn(j):
                        for b in range(4):
                            act.wait_ge(unit_done, u0 + b + 1 + 4 * j)
                            upper(u0 + b + 2, j)
                            t = tiles + b // 2
                            if b % 2 == 0:
                                if t >= 2 or not isinstance(j, int):
                                    act.wait_ge(*when((sems, "prod"), t - 1 + 2 * j))
                                g = (plan[key0][2] + b) % 4
                                act.activation(qr[:, b // 2, 0:n], G[g][:, 0:n], ACT.Silu).then_inc(PH[sems, "act"], 1)
                            else:
                                act.wait_ge(*when((sems, "prod"), t + 1 + 2 * j))
                                act.activation(ahi[:, bass.ds(j * 2 + b // 2, 1), 0:n] if not isinstance(j, int)
                                               else ahi[:, b // 2 + 2 * j:b // 2 + 2 * j + 1, 0:n],
                                               sq[:, b // 2:b // 2 + 1, 0:n], ACT.Copy).then_inc(PH[sems, "hi"], 1)

                    def plain_turn(j):
                        for b in range(4):
                            act.wait_ge(unit_done, u0 + b + 1 + 4 * j)
                            upper(u0 + b + 2, j)
                            t = tiles + b
                            if t >= 2 or not isinstance(j, int):
                                act.wait_ge(*when((sems, "lo"), t - 1 + 4 * j))
                            g = (plan[key0][2] + b) % 4
                            ins = act.activation(qr[:, b % 2, 0:n], G[g][:, 0:n], ACT.Relu)
                            ins.then_inc(PH[sems, "act"], 1)
                            act.wait_ge(*when((sems, "prod"), t + 1 + 4 * j))
                            act.activation(ahi[:, bass.ds(j * 4 + b, 1), 0:n] if not isinstance(j, int)
                                           else ahi[:, b + 4 * j:b + 4 * j + 1, 0:n],
                                           sq[:, b % 2:b % 2 + 1, 0:n], ACT.Copy).then_inc(PH[sems, "hi"], 1)

                    turn = plain_turn if l == 2 else gated_turn
                    per = 4 if l == 2 else 2
                    turn(0)
                    if nf // per > 1:
                        with act.Fori(1, nf // per) as j:
                            turn(j)
                    tiles += nf
                    last = c == len(chunks) - 1
                    for m in range(KD):
                        act.wait_ge(*product_of(("down", l, c, m)))
                        u = plan["down", l, c, m][0] + 2
                        if u < n_split:
                            upper(u)
                        if l == 0 and last and m < len(ADA_DOWN0) and ADA_DOWN0[m]:
                            ada(*ADA_DOWN0[m])
                        if last and last_i is not None:
                            residual_square(last_i, m, n)

            act_step = PH["set", "silu"]
            act.wait_ge(*auxiliary("cond"))
            act.activation(cs[:, :, 0], ps("cond")[:, 0:KD], ACT.Silu)
            act.activation(cs[:, :, 1], ps("cond")[:, KD:2 * KD], ACT.Silu).then_inc(PH["set", "silu"], 1)
            act.wait_ge(PH["set", "silu"], 1)
            free(act, "cond")
            for i in range(4):
                ada(0, i)
            upper(0)
            upper(1)
            residual_squares(0, True)
            norm(0, X_CTX, lambda k, q: mod[:, 0, k, q:q + 1])

            def pool_tile(i):
                def f(key):
                    g = ps(key)
                    act.activation(upad[:, i, 8:8 + TX], g[:, 0:TX], ACT.Copy)
                    ins = act.activation(upad[:, i, 24 + TX:24 + T], g[:, TX:T], ACT.Copy)
                    release(ins, key)
                return f

            inputs("in0", S0, L0_V, 12, {n: pool_tile(i) for i, n in enumerate(L0_POOL)}, ada_groups=ADA_IN0)
            for i in range(2):
                key = ("pool", i)
                act.wait_ge(*auxiliary(key))
                act.activation(hhi[:, i, :], ps(key), ACT.Copy, scale=vc("pscale", i)).then_inc(PH["in0", "pooly"], 1)
            attention(0)
            output_tiles(0, 6, T, hhi, 2)
            wout(0, 1, T)
            norm(1, X_CTX, lambda k, q: mod[:, 0, 24 + k, q:q + 1])
            ffn(0, FFN_CHUNKS, X_CTX, 2)
            norm(2, X_CTX, lambda k, q: mod[:, 1, k, q:q + 1])

            act.dma_start(rope[:], A["rope"][:, 2:4]).then_inc(PH["set", "rope1"], 16)

            def kr_rows(key):
                g = ps(key)
                ins = act.activation(krbuf[HD:MQK, :], g[HD:MQK, :], ACT.Copy)
                ins.then_inc(PH["in1", "kr"], 1)
                act.wait_ge(*when(("in1", "kr"), 1))
                free(act, key)

            inputs("in1", S1, (14, 15, 16, 17), 18, {5: kr_rows}, prefetch=False)
            inputs("mq", SQ, (), MH, {}, split=False)
            act.wait_ge(*when(("mq", "normed"), MH))
            act.wait_ge(aux_done, plan["mq", "S", MH - 1][0] + 1)
            for s in range(2):
                act.activation(qr[HD:MQK, s, :], krbuf[HD:MQK, :], ACT.Copy)
                act.activation(sq[HD:MQK, s, :], krbuf[HD:MQK, :], ACT.Square)
            inputs("mk", SK, tuple(range(MH)), MH, {}, split=False)
            upper(plan["wout", 1, 0][0])
            upper(plan["wout", 1, 1][0])
            act.wait_ge(*when(("mk", "normed"), MH))
            act.wait_ge(*when(("mk", "vdone"), MH))
            load_bias(0)
            load_bias(1)
            attention(1)
            attention(2)
            output_tiles(1, 4, TX, hhi, 0)
            output_tiles(2, 4, TX, hhi, 4)
            wout(1, 3, TX)
            norm(3, X_ONLY, lambda k, q: mod[:, 1, 24 + k, q:q + 1])
            ffn(1, FFN_CHUNKS, X_ONLY, 4)
            norm(4, X_ONLY, lambda k, q: zero8[:, k:k + 1])

            def forget(key):
                g = ps(key, TX, N_FOX)
                act.wait_ge(*when(("set", "b"), 16))
                act.wait_ge(*when(("mk", "rotated"), MH))
                link2(act.activation(cum[0:N_FOX, :], g, ACT.Identity, bias=bfox[:, 0:1]))
                link2(act.activation(lsig[0:N_FOX, :], cum[0:N_FOX, :], ACT.Abs))
                link2(act.activation(lsig[0:N_FOX, :], lsig[0:N_FOX, :], ACT.Exp, scale=-1.0))
                link2(act.activation(lsig[0:N_FOX, :], lsig[0:N_FOX, :], ACT.Ln, bias=1.0))
                free(act, key)

            fcount = [0]

            def link2(ins):
                fcount[0] += 1
                ins.then_inc(PH["in2", "fg"], 1)
                act.wait_ge(*when(("in2", "fg"), fcount[0]))

            def out_gate(i):
                def f(key):
                    release(act.activation(gsig[:, i, :], ps(key, TX), ACT.Sigmoid), key)
                return f

            inputs("in2", S2, tuple(range(16, 24)), 28, {24: forget, 25: out_gate(0), 26: out_gate(1), 27: out_gate(2)})
            act.wait_ge(unit_done, plan["in2", "U", 27][0] + 1)
            act.dma_start(band, A["band"]).then_inc(PH["set", "band"], 16)
            act.dma_start(sel[0:N_FOX], A["sel"]).then_inc(PH["set", "band"], 16)
            attention(3)
            act.wait_ge(*when(("att3", "o"), len(ATT[3])))
            groups = ((0, 256), (256, 384), (640, 384))
            for q in range(4):
                for gi, (c0, w) in enumerate(groups):
                    ins = act.activation(tmp[:, 0, 0:w], o2[:, q, c0:c0 + w], ACT.Square, accum_out=ss12[:, 0, gi, q:q + 1])
                    ins.then_inc(PH["in2", "outsq"], 1)
                    act.wait_ge(*when(("in2", "outsq"), 3 * q + gi + 1))
            act.activation(ss12[:, 1, 0:1, :], ss12[:, 0, 0:1, :], ACT.Sqrt, bias=eps[:, 0:1], scale=1.0 / 256)
            act.activation(ss12[:, 1, 1:3, :], ss12[:, 0, 1:3, :], ACT.Sqrt, bias=eps[:, 0:1],
                           scale=1.0 / 384).then_inc(PH["in2", "outstd"], 1)
            output_tiles(3, 8, TX, ahi, 0, lambda m: vc("og2", m), (2, 3, 4))
            wout(2, 5, TX)
            norm(5, X_ONLY, lambda k, q: zero8[:, k:k + 1])
            ffn(2, FF2_CHUNKS, X_ONLY, None)

        @block.tensor
        def _(pe):
            def take_group(g):
                if g >= 4:
                    pe.wait_ge(gfree[g % 4], g // 4)

            def unit(key, rhi, rlo, ranges, k_tiles=KD, j=0, h_ready=None):
                u, r, g = plan[key]
                pe.wait_ge(raw_free[r % RING], r // RING + 1 + j)
                if g >= 4:
                    pe.wait_ge(gfree[g % 4], g // 4 + j)
                for k in range(k_tiles):
                    if h_ready is not None:
                        pe.wait_ge(*when(h_ready[:2], k + 1 + (h_ready[2] if len(h_ready) > 2 else 0)))
                    for t0, w in ranges:
                        o = G[g % 4][:, t0:t0 + w]
                        pe.matmul(o, whi[:, u % 2, k], rlo[:, k, t0:t0 + w], start=k == 0, stop=False)
                        pe.matmul(o, wlo[:, u % 2, k], rhi[:, k, t0:t0 + w], start=False, stop=False)
                        mm = pe.matmul(o, whi[:, u % 2, k], rhi[:, k, t0:t0 + w], start=False, stop=k == k_tiles - 1)
                mm.then_inc(unit_done, 1)

            def first_units(keys, ranges_of, h_ready):
                for key in keys:
                    _, r, g = plan[key]
                    pe.wait_ge(raw_free[r % RING], r // RING + 1)
                    take_group(g)
                for k in range(KD):
                    pe.wait_ge(*when(h_ready, k + 1))
                    for i, key in enumerate(keys):
                        u, _, g = plan[key]
                        for t0, w in ranges_of(i):
                            o = G[g % 4][:, t0:t0 + w]
                            pe.matmul(o, whi[:, u % 2, k], hlo[:, k, t0:t0 + w], start=k == 0, stop=False)
                            pe.matmul(o, wlo[:, u % 2, k], hhi[:, k, t0:t0 + w], start=False, stop=False)
                            mm = pe.matmul(o, whi[:, u % 2, k], hhi[:, k, t0:t0 + w], start=False, stop=k == KD - 1)
                        if k == KD - 1:
                            mm.then_inc(unit_done, 1)

            def ada(l, i):
                g = plan["ada", l, i, 0][2]
                take_group(g)
                for q in range(4):
                    r = plan["ada", l, i, q][1]
                    pe.wait_ge(landed[r % RING], ring_total[r])
                    w = raw[:, r % RING].rearrange("p (a b) c -> p a (b c)", a=2)
                    for k in range(2):
                        mm = pe.matmul(G[g % 4][0:2, 0:512], cs[:, 2 * q + k, :], w[:, k],
                                       start=q == 0 and k == 0, stop=q == 3 and k == 1)
                    mm.then_inc(raw_free[r % RING], 1)

            def ada_turn(l, i):
                a, g = plan["adaT", l, i]
                turn = i + 12 * l
                key = ("ada", l, i, 3)
                pe.wait_ge(gfree[group_of(key) % 4], group_of(key) // 4 + 1)
                take_group(g)
                for b in range(4):
                    mm = pe.transpose(G[g % 4][:, 2 * b:2 * b + 2], arow[:, turn % 2, P * b:P * b + P], ident[0:2, 0:2])
                aux(mm)

            def direct(key, x, m, ranges, k_tiles):
                _, r, g = plan[key]
                pe.wait_ge(landed[r % RING], ring_total[r])
                take_group(g)
                for k in range(k_tiles):
                    for t0, w in ranges:
                        mm = pe.matmul(G[g % 4][0:m, t0:t0 + w], raw[:, r % RING, k, 0:m], x[:, k, t0:t0 + w],
                                       start=k == 0, stop=k == k_tiles - 1)
                mm.then_inc(raw_free[r % RING], 1)

            def aux(mm):
                mm.then_inc(aux_done, 1)

            def norm(i, n):
                a, g = plan["norm", i]
                pe.wait_ge(*when((f"res{i}", "ssq"), KD))
                take_group(g)
                for t in range(n // P):
                    mm = pe.matmul(G[g % 4][:, t:t + 1], ssq[:, P * t:P * t + P], ones_d[:, 0:1], start=True, stop=True)
                aux(mm)
                a, g = plan["spread", i]
                take_group(g)
                pe.wait_ge(*when((f"norm{i}", "diag"), 1))
                for t0 in range(0, n, 512):
                    w = min(512, n - t0)
                    mm = pe.matmul(G[g % 4][:, t0:t0 + w], ones_d, rsb[:, 0, t0:t0 + w], start=True, stop=True)
                aux(mm)

            def inputs(st, sums, vts, rhs, n_units, ranges_of, h_ready=None, direct_of=None):
                vs = sorted(vts)
                for op, n in plan[st, "seq"]:
                    if op == "A":
                        ada(*n)
                        continue
                    if op == "AT":
                        ada_turn(*n)
                        continue
                    if op == "U":
                        if direct_of is not None:
                            direct_of((st, "U", n))
                        elif n == 0:
                            first_units([(st, "U", 0), (st, "U", 1)], ranges_of, h_ready)
                        elif n > 1:
                            unit((st, "U", n), rhs[0], rhs[1], ranges_of(n))
                        continue
                    a, g = plan[st, op, n]
                    if op == "V":
                        i = vs.index(n)
                        pe.wait_ge(*when((st, "vcopy"), i + 1))
                        take_group(g)
                        tiles = 4 if st == "in2" else 6
                        for t in range(tiles):
                            mm = pe.transpose(G[g % 4][:, P * t:P * t + P], tmp[:, i % 2, P * t:P * t + P], ident)
                    elif op == "S":
                        it = sums[n]
                        pe.wait_ge(*when((st, "square"), it["s"] + 1))
                        if it["start"]:
                            take_group(g)
                        rows = it["rows"]
                        for t0 in range(0, it["n"], 512):
                            w = min(512, it["n"] - t0)
                            mm = pe.matmul(G[g % 4][0:rows, t0:t0 + w], it["mat"][0:rows, 0:rows],
                                           sq[0:rows, it["s"] % 2, t0:t0 + w], start=it["start"], stop=it["stop"])
                    else:
                        it = sums[n]
                        pe.wait_ge(*when((st, "normed"), normed_before(sums, it["s"] + 1)))
                        take_group(g)
                        rows = it["rows"]
                        m = rot64 if rows == P else rot32
                        mm = pe.matmul(G[g % 4][0:rows, 0:TX], m[0:rows, 0:rows], it["dst"][:, 0:TX], start=True, stop=True)
                    aux(mm)

            def attention(i, g_done):
                st = f"att{i}"
                units = ATT[i]
                for q in range(4):
                    uses = (g_done - q + 3) // 4
                    if uses > 0:
                        pe.wait_ge(gfree[q], uses)
                for n in range(len(units) + 2):
                    if n < len(units):
                        un = units[n]
                        if n >= 2:
                            pe.wait_ge(*when((st, "prob"), n - 1))
                        per = len(units) // len(QUERIES.get(i, units))
                        if i in QUERIES and n % per == 0:
                            pe.wait_ge(*when((st, "head"), n // per + 1))
                        fox = un.get("fox")
                        for q, (kt, c0, w) in enumerate(un["ks"]):
                            o = G[n % 2][:, c0:c0 + w]
                            mm = pe.matmul(o, un["q"], kt, start=True, stop=fox is None)
                            if fox is not None:
                                mm = pe.matmul(o, sel[0:N_FOX, fox, :], cum[0:N_FOX, 0:w], start=False, stop=True)
                        mm.then_inc(PH[st, "scores"], 1)
                    if 1 <= n <= len(units):
                        m = n - 1
                        pe.wait_ge(*when((st, "prob"), m + 1))
                        if m >= 1:
                            pe.wait_ge(*when((st, "pt"), m))
                        for t in range(len(units[m]["vs"])):
                            mm = pe.transpose(G[2][:, P * t:P * t + P], Pm[:, m % 2, P * t:P * t + P], ident)
                        mm.then_inc(PH[st, "turned"], 1)
                    if n >= 2:
                        m = n - 2
                        pe.wait_ge(*when((st, "pt"), m + 1))
                        if m >= 2:
                            pe.wait_ge(*when((st, "o"), m - 1))
                        vs = units[m]["vs"]
                        for t, v in enumerate(vs):
                            mm = pe.matmul(G[3][:, 512 * (m % 2):512 * (m % 2) + HD], PT[:, m % 2, P * t:P * t + P], v,
                                           start=t == 0, stop=t == len(vs) - 1)
                        mm.then_inc(PH[st, "pv"], 1)

            def turn_outputs(i, n_tiles, o, tiles, ready, value):
                pe.wait_ge(*when(ready, value))
                for m in range(n_tiles):
                    a, g = plan[f"ot{i}", "OT", m]
                    take_group(g)
                    for t in range(tiles):
                        mm = pe.transpose(G[g % 4][:, P * t:P * t + P], o[:, t, P * m:P * m + P], ident)
                    aux(mm)

            def square(key, rhs, ranges, k_tiles=KD, ada_groups=(), first_ready=None):
                for m in range(KD):
                    unit(key + (m,), rhs[0], rhs[1], ranges, k_tiles=k_tiles, h_ready=first_ready if m == 0 else None)
                    if 0 < m <= len(ada_groups) and ada_groups[m - 1]:
                        ada_turn(*ada_groups[m - 1])
                    if m < len(ada_groups) and ada_groups[m]:
                        ada(*ada_groups[m])

            def wout(l, rhs, ranges):
                square(("wout", l), rhs, ranges, ada_groups=ADA_WOUT0 if l == 0 else ())

            def ffn(l, chunks, ranges, h_ready):
                per = 4 if l == 2 else 2
                tiles = 0
                for c, (f0, nf) in enumerate(chunks):
                    if c == 0:
                        first_units([("up", l, 0, 0), ("up", l, 0, 1)], lambda b: ranges, h_ready)
                        for b in range(2, 4):
                            unit(("up", l, 0, b), hhi, hlo, ranges)
                    with pe.Fori(1 if c == 0 else 0, nf // per) as j:
                        for b in range(4):
                            unit(("up", l, c, b), hhi, hlo, ranges, j=j)
                    first = (f"ffn{l}", "lo", tiles)
                    tiles += nf
                    if l == 0 and c == len(chunks) - 1:
                        square(("down", l, c), (ahi, alo), ranges, nf, ADA_DOWN0, first)
                        continue
                    for b in range(4):
                        unit(("down", l, c, b), ahi, alo, ranges, k_tiles=nf, h_ready=first if b == 0 else None)
                    for b in range(4, 8):
                        unit(("down", l, c, b), ahi, alo, ranges, k_tiles=nf)

            pe.wait_ge(*when(("set", "cond"), 48))
            a, g = plan["cond"]
            aux(pe.transpose(G[g % 4][:, 0:2 * KD], vrow[0:2 * KD, 1, :], ident[0:2 * KD, 0:2 * KD]))
            pe.wait_ge(*when(("set", "silu"), 1))
            for i in range(4):
                ada(0, i)
                if i:
                    ada_turn(0, i - 1)
                    continue
                pe.wait_ge(*when(("set", "tables"), 32))
                pe.wait_ge(*when(("set", "rows"), 16 * 24))
                a, g = plan["vec"]
                pe.transpose(G[g % 4][:, 0:P], vrow[:, 0, :], ident)
                aux(pe.transpose(G[g % 4][:, P:P + VROWS2], vrow[0:VROWS2, 1, :], ident[0:VROWS2, 0:VROWS2]))
            ada_turn(0, 3)
            pe.wait_ge(*when(("set", "xload"), 32))
            for m in range(KD):
                a, g = plan["xin", m]
                take_group(g)
                for t in range(6):
                    mm = pe.transpose(G[g % 4][:, P * t:P * t + P], xtok[:, t, P * m:P * m + P], ident)
                aux(mm)
            norm(0, T)
            inputs("in0", S0, L0_V, (hhi, hlo), 12, lambda n: X_CTX, h_ready=("norm0", "h"))
            pe.wait_ge(*when(("in0", "pooled"), 1))
            pe.wait_ge(*when(("set", "poolw"), 64))
            for i in range(2):
                a, g = plan["pool", i]
                take_group(g)
                for t0, w in X_CTX:
                    mm = pe.matmul(G[g % 4][:, t0:t0 + w], poolw[:, i, :], dT[:, i, t0:t0 + w], start=True, stop=True)
                aux(mm)
            pe.wait_ge(*when(("in0", "rotated"), 8))
            pe.wait_ge(*when(("in0", "vdone"), 2))
            attention(0, group_of(("pool", 1)) + 1)
            turn_outputs(0, 6, o0, 6, ("att0", "o"), len(ATT[0]))
            pe.wait_ge(*when(("ot0", "done"), 6))
            pe.wait_ge(*when(("in0", "pooldone"), 2))
            wout(0, (hhi, hlo), X_CTX)
            norm(1, T)
            ffn(0, FFN_CHUNKS, X_CTX, ("norm1", "h"))
            norm(2, T)
            inputs("in1", S1, (14, 15, 16, 17), (hhi, hlo), 18,
                   lambda n: X_ONLY if n < 3 or 6 <= n < 10 else X_CTX, h_ready=("norm2", "h"))
            pe.wait_ge(*when(("in1", "normed"), 2))
            inputs("mq", SQ, (), None, MH, None, direct_of=lambda key: direct(key, cqn, MQK, X_ONLY, 3))
            inputs("mk", SK, range(MH), None, MH, None, direct_of=lambda key: direct(key, ckvn, P, X_CTX, 2))
            pe.wait_ge(*when(("mq", "rotated"), MH))
            pe.wait_ge(*when(("mk", "rotated"), MH))
            pe.wait_ge(*when(("mk", "vdone"), MH))
            pe.wait_ge(*when(("set", "below"), 1))
            attention(1, group_of(("mk", "R", MH - 1)) + 1)
            pe.wait_ge(*when(("in1", "vdone"), 4))
            pe.wait_ge(*when(("in1", "normed"), 10))
            pe.wait_ge(*when(("att1", "o"), len(ATT[1])))
            attention(2, group_of(("mk", "R", MH - 1)) + 1)
            turn_outputs(1, 4, omla, 4, ("att2", "o"), len(ATT[2]))
            turn_outputs(2, 4, ona, 4, ("att2", "o"), len(ATT[2]))
            pe.wait_ge(*when(("ot1", "done"), 4))
            pe.wait_ge(*when(("ot2", "done"), 4))
            wout(1, (hhi, hlo), X_ONLY)
            norm(3, TX)
            ffn(1, FFN_CHUNKS, X_ONLY, ("norm3", "h"))
            norm(4, TX)
            inputs("in2", S2, tuple(range(16, 24)), (hhi, hlo), 28, lambda n: X_ONLY, h_ready=("norm4", "h"))
            pe.wait_ge(*when(("in2", "normed"), 16))
            pe.wait_ge(*when(("in2", "vdone"), 8))
            pe.wait_ge(*when(("in2", "cum"), 1))
            pe.wait_ge(*when(("set", "band"), 32))
            attention(3, group_of(("in2", "U", 27)) + 1)
            turn_outputs(3, 8, o2, 4, ("in2", "outn"), 12)
            pe.wait_ge(*when(("ot3", "done"), 8))
            wout(2, (ahi, alo), X_ONLY)
            norm(5, TX)
            ffn(2, FF2_CHUNKS, X_ONLY, ("norm5", "h"))
            pe.wait_ge(*when(("fin", "x"), KD))
            for t in range(4):
                a, g = plan["xout", t]
                take_group(g)
                for m in range(KD):
                    mm = pe.transpose(G[g % 4][:, P * m:P * m + P], xT[:, m, P * t:P * t + P], ident)
                aux(mm)

        @block.vector
        def _(dve):
            dve_step = PH["set", "steps"]
            chain = [0]

            def mark(ins):
                chain[0] += 1
                return ins.then_inc(dve_step, 1)

            def link(ins):
                mark(ins)
                dve.wait_ge(dve_step, chain[0])

            def ada_columns(l, i):
                key = ("adaT", l, i)
                dve.wait_ge(*auxiliary(key))
                release(dve.tensor_tensor(mod[:, l, 4 * i:4 * i + 4, :], ps(key, 8).rearrange("p (a b) -> p a b", b=2),
                                          vcol[:, 0, 64 * l + 4 * i:64 * l + 4 * i + 4].rearrange("p (a b) -> p a b", b=1)
                                          .broadcast_to([P, 4, 2]), ALU.add), key)

            def modulation_gain(l, s):
                key = ("adaT", l, (24 * s + 15) // 4)
                dve.wait_ge(gfree[group_of(key) % 4], group_of(key) // 4 + 1)
                gains = vcol[:, 0, 64 * l + 48 + 8 * s:64 * l + 56 + 8 * s]
                link(dve.scalar_tensor_tensor(out=amix[:, 2 * l + s], in0=mod[:, l, 24 * s + 8:24 * s + 16, :], scalar=1.0,
                                              in1=gains.rearrange("p (a b) -> p a b", b=1).broadcast_to([P, KD, 2]),
                                              op0=ALU.add, op1=ALU.mult))

            def sum_squares(i, m, n):
                dve.wait_ge(*when((f"res{i}", "sq"), m + 1))
                if m == 0:
                    ins = dve.tensor_copy(ssq[:, 0:n], sq[:, 0, 0:n])
                else:
                    dve.wait_ge(*when((f"res{i}", "ssq"), m))
                    ins = dve.tensor_tensor(ssq[:, 0:n], ssq[:, 0:n], sq[:, m % 2, 0:n], ALU.add)
                ins.then_inc(PH[f"res{i}", "ssq"], 1)

            def norm(i, ranges, gain, shift):
                n = sum(r[1] for r in ranges)
                dve.wait_ge(*when((f"norm{i}", "std"), 1))
                tiles = n // P
                link(dve.reciprocal(rsb[:, 1, 8:8 + tiles], rsb[:, 1, 0:tiles]))
                dve.scalar_tensor_tensor(out=rsb[:, 0, 0:n].rearrange("p (a b) -> p a b", b=P),
                                         in0=ident.rearrange("p (a b) -> p a b", a=1).broadcast_to([P, tiles, P]),
                                         scalar=float(D),
                                         in1=rsb[:, 1, 8:8 + tiles].rearrange("p (a b) -> p a b", b=1)
                                         .broadcast_to([P, tiles, P]),
                                         op0=ALU.mult, op1=ALU.mult).then_inc(PH[f"norm{i}", "diag"], 1)
                dve.wait_ge(*auxiliary(("spread", i)))
                inv = ps(("spread", i), n)
                for k in range(KD + 1):
                    if k < KD:
                        if k >= 2:
                            dve.wait_ge(*when((f"norm{i}", "h"), k - 1))
                        for q, (t0, w) in enumerate(ranges):
                            ins = dve.scalar_tensor_tensor(out=tmp[:, k % 2, t0:t0 + w], in0=xT[:, k, t0:t0 + w],
                                                           scalar=gain(k, q), in1=inv[:, t0:t0 + w],
                                                           op0=ALU.mult, op1=ALU.mult)
                        ins.then_inc(PH[f"norm{i}", "tmp"], 1)
                        if k == KD - 1:
                            dve.wait_ge(*when((f"norm{i}", "tmp"), KD))
                            free(dve, ("spread", i))
                    if k >= 1:
                        dve.wait_ge(*when((f"norm{i}", "hi"), k))
                        for q, (t0, w) in enumerate(ranges):
                            ins = dve.scalar_tensor_tensor(out=hlo[:, k - 1, t0:t0 + w], in0=tmp[:, (k - 1) % 2, t0:t0 + w],
                                                           scalar=shift(k - 1, q),
                                                           in1=hhi[:, k - 1, t0:t0 + w].bitcast(F32),
                                                           op0=ALU.add, op1=ALU.subtract)
                        ins.then_inc(PH[f"norm{i}", "h"], 1)

            def inputs(st, sums, vts, n_units, vdst, extra=None, ada_groups=()):
                vs = sorted(vts)
                done = rotated = 0
                for n in range(1, n_units + 2):
                    if n - 1 < len(ada_groups):
                        ada_columns(*ada_groups[n - 1])
                    if n - 1 in vts:
                        key, i = (st, "V", n - 1), vs.index(n - 1)
                        dve.wait_ge(*auxiliary(key))
                        vdst(i, key)
                    if n - 1 in sums and sums[n - 1]["stop"]:
                        it, key = sums[n - 1], (st, "S", n - 1)
                        rows, w = it["rows"], it["n"]
                        dve.wait_ge(*when((st, "std"), done + 1))
                        rs = rsb[0:rows, done % 2, 0:w]
                        release(dve.reciprocal(rs, rs), key)
                        dve.wait_ge(gfree[group_of(key) % 4], group_of(key) // 4 + 1)
                        members = it["members"] or [(qr[0:rows, it["s"] % 2, 0:w], it["dst"][:, 0:w], it["gain"])]
                        for src, dst, gain in members:
                            ins = dve.scalar_tensor_tensor(out=dst, in0=src, scalar=gain[0:rows], in1=rs,
                                                           op0=ALU.mult, op1=ALU.mult)
                        ins.then_inc(PH[st, "normed"], 1)
                        done += 1
                    if n - 2 in sums and sums[n - 2]["rope"]:
                        it, key = sums[n - 2], (st, "R", n - 2)
                        rows = it["rows"]
                        dve.wait_ge(*auxiliary(key))
                        if rotated:
                            dve.wait_ge(*when((st, "rotated"), rotated))
                        rotated += 1
                        release(dve.tensor_tensor(rt[0:rows, 0, :], ps(key, TX, rows), rope[0:rows, 1, :], ALU.mult), key)
                        link(dve.tensor_tensor(rt[0:rows, 1, :], it["dst"][:, 0:TX], rope[0:rows, 0, :], ALU.mult))
                        dve.wait_ge(gfree[group_of(key) % 4], group_of(key) // 4 + 1)
                        dve.tensor_tensor(it["dst"][:, 0:TX], rt[0:rows, 1, :], rt[0:rows, 0, :],
                                          ALU.add).then_inc(PH[st, "rotated"], 1)
                    if extra and n in extra:
                        extra[n]()

            def attention(i):
                st = f"att{i}"
                units = ATT[i]
                for n in range(len(units) + 2):
                    if n < len(units):
                        un = units[n]
                        w = sum(k[2] for k in un["ks"])
                        g = G[n % 2]
                        if un["kind"] == "na" and n % 4 == 0:
                            dve.wait_ge(*when((st, "masked"), un["head"] + 1))
                        if un["kind"] == "band" and n % 4 == 0 and un["fox"] is None:
                            h = un["head"]
                            moba = h < N_MOBA
                            slope = SLOPES[N_DIL + h] if moba else SLOPES[h - N_MOBA - N_FOX]
                            if n == 0:
                                dve.wait_ge(*when(("set", "band"), 32))
                            if h >= 2:
                                dve.wait_ge(*when((st, "max"), 4 * (h - 1)))
                            if moba:
                                link(dve.tensor_scalar(th[:, h % 2], band[:, 0], -slope, None, ALU.mult))
                            else:
                                link(dve.scalar_tensor_tensor(out=th[:, h % 2], in0=band[:, 1], scalar=-slope,
                                                              in1=band[:, 2], op0=ALU.mult, op1=ALU.add))
                        dve.wait_ge(*when((st, "scores"), n + 1))
                        if un["kind"] == "plain":
                            dve.tensor_reduce(stat[:, 0, n:n + 1], g[:, 0:w], AX_X, ALU.max,
                                              negate=True).then_inc(PH[st, "max"], 1)
                        else:
                            if n >= 2:
                                dve.wait_ge(*when((st, "turned"), n - 1))
                            wb = TX if un["kind"] == "na" else w
                            dst, src = Pm[:, n % 2, 0:wb], g[:, 0:wb]
                            if un["kind"] == "na":
                                dst, src = (v.rearrange("p (a b) -> p a b", b=GRID) for v in (dst, src))
                            mark(dve.tensor_tensor(dst, src, un["bias"], ALU.add))
                            dve.wait_ge(dve_step, chain[0])
                            if un["kind"] == "na":
                                mark(dve.tensor_reduce(stat[:, 2, n:n + 1], Pm[:, n % 2, 0:wb], AX_X, ALU.max, negate=True))
                                link(dve.tensor_reduce(stat[:, 3, n:n + 1], g[:, TX:T], AX_X, ALU.max, negate=True))
                                dve.tensor_tensor(stat[:, 0, n:n + 1], stat[:, 2, n:n + 1], stat[:, 3, n:n + 1],
                                                  ALU.min).then_inc(PH[st, "max"], 1)
                            else:
                                dve.tensor_reduce(stat[:, 0, n:n + 1], Pm[:, n % 2, 0:wb], AX_X, ALU.max,
                                                  negate=True).then_inc(PH[st, "max"], 1)
                    if n >= 2:
                        m = n - 2
                        dve.wait_ge(*when((st, "pv"), m + 1))
                        total = stat[:, 1, m:m + 1]
                        if units[m]["kind"] == "na":
                            link(dve.tensor_tensor(total, total, stat[:, 2, m:m + 1], ALU.add))
                        link(dve.reciprocal(stat[:, 3, m:m + 1], total))
                        dve.tensor_scalar(units[m]["o"], G[3][:, 512 * (m % 2):512 * (m % 2) + HD],
                                          stat[:, 3, m:m + 1], None, ALU.mult).then_inc(PH[st, "o"], 1)

            def output_tiles(i, n_tiles, w, dst_hi, dst_lo, t0, scale=None, gated=()):
                for m in range(n_tiles):
                    key = (f"ot{i}", "OT", m)
                    if m in gated:
                        gi = sorted(gated).index(m)
                        dve.wait_ge(*when((f"ot{i}", "a"), gi + 1))
                        t = tmp[:, m % 2, 0:w]
                        dve.tensor_tensor(t, t, gsig[:, gi, 0:w], ALU.mult).then_inc(PH[f"ot{i}", "b"], 1)
                        dve.wait_ge(*when((f"ot{i}", "hi"), m + 1))
                        ins = dve.tensor_tensor(dst_lo[:, t0 + m, 0:w], t, dst_hi[:, t0 + m, 0:w].bitcast(F32), ALU.subtract)
                    else:
                        dve.wait_ge(*when((f"ot{i}", "hi"), m + 1))
                        s = 1.0 if scale is None else scale(m)
                        ins = dve.scalar_tensor_tensor(out=dst_lo[:, t0 + m, 0:w], in0=ps(key, w), scalar=s,
                                                       in1=dst_hi[:, t0 + m, 0:w].bitcast(F32), op0=ALU.mult, op1=ALU.subtract)
                    ins.then_inc(PH[f"ot{i}", "done"], 1)
                    dve.wait_ge(*when((f"ot{i}", "done"), m + 1))
                    free(dve, key)

            def residual(key, m, ranges, gate, j=0, dyn=False):
                g = group_of(key) % 4
                for q, (t0, w) in enumerate(ranges):
                    x = xT[:, bass.ds(j * 4 + m, 1), t0:t0 + w] if dyn else xT[:, m:m + 1, t0:t0 + w]
                    src = G[g][:, t0:t0 + w].rearrange("p (a t) -> p a t", a=1)
                    if gate is None:
                        ins = dve.tensor_tensor(x, src, x, ALU.add)
                    else:
                        ins = dve.scalar_tensor_tensor(out=x, in0=src, scalar=gate(m, q, j, dyn), in1=x,
                                                       op0=ALU.mult, op1=ALU.add)
                return ins

            def residual_tiles(keys, i, ranges, gate, ada_groups=()):
                n = sum(r[1] for r in ranges)
                for m in range(KD + 1):
                    if m < KD:
                        dve.wait_ge(*product_of(keys(m)))
                        ins = residual(keys(m), m, ranges, gate)
                        ins.then_inc(PH[f"res{i}", "x"] if i is not None else PH["fin", "x"], 1)
                        dve.wait_ge(*when((f"res{i}", "x") if i is not None else ("fin", "x"), m + 1))
                        free(dve, keys(m))
                        if 0 < m <= len(ada_groups) and ada_groups[m - 1]:
                            ada_columns(*ada_groups[m - 1])
                    if m >= 1 and i is not None:
                        sum_squares(i, m - 1, n)

            def gate_of(l, at):
                def f(m, q, j, dyn):
                    if dyn:
                        return mod[:, l, bass.ds(j * 4 + (at + m), 1), q:q + 1].rearrange("p a b -> p (a b)")
                    return mod[:, l, at + m, q:q + 1]
                return f

            def ffn(l, chunks, ranges, gate, last_i):
                n = sum(r[1] for r in ranges)
                sems = f"ffn{l}"
                tiles = 0
                for c, (f0, nf) in enumerate(chunks):
                    key0 = ("up", l, c, 0)
                    u0, _, g0 = plan[key0]

                    def tile_at(j, per, b):
                        if isinstance(j, int):
                            return slice(per * j + b, per * j + b + 1)
                        return bass.ds(j * per + b, 1)

                    def gated_turn(j):
                        for b in range(2):
                            t = tiles + b
                            dve.wait_ge(unit_done, u0 + 2 * b + 2 + 4 * j)
                            dve.wait_ge(*when((sems, "act"), t + 1 + 2 * j))
                            if t >= 2 or not isinstance(j, int):
                                dve.wait_ge(*when((sems, "lo"), t - 1 + 2 * j))
                            gg, gu = (g0 + 2 * b) % 4, (g0 + 2 * b + 1) % 4
                            dve.tensor_tensor(sq[:, b, 0:n], G[gu][:, 0:n], qr[:, b, 0:n], ALU.mult).then_inc(PH[sems, "prod"], 1)
                            dve.wait_ge(*when((sems, "prod"), t + 1 + 2 * j))
                            dve.sem_inc(gfree[gg], 1)
                            dve.sem_inc(gfree[gu], 1)
                            dve.wait_ge(*when((sems, "hi"), t + 1 + 2 * j))
                            dve.tensor_tensor(alo[:, tile_at(j, 2, b), 0:n], sq[:, b:b + 1, 0:n],
                                              ahi[:, tile_at(j, 2, b), 0:n].bitcast(F32),
                                              ALU.subtract).then_inc(PH[sems, "lo"], 1)

                    def plain_turn(j):
                        for b in range(4):
                            t = tiles + b
                            dve.wait_ge(*when((sems, "act"), t + 1 + 4 * j))
                            dve.tensor_tensor(sq[:, b % 2, 0:n], qr[:, b % 2, 0:n], qr[:, b % 2, 0:n],
                                              ALU.mult).then_inc(PH[sems, "prod"], 1)
                            dve.sem_inc(gfree[(g0 + b) % 4], 1)
                            dve.wait_ge(*when((sems, "hi"), t + 1 + 4 * j))
                            dve.tensor_tensor(alo[:, tile_at(j, 4, b), 0:n], sq[:, b % 2:b % 2 + 1, 0:n],
                                              ahi[:, tile_at(j, 4, b), 0:n].bitcast(F32),
                                              ALU.subtract).then_inc(PH[sems, "lo"], 1)

                    turn = plain_turn if l == 2 else gated_turn
                    per = 4 if l == 2 else 2
                    turn(0)
                    if nf // per > 1:
                        with dve.Fori(1, nf // per) as j:
                            turn(j)
                    tiles += nf
                    if c == len(chunks) - 1:
                        residual_tiles(lambda m: ("down", l, c, m), last_i, ranges, gate, ADA_DOWN0 if l == 0 else ())
                    else:
                        with dve.Fori(0, 2) as j:
                            for b in range(4):
                                key = ("down", l, c, b)
                                dve.wait_ge(*product_of(key, j))
                                residual(key, b, ranges, gate, j, dyn=True).then_inc(gfree[group_of(key) % 4], 1)

            mark(dve.memset(eps[:], EPS))
            mark(dve.memset(zero8[:], 0.0))
            mark(dve.memset(stat[:], 0.0))
            dve.wait_ge(*auxiliary("vec"))
            link(dve.tensor_copy(vcol[:, 0, :], ps("vec")[:, 0:P]))
            key = "vec"
            dve.tensor_copy(vcol[:, 1, 0:VROWS2], ps("vec")[:, P:P + VROWS2]).then_inc(PH["set", "cols"], 1)
            dve.wait_ge(*when(("set", "cols"), 1))
            scaled = ((VC["q2"], 8, HD), (VC["q0"], 1, HD), (VC["nq"], 1, HD), (VC["mq"], 1, MQK))
            for c0, w, d in scaled:
                ins = mark(dve.tensor_scalar(vcol[:, 1, c0:c0 + w], vcol[:, 1, c0:c0 + w], float(d) ** -0.5, None, ALU.mult))
            dve.wait_ge(dve_step, chain[0])
            dve.sem_inc(PH["set", "cols"], 1)
            free(dve, "vec")
            for i in range(4):
                ada_columns(0, i)
            modulation_gain(0, 0)
            for m in range(KD + 1):
                if m < KD:
                    key = ("xin", m)
                    dve.wait_ge(*auxiliary(key))
                    dve.tensor_copy(xT[:, m, :], ps(key)).then_inc(PH["res0", "x"], 1)
                    dve.wait_ge(*when(("res0", "x"), m + 1))
                    free(dve, key)
                if m >= 1:
                    sum_squares(0, m - 1, T)
            with nc.allow_non_contiguous_dma(reason="edges"):
                mark(dve.memset(upad[:], 0.0))
            dve.wait_ge(dve_step, chain[0])
            norm(0, X_CTX, lambda k, q: amix[:, 0, k, q:q + 1], lambda k, q: mod[:, 0, k, q:q + 1])

            def v0_tile(i, key):
                dst = v0[:, :, P * i:P * i + P]
                release(dve.tensor_copy(dst, ps(key).rearrange("p (a b) -> p a b", a=6)), key)
                dve.wait_ge(gfree[group_of(key) % 4], group_of(key) // 4 + 1)
                dve.sem_inc(PH["in0", "vdone"], 1)

            def pooling():
                for i in range(2):
                    key = ("in0", "U", L0_POOL[i])
                    dve.wait_ge(gfree[group_of(key) % 4], group_of(key) // 4 + 1)
                dve.wait_ge(*when(("set", "icnt"), 16))
                L = UPW
                for i in range(2):
                    u, a, b = upad[:, i], ptmp[:, 0], ptmp[:, 1]
                    link(dve.tensor_tensor(a[:, 1:L], u[:, 1:L], u[:, 0:L - 1], ALU.add))
                    link(dve.tensor_tensor(b[:, 2:L - 1], a[:, 1:L - 2], a[:, 3:L], ALU.add))
                    if i == 0:
                        tiers = ((0, a), (1, b))
                    else:
                        link(dve.tensor_tensor(a[:, 4:L - 3], b[:, 2:L - 5], b[:, 6:L - 1], ALU.add))
                        link(dve.tensor_tensor(b[:, 8:L - 7], a[:, 4:L - 11], a[:, 12:L - 3], ALU.add))
                        tiers = ((0, a), (1, b))
                    for half, s in tiers:
                        rows = slice(HD * half, HD * half + HD)
                        for t0, w, p0 in ((0, TX, 8), (TX, TC, 24 + TX)):
                            d = dT[rows, i, t0:t0 + w]
                            link(dve.tensor_tensor(d, s[rows, p0:p0 + w], d, ALU.mult))
                            link(dve.tensor_tensor(d, d, u[rows, p0:p0 + w], ALU.subtract))
                dve.sem_inc(PH["in0", "pooled"], 1)

            inputs("in0", S0, L0_V, 12, v0_tile, {5: pooling}, ADA_IN0)
            for i in range(2):
                key = ("pool", i)
                dve.wait_ge(*when(("in0", "pooly"), i + 1))
                ins = dve.scalar_tensor_tensor(out=hlo[:, i, :], in0=ps(key), scalar=vc("pscale", i),
                                               in1=hhi[:, i, :].bitcast(F32), op0=ALU.mult, op1=ALU.subtract)
                ins.then_inc(PH["in0", "pooldone"], 1)
                dve.wait_ge(*when(("in0", "pooldone"), i + 1))
                free(dve, key)
            attention(0)
            output_tiles(0, 6, T, hhi, hlo, 2)
            residual_tiles(lambda m: ("wout", 0, m), 1, X_CTX, gate_of(0, 16), ADA_WOUT0)
            modulation_gain(0, 1)
            norm(1, X_CTX, lambda k, q: amix[:, 1, k, q:q + 1], lambda k, q: mod[:, 0, 24 + k, q:q + 1])
            ffn(0, FFN_CHUNKS, X_CTX, gate_of(0, 40), 2)
            modulation_gain(1, 0)
            modulation_gain(1, 1)
            norm(2, X_CTX, lambda k, q: amix[:, 2, k, q:q + 1], lambda k, q: mod[:, 1, k, q:q + 1])

            def nv_tile(i, key):
                release(dve.tensor_copy(nv[:, :, P * i:P * i + P], ps(key).rearrange("p (a b) -> p a b", a=6)), key)
                dve.wait_ge(gfree[group_of(key) % 4], group_of(key) // 4 + 1)
                dve.sem_inc(PH["in1", "vdone"], 1)

            def mv_tile(h, key):
                src = ps(key).rearrange("p (a b) -> p a b", a=6)
                if h == 0:
                    dve.wait_ge(*product_of(("mq", "U", MH - 1)))
                mark(dve.tensor_copy(mvx[:, :, HD * h:HD * h + HD], src[:, 0:4, HD:P]))
                dve.tensor_copy(mvc[:, :, HD * h:HD * h + HD], src[:, 4:6, HD:P]).then_inc(PH["mk", "vdone"], 1)
                dve.wait_ge(*when(("mk", "vdone"), h + 1))
                free(dve, key)

            inputs("in1", S1, (14, 15, 16, 17), 18, nv_tile)
            dve.wait_ge(*when(("set", "rope1"), 16))
            inputs("mq", SQ, (), MH, None)
            inputs("mk", SK, tuple(range(MH)), MH, mv_tile)
            attention(1)
            attention(2)
            output_tiles(1, 4, TX, hhi, hlo, 0)
            output_tiles(2, 4, TX, hhi, hlo, 4)
            residual_tiles(lambda m: ("wout", 1, m), 3, X_ONLY, gate_of(1, 16))
            norm(3, X_ONLY, lambda k, q: amix[:, 3, k, q:q + 1], lambda k, q: mod[:, 1, 24 + k, q:q + 1])
            ffn(1, FFN_CHUNKS, X_ONLY, gate_of(1, 40), 4)
            norm(4, X_ONLY, lambda k, q: vc("an2", k), lambda k, q: zero8[:, k:k + 1])

            def v2_tile(i, key):
                release(dve.tensor_copy(v2[:, :, P * i:P * i + P], ps(key, TX).rearrange("p (a b) -> p a b", a=4)), key)
                dve.wait_ge(gfree[group_of(key) % 4], group_of(key) // 4 + 1)
                dve.sem_inc(PH["in2", "vdone"], 1)

            def forget_sums():
                dve.wait_ge(*when(("in2", "fg"), 4))
                c, s = cum[0:N_FOX, :], lsig[0:N_FOX, :]
                link(dve.tensor_scalar(c, c, 0.0, -1.0, ALU.min, ALU.mult))
                link(dve.tensor_tensor(s, s, c, ALU.add))
                dve.tensor_tensor_scan(c, s, s, 0.0, ALU.add, ALU.bypass).then_inc(PH["in2", "cum"], 1)

            inputs("in2", S2, tuple(range(16, 24)), 28, v2_tile, {26: forget_sums})
            attention(3)
            dve.wait_ge(*when(("in2", "outstd"), 1))
            link(dve.reciprocal(ss12[:, 0], ss12[:, 1]))
            for q in range(4):
                for gi, (c0, w) in enumerate(((0, 256), (256, 384), (640, 384))):
                    dve.tensor_scalar(o2[:, q, c0:c0 + w], o2[:, q, c0:c0 + w], ss12[:, 0, gi, q:q + 1], None,
                                      ALU.mult).then_inc(PH["in2", "outn"], 1)
            output_tiles(3, 8, TX, ahi, alo, 0, lambda m: vc("og2", m), (2, 3, 4))
            residual_tiles(lambda m: ("wout", 2, m), 5, X_ONLY, None)
            norm(5, X_ONLY, lambda k, q: vc("mn2", k), lambda k, q: zero8[:, k:k + 1])
            ffn(2, FF2_CHUNKS, X_ONLY, None, None)
            for t in range(4):
                dve.wait_ge(*auxiliary(("xout", t)))
                dve.tensor_copy(ostage[:, t, :], G[group_of(("xout", t)) % 4][:]).then_inc(PH["fin", "copy"], 1)


def normed_before(sums, s):
    return sum(1 for it in sums.values() if it["stop"] and it["s"] < s)


_INS = [
    "x", "c", "ctx", "c_ctx", "l0_ada_w", "l0_ada_b", "l0_norm_mix", "l0_norm_ffn", "l0_w_in", "l0_pool_w",
    "l0_pool_scale", "l0_q_gain", "l0_k_gain", "l0_w_out", "l0_ffn_w_gate", "l0_ffn_w_up", "l0_ffn_w_down",
    "l1_ada_w", "l1_ada_b", "l1_norm_mix", "l1_norm_ffn", "l1_w_in", "l1_mla_q_a_gain", "l1_mla_kv_a_gain",
    "l1_mla_w_uq", "l1_mla_w_ukv", "l1_mla_q_gain", "l1_mla_k_gain", "l1_na_q_gain", "l1_na_k_gain",
    "l1_na_rpb", "l1_w_out", "l1_ffn_w_gate", "l1_ffn_w_up", "l1_ffn_w_down", "attn_norm_2", "w_in_2",
    "b_forget_2", "q_gain_2", "k_gain_2", "out_gain_2", "w_out_2", "mlp_norm_2", "w_up_2", "w_down_2",
]


def kernel(**inputs):
    import concourse.bacc as _bacc
    from concourse.bass_utils import run_bass_kernel_spmd as _run

    nc = _bacc.Bacc("TRN2", target_bir_lowering=False, num_devices=1)
    arrays, aps = {}, {}
    for name in _INS:
        a = np.ascontiguousarray(inputs[name])
        arrays[f"in_{name}_dram"] = a
        aps[name] = nc.dram_tensor(f"in_{name}_dram", a.shape, mybir.dt.from_np(a.dtype), kind="ExternalInput").ap()
    for name, a in shape_tables().items():
        arrays[f"const_{name}_dram"] = a
        aps[name] = nc.dram_tensor(f"const_{name}_dram", a.shape, mybir.dt.from_np(a.dtype), kind="ExternalInput").ap()
    out = nc.dram_tensor("out_0_dram", (1, TX, D), F32, kind="ExternalOutput").ap()
    build(nc, aps, out)
    r = _run(nc, [arrays], core_ids=[0])
    return r.results[0]["out_0_dram"]
```
